# Optimizing a Trainium2 kernel written in Bass

```python
import jax, jax.numpy as jnp
from jax import lax
import numpy as np

D_MODEL = 1024
BATCH = 1
SEQ = 256
DEPTH = 2
DEC_BATCH = 8
DEC_SEQ = 4
PAST_LEN = 256
PAGE_SIZE = 128

HEAD_DIM = 64
BLK = 128
ROPE_THETA = 10000.0
LN_EPS = 1e-5
RMS_EPS = 1e-6
TINY = 1e-30
ALPHA = (2 * DEPTH) ** 0.25
BETA = (8 * DEPTH) ** -0.25
N_EVEN = (DEPTH + 1) // 2
N_ODD = DEPTH // 2

HG_HEADS = 8
HG_DK = 64
HG_DV = 64
HG_CHUNK = 64

NSA_HEADS = 8
NSA_KV_HEADS = 2
NSA_GROUP = NSA_HEADS // NSA_KV_HEADS
CMP_BLOCK = 32
SEL_BLOCK = 64
SEL_RATIO = SEL_BLOCK // CMP_BLOCK
SEL_TOPN = 8
SEL_FORCE = 1e4
NSA_WINDOW = 512

EVEN_SPLITS = (HG_HEADS * HG_DK, HG_HEADS * HG_DK, HG_HEADS * HG_DV, HG_HEADS * HG_DV,
               NSA_HEADS * HEAD_DIM, 2 * NSA_KV_HEADS * HEAD_DIM, 2 * NSA_KV_HEADS * HEAD_DIM,
               2 * NSA_KV_HEADS * HEAD_DIM, 3 * NSA_HEADS)
EVEN_IN = sum(EVEN_SPLITS)
EVEN_MIX = HG_HEADS * HG_DV + NSA_HEADS * HEAD_DIM

DIL_HEADS = 16
DIL_CONFIGS = ((128, 1), (512, 4), (2048, 16))
DIL_MAX_WINDOW = 2048
ODD_IN = 3 * DIL_HEADS * HEAD_DIM
ODD_MIX = DIL_HEADS * HEAD_DIM

PEER_HEADS = 8
PEER_NKEYS = 128
PEER_EXPERTS = PEER_NKEYS * PEER_NKEYS
PEER_TOPK = 16
PEER_QDIM = 256
PEER_BLOCK = 128

kernel_name = 'hybrid_hgrn2_nsa_dilated_peer_step'

def layer_norm(x, g, b):
    xf = x.astype(jnp.float32)
    mu = jnp.mean(xf, -1, keepdims=True)
    var = jnp.mean(jnp.square(xf - mu), -1, keepdims=True)
    return ((xf - mu) * lax.rsqrt(var + LN_EPS) * g + b).astype(x.dtype)

def rope(x, pos):
    half = x.shape[-1] // 2
    inv = ROPE_THETA ** (-jnp.arange(half, dtype=jnp.float32) / half)
    ang = pos.astype(jnp.float32)[:, None] * inv[None, :]
    cos = jnp.cos(ang)[None, :, None, :]
    sin = jnp.sin(ang)[None, :, None, :]
    x1 = x[..., :half].astype(jnp.float32)
    x2 = x[..., half:].astype(jnp.float32)
    return jnp.concatenate([x1 * cos - x2 * sin, x1 * sin + x2 * cos], -1).astype(x.dtype)

def masked_softmax(s, mask):
    s = jnp.where(mask, s.astype(jnp.float32), -jnp.inf)
    m = jnp.max(s, axis=-1, keepdims=True)
    m = jnp.where(jnp.isfinite(m), m, 0.0)
    e = jnp.exp(s - m)
    l = jnp.sum(e, axis=-1, keepdims=True)
    return m, l, e

def band_attn(q, k, v, window):
    B, T, Hk, G, D = q.shape
    back = -(-window // BLK)
    nb = -(-T // BLK)
    Tp = nb * BLK
    qb = jnp.pad(q, ((0, 0), (0, Tp - T), (0, 0), (0, 0), (0, 0))).reshape(B, nb, BLK, Hk, G, D)
    padk = ((0, 0), (back * BLK, Tp - T), (0, 0), (0, 0))
    kb = jnp.pad(k, padk).reshape(B, nb + back, BLK, Hk, D)
    vb = jnp.pad(v, padk).reshape(B, nb + back, BLK, Hk, D)
    widx = jnp.arange(nb)[:, None] + jnp.arange(back + 1)[None, :]
    kw = kb[:, widx].reshape(B, nb, (back + 1) * BLK, Hk, D)
    vw = vb[:, widx].reshape(B, nb, (back + 1) * BLK, Hk, D)
    qpos = jnp.arange(Tp).reshape(nb, BLK)
    kpos = (jnp.arange(nb)[:, None] - back) * BLK + jnp.arange((back + 1) * BLK)[None, :]
    dist = qpos[:, :, None] - kpos[:, None, :]
    mask = (dist >= 0) & (dist <= window) & (kpos[:, None, :] >= 0)
    s = jnp.einsum('bnqhgd,bnkhd->bnqhgk', qb, kw) * (D ** -0.5)
    m, l, e = masked_softmax(s, mask[None, :, :, None, None, :])
    o = jnp.einsum('bnqhgk,bnkhd->bnqhgd', e, vw.astype(jnp.float32)) / jnp.maximum(l, TINY)
    m = m[..., 0].reshape(B, Tp, Hk, G)[:, :T]
    l = l[..., 0].reshape(B, Tp, Hk, G)[:, :T]
    o = o.reshape(B, Tp, Hk, G, D)[:, :T]
    return m, l, o

def merge_by_denominator(stats):
    m = jnp.stack([st[0] for st in stats])
    l = jnp.stack([st[1] for st in stats])
    o = jnp.stack([st[2] for st in stats])
    w = l * jnp.exp(m - jnp.max(m, axis=0, keepdims=True))
    return jnp.sum(w[..., None] * o, axis=0) / jnp.sum(w, axis=0)[..., None]

def hgrn2_chunk(S0, q, k, v, lf):
    C = q.shape[1]
    b = jnp.cumsum(lf, axis=1)
    causal = jnp.tril(jnp.ones((C, C), dtype=bool))
    diff = b[:, :, None] - b[:, None, :]
    decay = jnp.exp(jnp.where(causal[None, :, :, None, None], diff, -jnp.inf))
    a = jnp.einsum('bthk,btshk,bshk->bhts', q, decay, k)
    o = jnp.einsum('bhts,bshv->bthv', a, v) + jnp.einsum('bthk,bhkv->bthv', q * jnp.exp(b), S0)
    b_end = b[:, -1]
    S = jnp.exp(b_end)[..., None] * S0 + jnp.einsum('bshk,bshv->bhkv', k * jnp.exp(b_end[:, None] - b), v)
    return S, o

def nsa_blocks(cmp_kv, slc_kv, pe):
    B, Tk = cmp_kv.shape[:2]
    nc = Tk // CMP_BLOCK
    cb = cmp_kv[:, :nc * CMP_BLOCK].astype(jnp.float32).reshape(B, nc, CMP_BLOCK, 2, NSA_KV_HEADS, HEAD_DIM)
    kc = jnp.mean(cb[:, :, :, 0] + pe.astype(jnp.float32), axis=2)
    vc = jnp.mean(cb[:, :, :, 1], axis=2)
    nsel = -(-Tk // SEL_BLOCK)
    sb = jnp.pad(slc_kv, ((0, 0), (0, nsel * SEL_BLOCK - Tk), (0, 0), (0, 0), (0, 0)))
    sb = jnp.moveaxis(sb.reshape(B, nsel, SEL_BLOCK, 2, NSA_KV_HEADS, HEAD_DIM), 4, 1)
    return kc, vc, sb[..., 0, :], sb[..., 1, :]

def nsa_core(q_nope, q_rope, qpos, kc, vc, ks_blk, vs_blk):
    B, Tq = q_nope.shape[:2]
    scale = HEAD_DIM ** -0.5
    nc = kc.shape[1]
    nsel = ks_blk.shape[2]
    s = jnp.einsum('bqhgd,bchd->bqhgc', q_nope, kc) * scale
    avail = ((jnp.arange(nc) + 1) * CMP_BLOCK - 1)[None, :] <= qpos[:, None]
    _, l, e = masked_softmax(s, avail[None, :, None, None, :])
    p_cmp = e / jnp.maximum(l, TINY)
    o_cmp = jnp.einsum('bqhgc,bchd->bqhgd', p_cmp, vc)
    imp = jnp.sum(p_cmp, axis=3)
    imp = jnp.pad(imp, ((0, 0), (0, 0), (0, 0), (0, nsel * SEL_RATIO - nc)))
    imp = imp.reshape(B, Tq, NSA_KV_HEADS, nsel, SEL_RATIO).sum(-1)
    blk = jnp.arange(nsel)
    forced = (blk[None, :] == (qpos // SEL_BLOCK)[:, None]) | (blk[None, :] == 0)
    avail_b = blk[None, :] * SEL_BLOCK <= qpos[:, None]
    imp = jnp.where(forced[None, :, None, :], SEL_FORCE, jnp.where(avail_b[None, :, None, :], imp, -1.0))
    n_top = min(SEL_TOPN, nsel)
    _, idx = lax.top_k(imp, n_top)
    idx = jnp.transpose(idx, (0, 2, 1, 3))
    gather = jax.vmap(jax.vmap(lambda kb, ib: kb[ib]))
    kg = gather(ks_blk, idx).reshape(B, NSA_KV_HEADS, Tq, n_top * SEL_BLOCK, HEAD_DIM)
    vg = gather(vs_blk, idx).reshape(B, NSA_KV_HEADS, Tq, n_top * SEL_BLOCK, HEAD_DIM)
    kpos = (idx[..., None] * SEL_BLOCK + jnp.arange(SEL_BLOCK)).reshape(B, NSA_KV_HEADS, Tq, n_top * SEL_BLOCK)
    ss = jnp.einsum('bqhgd,bhqkd->bhqgk', q_rope, kg) * scale
    _, l2, e2 = masked_softmax(ss, (kpos <= qpos[None, None, :, None])[:, :, :, None, :])
    o_slc = jnp.einsum('bhqgk,bhqkd->bqhgd', e2 / jnp.maximum(l2, TINY), vg.astype(jnp.float32))
    return o_cmp, o_slc

def even_project(x, pos, lb, w_in):
    B, T, _ = x.shape
    h = x @ w_in
    hq, hf, hi, hg, nq, ncmp, nslc, nwin, ngate = jnp.split(h, np.cumsum(EVEN_SPLITS)[:-1], axis=-1)
    f = lb + (1.0 - lb) * jax.nn.sigmoid(hf.astype(jnp.float32))
    f = f.reshape(B, T, HG_HEADS, HG_DK)
    hg_q = jax.nn.silu(hq.astype(jnp.float32)).reshape(B, T, HG_HEADS, HG_DK)
    hg_k = 1.0 - f
    hg_lf = jnp.log(f)
    hg_v = hi.astype(jnp.float32).reshape(B, T, HG_HEADS, HG_DV)
    hg_gate = hg.reshape(B, T, HG_HEADS, HG_DV)
    q = nq.reshape(B, T, NSA_HEADS, HEAD_DIM)
    q_nope = q.reshape(B, T, NSA_KV_HEADS, NSA_GROUP, HEAD_DIM)
    q_rope = rope(q, pos).reshape(B, T, NSA_KV_HEADS, NSA_GROUP, HEAD_DIM)
    cmp_kv = ncmp.reshape(B, T, 2, NSA_KV_HEADS, HEAD_DIM)
    slc = nslc.reshape(B, T, 2, NSA_KV_HEADS, HEAD_DIM)
    slc_kv = jnp.stack([rope(slc[:, :, 0], pos), slc[:, :, 1]], axis=2)
    win = nwin.reshape(B, T, 2, NSA_KV_HEADS, HEAD_DIM)
    win_kv = jnp.stack([rope(win[:, :, 0], pos), win[:, :, 1]], axis=2)
    gates = jax.nn.sigmoid(ngate.astype(jnp.float32)).reshape(B, T, 3, NSA_KV_HEADS, NSA_GROUP)[..., None]
    return hg_q, hg_k, hg_v, hg_lf, hg_gate, q_nope, q_rope, cmp_kv, slc_kv, win_kv, gates

def even_finish(dtype, o_hg, hg_gate, o_cmp, o_slc, o_win, gates, hg_norm_g, w_out):
    B, T = o_hg.shape[:2]
    o = o_hg * lax.rsqrt(jnp.mean(jnp.square(o_hg), -1, keepdims=True) + RMS_EPS)
    o = o * hg_norm_g.astype(jnp.float32).reshape(HG_HEADS, HG_DV) * jax.nn.silu(hg_gate.astype(jnp.float32))
    nsa = gates[:, :, 0] * o_cmp + gates[:, :, 1] * o_slc + gates[:, :, 2] * o_win
    cat = jnp.concatenate([o.reshape(B, T, -1), nsa.reshape(B, T, -1)], axis=-1).astype(dtype)
    return cat @ w_out

def even_prompt(x, lb, w_in, w_out, hg_norm_g, cmp_pe):
    B, T, _ = x.shape
    pos = jnp.arange(T)
    hq, hk, hv, hlf, hgate, q_nope, q_rope, cmp_kv, slc_kv, win_kv, gates = even_project(x, pos, lb, w_in)
    nch = T // HG_CHUNK
    to_ch = lambda a: jnp.moveaxis(a.reshape(B, nch, HG_CHUNK, *a.shape[2:]), 1, 0)
    S0 = jnp.zeros((B, HG_HEADS, HG_DK, HG_DV), jnp.float32)
    S_fin, o_hg = lax.scan(lambda S, c: hgrn2_chunk(S, *c), S0, (to_ch(hq), to_ch(hk), to_ch(hv), to_ch(hlf)))
    o_hg = jnp.moveaxis(o_hg, 0, 1).reshape(B, T, HG_HEADS, HG_DV)
    kc, vc, ksb, vsb = nsa_blocks(cmp_kv, slc_kv, cmp_pe)
    nq = T // BLK
    to_q = lambda a: jnp.moveaxis(a.reshape(B, nq, BLK, *a.shape[2:]), 1, 0)
    from_q = lambda a: jnp.moveaxis(a, 0, 1).reshape(B, T, *a.shape[3:])
    o_cmp, o_slc = lax.map(lambda c: nsa_core(c[0], c[1], c[2], kc, vc, ksb, vsb),
                           (to_q(q_nope), to_q(q_rope), pos.reshape(nq, BLK)))
    o_cmp, o_slc = from_q(o_cmp), from_q(o_slc)
    _, _, o_win = band_attn(q_rope, win_kv[:, :, 0], win_kv[:, :, 1], NSA_WINDOW)
    y = even_finish(x.dtype, o_hg, hgate, o_cmp, o_slc, o_win, gates, hg_norm_g, w_out)
    return y, (S_fin, cmp_kv, slc_kv, win_kv[:, -min(NSA_WINDOW, T):])

def even_sample(x, past_len, page_table, hg_state, cmp_pool, slc_pool, win_buf, lb, w_in, w_out, hg_norm_g, cmp_pe):
    B, T, _ = x.shape
    pos = past_len + jnp.arange(T)
    hq, hk, hv, hlf, hgate, q_nope, q_rope, cmp_kv, slc_kv, win_kv, gates = even_project(x, pos, lb, w_in)
    S_new, o_hg = hgrn2_chunk(hg_state.astype(jnp.float32), hq, hk, hv, hlf)
    gather_pages = lambda pool: pool[page_table].reshape(B, past_len, *pool.shape[2:])
    cmp_all = jnp.concatenate([gather_pages(cmp_pool), cmp_kv], axis=1)
    slc_all = jnp.concatenate([gather_pages(slc_pool), slc_kv], axis=1)
    kc, vc, ksb, vsb = nsa_blocks(cmp_all, slc_all, cmp_pe)
    o_cmp, o_slc = nsa_core(q_nope, q_rope, pos, kc, vc, ksb, vsb)
    Lw = win_buf.shape[1]
    rows = jnp.concatenate([win_buf, win_kv], axis=1)
    kpos = past_len - Lw + jnp.arange(Lw + T)
    dist = pos[:, None] - kpos[None, :]
    mask = (dist >= 0) & (dist <= NSA_WINDOW)
    s = jnp.einsum('bqhgd,bkhd->bqhgk', q_rope, rows[:, :, 0]) * (HEAD_DIM ** -0.5)
    _, l, e = masked_softmax(s, mask[None, :, None, None, :])
    o_win = jnp.einsum('bqhgk,bkhd->bqhgd', e, rows[:, :, 1].astype(jnp.float32)) / jnp.maximum(l, TINY)
    y = even_finish(x.dtype, o_hg, hgate, o_cmp, o_slc, o_win, gates, hg_norm_g, w_out)
    return y, (S_new, cmp_kv, slc_kv, win_kv)

def odd_project(x, pos, w_in):
    B, T, _ = x.shape
    h = (x @ w_in).reshape(B, T, 3, DIL_HEADS, HEAD_DIM)
    return rope(h[:, :, 0], pos), rope(h[:, :, 1], pos), h[:, :, 2]

def to_sub(a, d):
    B, T = a.shape[:2]
    return a.reshape(B, T // d, d, *a.shape[2:]).swapaxes(1, 2).reshape(B * d, T // d, *a.shape[2:])

def from_sub(a, d, B):
    n = a.shape[1]
    return a.reshape(B, d, n, *a.shape[2:]).swapaxes(1, 2).reshape(B, n * d, *a.shape[2:])

def odd_prompt(x, w_in, w_out):
    B, T, _ = x.shape
    pos = jnp.arange(T)
    q, k, v = odd_project(x, pos, w_in)
    stats = []
    for window, dil in DIL_CONFIGS:
        m, l, o = band_attn(to_sub(q, dil)[:, :, :, None], to_sub(k, dil), to_sub(v, dil), window // dil)
        stats.append((from_sub(m[..., 0], dil, B), from_sub(l[..., 0], dil, B), from_sub(o[:, :, :, 0], dil, B)))
    o = merge_by_denominator(stats)
    y = o.reshape(B, T, ODD_MIX).astype(x.dtype) @ w_out
    return y, jnp.stack([k, v], axis=2)[:, -min(DIL_MAX_WINDOW, T):]

def odd_sample(x, past_len, buf, w_in, w_out):
    B, T, _ = x.shape
    pos = past_len + jnp.arange(T)
    q, k, v = odd_project(x, pos, w_in)
    new_kv = jnp.stack([k, v], axis=2)
    L = buf.shape[1]
    rows = jnp.concatenate([buf, new_kv], axis=1)
    stats = []
    for window, dil in DIL_CONFIGS:
        nk = window // dil + 1
        ridx = L + jnp.arange(T)[:, None] - dil * jnp.arange(nk)[None, :]
        g = rows[:, jnp.maximum(ridx, 0)]
        s = jnp.einsum('bqhd,bqkhd->bqhk', q, g[:, :, :, 0]) * (HEAD_DIM ** -0.5)
        m, l, e = masked_softmax(s, (ridx >= 0)[None, :, None, :])
        o = jnp.einsum('bqhk,bqkhd->bqhd', e, g[:, :, :, 1].astype(jnp.float32)) / jnp.maximum(l, TINY)
        stats.append((m[..., 0], l[..., 0], o))
    o = merge_by_denominator(stats)
    y = o.reshape(B, T, ODD_MIX).astype(x.dtype) @ w_out
    return y, new_kv

def peer_ffn(x, w_q, sub_keys, u, v):
    B, T, D = x.shape
    n = B * T
    xt = x.reshape(n, D)
    q = (xt @ w_q).reshape(n, PEER_HEADS, 2, PEER_QDIM // 2)
    s = jnp.einsum('nhcd,hckd->nhck', q, sub_keys).astype(jnp.float32)
    s1, i1 = lax.top_k(s[:, :, 0], PEER_TOPK)
    s2, i2 = lax.top_k(s[:, :, 1], PEER_TOPK)
    cand = (s1[..., :, None] + s2[..., None, :]).reshape(n, PEER_HEADS, PEER_TOPK * PEER_TOPK)
    cidx = (i1[..., :, None] * PEER_NKEYS + i2[..., None, :]).reshape(n, PEER_HEADS, PEER_TOPK * PEER_TOPK)
    top, sel = lax.top_k(cand, PEER_TOPK)
    eidx = jnp.take_along_axis(cidx, sel, axis=-1)
    gate = jax.nn.softmax(top, axis=-1)
    nblk = -(-n // PEER_BLOCK)
    npad = nblk * PEER_BLOCK - n
    xb = jnp.pad(xt, ((0, npad), (0, 0))).reshape(nblk, PEER_BLOCK, D)
    eb = jnp.pad(eidx, ((0, npad), (0, 0), (0, 0))).reshape(nblk, PEER_BLOCK, PEER_HEADS, PEER_TOPK)
    gb = jnp.pad(gate, ((0, npad), (0, 0), (0, 0))).reshape(nblk, PEER_BLOCK, PEER_HEADS, PEER_TOPK)

    def expert_block(args):
        xk, ek, gk = args
        a = jax.nn.gelu(jnp.einsum('nhkd,nd->nhk', u[ek], xk).astype(jnp.float32), approximate=False)
        return jnp.einsum('nhk,nhkd->nd', (gk * a).astype(v.dtype), v[ek])

    y = lax.map(expert_block, (xb, eb, gb)).reshape(nblk * PEER_BLOCK, D)[:n]
    return y.reshape(B, T, D).astype(x.dtype)

def setup_inputs(seed: int = 0) -> dict:
    key = jax.random.key(seed)
    ks = jax.random.split(key, 24)
    f32 = jnp.float32
    n_pages = PAST_LEN // PAGE_SIZE
    used = DEC_BATCH * n_pages
    n_pool = used + max(1, used // 4)
    win_len = min(NSA_WINDOW, PAST_LEN)
    dil_len = min(DIL_MAX_WINDOW, PAST_LEN)

    def nrm(i, shape, scale):
        return jax.random.normal(ks[i], shape, f32) * scale

    page_table = jax.random.permutation(ks[7], n_pool)[:used].reshape(DEC_BATCH, n_pages).astype(jnp.int32)
    return {
        'x_prompt': nrm(0, (BATCH, SEQ, D_MODEL), 1.0),
        'x_sample': nrm(1, (DEC_BATCH, DEC_SEQ, D_MODEL), 1.0),
        'state_hgrn': nrm(2, (N_EVEN, DEC_BATCH, HG_HEADS, HG_DK, HG_DV), 0.5),
        'cache_cmp_kv': nrm(3, (N_EVEN, n_pool, PAGE_SIZE, 2, NSA_KV_HEADS, HEAD_DIM), 1.0),
        'cache_slc_kv': nrm(4, (N_EVEN, n_pool, PAGE_SIZE, 2, NSA_KV_HEADS, HEAD_DIM), 1.0),
        'cache_win_kv': nrm(5, (N_EVEN, DEC_BATCH, win_len, 2, NSA_KV_HEADS, HEAD_DIM), 1.0),
        'cache_dil_kv': nrm(6, (N_ODD, DEC_BATCH, dil_len, 2, DIL_HEADS, HEAD_DIM), 1.0),
        'page_table': page_table,
        'hg_gamma': nrm(8, (DEPTH + 1, HG_HEADS * HG_DK), 0.5),
        'even_w_in': nrm(9, (N_EVEN, D_MODEL, EVEN_IN), D_MODEL ** -0.5),
        'even_w_out': nrm(10, (N_EVEN, EVEN_MIX, D_MODEL), BETA * EVEN_MIX ** -0.5),
        'hg_norm_g': 1.0 + nrm(11, (N_EVEN, HG_HEADS * HG_DV), 0.02),
        'nsa_cmp_pe': nrm(12, (N_EVEN, CMP_BLOCK, NSA_KV_HEADS, HEAD_DIM), 0.1),
        'odd_w_in': nrm(13, (N_ODD, D_MODEL, ODD_IN), D_MODEL ** -0.5),
        'odd_w_out': nrm(14, (N_ODD, ODD_MIX, D_MODEL), BETA * ODD_MIX ** -0.5),
        'ln_mix_g': 1.0 + nrm(15, (DEPTH, D_MODEL), 0.02),
        'ln_mix_b': nrm(16, (DEPTH, D_MODEL), 0.02),
        'peer_w_q': nrm(17, (DEPTH, D_MODEL, PEER_HEADS * PEER_QDIM), D_MODEL ** -0.5),
        'peer_sub_keys': nrm(18, (DEPTH, PEER_HEADS, 2, PEER_NKEYS, PEER_QDIM // 2), (PEER_QDIM // 2) ** -0.5),
        'peer_u': nrm(19, (DEPTH, PEER_EXPERTS, D_MODEL), D_MODEL ** -0.5),
        'peer_v': nrm(20, (DEPTH, PEER_EXPERTS, D_MODEL), BETA * PEER_TOPK ** -0.5),
        'ln_ffn_g': 1.0 + nrm(21, (DEPTH, D_MODEL), 0.02),
        'ln_ffn_b': nrm(22, (DEPTH, D_MODEL), 0.02),
    }

def reference(x_prompt, x_sample, state_hgrn, cache_cmp_kv, cache_slc_kv, cache_win_kv, cache_dil_kv,
              page_table, hg_gamma, even_w_in, even_w_out, hg_norm_g, nsa_cmp_pe, odd_w_in, odd_w_out,
              ln_mix_g, ln_mix_b, peer_w_q, peer_sub_keys, peer_u, peer_v, ln_ffn_g, ln_ffn_b):
    past_len = page_table.shape[1] * PAGE_SIZE
    lb_table = jnp.cumsum(jax.nn.softmax(hg_gamma.astype(jnp.float32), axis=0), axis=0)
    yp, ys = x_prompt, x_sample
    hg_p, hg_s, cmp_p, cmp_s, slc_p, slc_s, win_p, win_s, dil_p, dil_s = ([] for _ in range(10))
    for layer in range(DEPTH):
        if layer % 2 == 0:
            e = layer // 2
            mp, (a, b, c, d) = even_prompt(yp, lb_table[layer], even_w_in[e], even_w_out[e], hg_norm_g[e], nsa_cmp_pe[e])
            ms, (a2, b2, c2, d2) = even_sample(ys, past_len, page_table, state_hgrn[e], cache_cmp_kv[e], cache_slc_kv[e],
                                               cache_win_kv[e], lb_table[layer], even_w_in[e], even_w_out[e],
                                               hg_norm_g[e], nsa_cmp_pe[e])
            hg_p.append(a); cmp_p.append(b); slc_p.append(c); win_p.append(d)
            hg_s.append(a2); cmp_s.append(b2); slc_s.append(c2); win_s.append(d2)
        else:
            o = layer // 2
            mp, kvp = odd_prompt(yp, odd_w_in[o], odd_w_out[o])
            ms, kvs = odd_sample(ys, past_len, cache_dil_kv[o], odd_w_in[o], odd_w_out[o])
            dil_p.append(kvp); dil_s.append(kvs)
        yp = layer_norm(ALPHA * yp + mp, ln_mix_g[layer], ln_mix_b[layer])
        ys = layer_norm(ALPHA * ys + ms, ln_mix_g[layer], ln_mix_b[layer])
        yp = layer_norm(ALPHA * yp + peer_ffn(yp, peer_w_q[layer], peer_sub_keys[layer], peer_u[layer], peer_v[layer]),
                        ln_ffn_g[layer], ln_ffn_b[layer])
        ys = layer_norm(ALPHA * ys + peer_ffn(ys, peer_w_q[layer], peer_sub_keys[layer], peer_u[layer], peer_v[layer]),
                        ln_ffn_g[layer], ln_ffn_b[layer])
    return (yp, ys, jnp.stack(hg_p), jnp.stack(hg_s), jnp.stack(cmp_p), jnp.stack(cmp_s),
            jnp.stack(slc_p), jnp.stack(slc_s), jnp.stack(win_p), jnp.stack(win_s),
            jnp.stack(dil_p), jnp.stack(dil_s))


_drawn_inputs = setup_inputs


def setup_inputs(seed=0):
    import zlib

    import numpy as np

    out = dict(_drawn_inputs(seed))
    spreads = {}
    factors = {'cache_cmp_kv': 16.88,
     'cache_slc_kv': 3.714,
     'cache_win_kv': 3.538,
     'hg_norm_g': 25.499,
     'nsa_cmp_pe': 200.0}
    for name, (base, spread) in spreads.items():
        noise = np.random.default_rng([zlib.crc32(name.encode()), seed]).standard_normal(out[name].shape)
        drawn = base * np.exp(spread * noise) if base else spread * noise
        out[name] = __import__('jax').numpy.asarray(drawn.astype(out[name].dtype))
    for name, factor in factors.items():
        out[name] = (out[name] * factor).astype(out[name].dtype)
    return out
```

```python
from contextlib import ExitStack

import numpy as np

import concourse.bass as bass
from concourse import mybir

F32 = mybir.dt.float32
U32 = mybir.dt.uint32
I32 = mybir.dt.int32
ALU = mybir.AluOpType
ACT = mybir.ActivationFunctionType
AX = mybir.AxisListType.X

D = 1024
KC = D // 128
SEQ = 256
DEC_B, DEC_T = 8, 4
NS = DEC_B * DEC_T
PAST = 256
PAGE = 128
NPG = PAST // PAGE
NTOK = SEQ + NS
ROWS = (128, 128, NS)
TILES = len(ROWS)
DEPTH = 2
ALPHA = float((2 * DEPTH) ** 0.25)
LN_EPS, RMS_EPS, TINY = 1e-5, 1e-6, 1e-30
HD = 64
SCALE = HD ** -0.5
HG = 8
KV, GR = 2, 4
NBLK = PAST // 32
MASKED = -1e30
LEAST = -1e28
HEADS = 16
HP = HEADS // 2
DIL = ((128, 1), (512, 4), (2048, 16))
PH, PK, NK = 8, 16, 128
EXPERTS = NK * NK
SLOTS = PH * PK
RING = 8
GROUP = 4
LEVELS = (1, 2, 4, 8, 16, 32, 64)

V0, G0, Q0, CMP0, SLC0, WIN0, GATE0, EVEN_ROWS = 0, 512, 1024, 1536, 1792, 2048, 2304, 2328


def shape_constants():
    half = HD // 2
    inv = np.float32(10000.0) ** (-np.arange(half, dtype=np.float32) / np.float32(half))
    cos = np.zeros((128, TILES, half), np.float32)
    sin = np.zeros((128, TILES, half), np.float32)
    for t in range(TILES):
        pos = np.arange(128) + 128 * t if t < 2 else PAST + np.arange(128) % DEC_T
        ang = pos.astype(np.float32)[:, None] * inv[None, :].astype(np.float32)
        cos[:, t], sin[:, t] = np.cos(ang.astype(np.float64)), np.sin(ang.astype(np.float64))

    def reach(qpos, kpos):
        dist = qpos[:, None] - kpos[None, :]
        count = np.zeros(dist.shape, np.float32)
        for window, dil in DIL:
            count += (dist >= 0) & (dist <= window // dil * dil) & (dist % dil == 0)
        return (dist >= 0), count

    p = np.arange(128)
    causal = np.zeros((128, 2, SEQ), np.float32)
    dil_mask = np.zeros((128, 2, SEQ), np.float32)
    dil_count = np.zeros((128, 2, SEQ), np.float32)
    cmp_mask = np.zeros((128, 2, NBLK), np.float32)
    for t in range(2):
        seen, count = reach(p + 128 * t, np.arange(SEQ))
        causal[:, t] = np.where(seen, 0, MASKED)
        dil_mask[:, t] = np.where(count > 0, 0, MASKED)
        dil_count[:, t] = count
        cmp_mask[:, t] = np.where((np.arange(NBLK) + 1)[None] * 32 - 1 <= (p + 128 * t)[:, None], 0, MASKED)
    tok = p % NS
    seen, count = reach(PAST + tok % DEC_T, np.concatenate([np.arange(PAST), PAST + np.arange(NS) % DEC_T]))
    own = np.concatenate([np.ones((128, PAST), bool), tok[:, None] // DEC_T == np.arange(NS)[None] // DEC_T], 1)
    new_causal = np.where(seen & own, 0, MASKED).astype(np.float32)
    new_mask = np.where((count > 0) & own, 0, MASKED).astype(np.float32)
    new_count = np.where(own, count, 0).astype(np.float32)
    batch_cols = np.broadcast_to((np.arange(NS)[None] // DEC_T == np.arange(DEC_B)[:, None]), (128, DEC_B, NS))
    batch_rows = tok[:, None] // DEC_T == np.arange(DEC_B)[None]
    pool = np.zeros((128, NPG, NBLK), np.float32)
    for t in range(NPG):
        pool[p, t, 4 * t + p // 32] = 1 / 32
    fold = tok[:, None] == np.arange(NS)[None]
    parts = dict(
        ident=np.eye(128), cos=cos, sin=sin, causal=causal, dil_mask=dil_mask, dil_count=dil_count,
        cmp_mask=cmp_mask, new_causal=new_causal, new_mask=new_mask, new_count=new_count,
        batch_cols=batch_cols, batch_rows=batch_rows, pool=pool, mean32=np.full((128, NBLK), 1 / 32), fold=fold,
        iota16=np.broadcast_to(np.arange(PK), (128, PK)), row=p[:, None],
    )
    at, cols = {}, []
    for name, a in parts.items():
        a = np.asarray(a, np.float32)
        n = sum(c.shape[1] for c in cols)
        at[name] = (n, a.shape[1:])
        cols.append(a.reshape(128, -1))
    s, t = p[:, None], p[None, :]
    levels = [s == t] + [(s // (2 * m) == t // (2 * m)) & (s // m % 2 == 0) & (t // m % 2 == 1) for m in LEVELS]
    return np.concatenate(cols, 1), at, np.stack(levels, 1).astype(np.uint32)


CONST, CONST_AT, LEVEL_MASKS = shape_constants()


class Steps:

    def __init__(self, k, eng, name):
        self.sem, self.eng, self.n = k.sem(name), eng, 0

    def __call__(self, ins):
        self.n += 1
        ins.then_inc(self.sem, 1)
        self.eng.wait_ge(self.sem, self.n)


class Core:

    def __init__(self, nc, ctx):
        self.nc, self.ctx, self.serial, self.stage_sems = nc, ctx, 0, []
        self.dve_steps = Steps(self, nc.vector, "dve_steps")
        self.x = self.sbuf("x", [128, TILES, D])
        self.xT = self.sbuf("xT", [128, KC, NTOK])
        self.const = self.sbuf("const", list(CONST.shape))
        self.ps = ctx.enter_context(nc.psum_tensor("ps", [128, 8, 512], F32))

    def sem(self, name):
        self.serial += 1
        self.stage_sems.append(self.nc.alloc_semaphore(f"{name}_{self.serial}"))
        return self.stage_sems[-1]

    def fresh_semaphores(self):
        self.nc.clear_and_free_semaphores(self.stage_sems)
        self.stage_sems = []
        self.nc.all_engine_barrier()
        self.dve_steps.n = 0
        self.dve_steps.sem = self.sem("dve_steps")

    def sbuf(self, name, shape, dt=F32, ctx=None):
        self.serial += 1
        return (ctx or self.ctx).enter_context(self.nc.sbuf_tensor(f"{name}_{self.serial}", shape, dt))

    def c(self, name):
        n, shape = CONST_AT[name]
        size = int(np.prod(shape))
        flat = self.const[:, n:n + size]
        if len(shape) == 2:
            return flat.rearrange("p (a b) -> p a b", b=shape[1])
        return flat

    def bank(self, b):
        return self.ps[:, b, :]


def bc(ap, axis, n):
    ap = ap.unsqueeze(axis)
    shape = list(ap.shape)
    shape[axis] = n
    return ap.broadcast_to(shape)


def cols(t):
    return slice(128 * t, 128 * t + ROWS[t])




def load_inputs(k, x_prompt, x_sample, const):
    nc = k.nc
    loaded = k.sem("loaded")
    with nc.Block() as block:
        @block.sync
        def _(sp):
            sp.dma_start(k.const[:, :], const).then_inc(loaded, 16)
            sp.dma_start(k.x[:, 0:2, :], x_prompt.rearrange("o (t p) d -> p (o t) d", p=128)).then_inc(loaded, 16)
            sp.dma_start(k.x[0:NS, 2, :], x_sample.rearrange("b t d -> (b t) d")).then_inc(loaded, 16)
            sp.wait_ge(loaded, 48)


def transposes(k, name, groups):
    nc = k.nc
    turned, v_out, s_out = k.sem(name + "_turned"), k.sem(name + "_v_out"), k.sem(name + "_s_out")
    ident = k.c("ident")
    sizes = []
    for srcs, dst in groups:
        sizes.append((srcs[0].shape[0], int(np.prod(srcs[0].shape[1:]))))

    def out_view(i):
        (rows, width), (srcs, dst) = sizes[i], groups[i]
        flat = k.bank(i % 8)[0:width, 0:rows * len(srcs)]
        if len(dst.shape) == 3:
            return flat.rearrange("p (a b) -> p a b", b=dst.shape[2])
        return flat

    with nc.Block() as block:
        @block.tensor
        def _(pe):
            for i, (srcs, dst) in enumerate(groups):
                rows, width = sizes[i]
                if i >= 8:
                    pe.wait_ge((v_out, s_out)[i % 2], (i - 8) // 2 + 1)
                for j, src in enumerate(srcs):
                    last = nc.tensor.transpose(k.bank(i % 8)[0:width, j * rows:(j + 1) * rows], src, ident[0:rows, 0:rows])
                last.then_inc(turned, 1)

        @block.vector
        def _(dve):
            for i in range(0, len(groups), 2):
                dve.wait_ge(turned, i + 1)
                nc.vector.tensor_copy(groups[i][1], out_view(i)).then_inc(v_out, 1)

        @block.scalar
        def _(act):
            for i in range(1, len(groups), 2):
                act.wait_ge(turned, i + 1)
                nc.scalar.copy(groups[i][1], out_view(i)).then_inc(s_out, 1)


def transpose_x(k, name):
    groups = []
    for t, rows in enumerate(ROWS):
        for c in range(0, KC, 4):
            groups.append(([k.x[0:rows, t, (c + j) * 128:(c + j + 1) * 128] for j in range(4)],
                           k.xT[:, c:c + 4, cols(t)]))
    transposes(k, name, groups)


def project_rows(k, name, w, widths, out):
    nc = k.nc
    starts = [sum(widths[:i]) for i in range(len(widths))]
    w_v = w.rearrange("(c p) n -> p c n", p=128)
    landed = [k.sem(f"{name}_w_landed{i}") for i in range(3)]
    product, v_out, s_out = k.sem(name + "_product"), k.sem(name + "_v_out"), k.sem(name + "_s_out")
    jobs = [(j, t) for j in range(len(widths)) for t in range(TILES)]
    with ExitStack() as ctx:
        wbuf = k.sbuf(name + "_w", [128, 3, KC, 512], ctx=ctx)
        block = ctx.enter_context(nc.Block())

        @block.sync
        def _(sp):
            for j, (at, n) in enumerate(zip(starts, widths)):
                if j >= 3:
                    sp.wait_ge(product, TILES * (j - 2))
                sp.dma_start(wbuf[:, j % 3, :, 0:n], w_v[:, :, at:at + n]).then_inc(landed[j % 3], 16)

        @block.tensor
        def _(pe):
            for i, (j, t) in enumerate(jobs):
                if t == 0:
                    pe.wait_ge(landed[j % 3], 16 * (j // 3 + 1))
                if i >= 8:
                    pe.wait_ge((v_out, s_out)[i % 2], (i - 8) // 2 + 1)
                for c in range(KC):
                    last = nc.tensor.matmul(k.bank(i % 8)[0:ROWS[t], 0:widths[j]], k.xT[:, c, cols(t)],
                                            wbuf[:, j % 3, c, 0:widths[j]], start=(c == 0), stop=(c == KC - 1))
                last.then_inc(product, 1)

        def piece(i):
            j, t = jobs[i]
            return out[0:ROWS[t], t, starts[j]:starts[j] + widths[j]], k.bank(i % 8)[0:ROWS[t], 0:widths[j]]

        @block.vector
        def _(dve):
            for i in range(0, len(jobs), 2):
                dve.wait_ge(product, i + 1)
                nc.vector.tensor_copy(*piece(i)).then_inc(v_out, 1)

        @block.scalar
        def _(act):
            for i in range(1, len(jobs), 2):
                act.wait_ge(product, i + 1)
                nc.scalar.copy(*piece(i)).then_inc(s_out, 1)


def project_cols(k, name, w, n, outT):
    nc = k.nc
    w_v = w.rearrange("(c p) n -> p c n", p=128)
    landed = [k.sem(f"{name}_w_landed{i}") for i in range(3)]
    product, v_out, s_out = k.sem(name + "_product"), k.sem(name + "_v_out"), k.sem(name + "_s_out")
    with ExitStack() as ctx:
        wbuf = k.sbuf(name + "_w", [128, 3, KC, 512], ctx=ctx)
        block = ctx.enter_context(nc.Block())

        @block.sync
        def _(sp):
            for j in range(n // 512):
                if j >= 3:
                    sp.wait_ge(product, 4 * (j - 2))
                sp.dma_start(wbuf[:, j % 3, :, :], w_v[:, :, 512 * j:512 * (j + 1)]).then_inc(landed[j % 3], 16)

        @block.tensor
        def _(pe):
            for i in range(n // 128):
                j = i // 4
                if i % 4 == 0:
                    pe.wait_ge(landed[j % 3], 16 * (j // 3 + 1))
                if i >= 8:
                    pe.wait_ge((v_out, s_out)[i % 2], (i - 8) // 2 + 1)
                for c in range(KC):
                    last = nc.tensor.matmul(k.bank(i % 8)[:, 0:NTOK], wbuf[:, j % 3, c, 128 * (i % 4):128 * (i % 4 + 1)],
                                            k.xT[:, c, :], start=(c == 0), stop=(c == KC - 1))
                last.then_inc(product, 1)

        @block.vector
        def _(dve):
            for i in range(0, n // 128, 2):
                dve.wait_ge(product, i + 1)
                nc.vector.tensor_copy(outT[:, i, :], k.bank(i % 8)[:, 0:NTOK]).then_inc(v_out, 1)

        @block.scalar
        def _(act):
            for i in range(1, n // 128, 2):
                act.wait_ge(product, i + 1)
                nc.scalar.copy(outT[:, i, :], k.bank(i % 8)[:, 0:NTOK]).then_inc(s_out, 1)


def norm_steps(k, z, stats, root, done, turn, out, gain, bias):
    nc, step = k.nc, k.dve_steps
    for h in range(2):
        step(nc.vector.bn_stats(stats[:, 6 * h:6 * h + 6], z[:, 512 * h:512 * (h + 1)]))
    step(nc.vector.bn_aggr(stats[:, 12:14], stats[:, 0:12]))
    nc.vector.tensor_scalar(stats[:, 14:15], stats[:, 13:14], LN_EPS, None, ALU.add).then_inc(root, 1)
    nc.vector.wait_ge(done, turn)
    step(nc.vector.reciprocal(stats[:, 15:16], stats[:, 15:16]))
    step(nc.vector.tensor_scalar(z, z, stats[:, 12:13], stats[:, 15:16], ALU.subtract, ALU.mult))
    step(nc.vector.tensor_tensor(z, z, gain, ALU.mult))
    step(nc.vector.tensor_tensor(out, z, bias, ALU.add))


def project_out_and_norm(k, name, catT, w_loads, gain, bias):
    nc = k.nc
    landed, row_landed, product = k.sem(name + "_w_landed"), k.sem(name + "_rows_landed"), k.sem(name + "_product")
    summed, root, rooted = k.sem(name + "_summed"), k.sem(name + "_variance"), k.sem(name + "_rooted")
    with ExitStack() as ctx:
        w = k.sbuf(name + "_w", [128, KC, D], ctx=ctx)
        g, b = k.sbuf(name + "_g", [128, D], ctx=ctx), k.sbuf(name + "_b", [128, D], ctx=ctx)
        z = k.sbuf(name + "_z", [128, D], ctx=ctx)
        stats = k.sbuf(name + "_stats", [128, 16], ctx=ctx)
        loads = w_loads(w)
        block = ctx.enter_context(nc.Block())

        @block.sync
        def _(sp):
            for dst, src in loads:
                sp.dma_start(dst, src).then_inc(landed, 16)
            sp.dma_start(g[:, :], gain.partition_broadcast(128)).then_inc(row_landed, 16)
            sp.dma_start(b[:, :], bias.partition_broadcast(128)).then_inc(row_landed, 16)

        @block.tensor
        def _(pe):
            pe.wait_ge(landed, 16 * len(loads))
            for t in range(TILES):
                for h in range(2):
                    for c in range(KC):
                        last = nc.tensor.matmul(k.bank(2 * t + h)[0:ROWS[t], :], catT[:, c, cols(t)],
                                                w[:, c, 512 * h:512 * (h + 1)], start=(c == 0), stop=(c == KC - 1))
                last.then_inc(product, 1)

        @block.vector
        def _(dve):
            dve.wait_ge(row_landed, 32)
            for t, r in enumerate(ROWS):
                dve.wait_ge(product, t + 1)
                mixed = k.ps[0:r, 2 * t:2 * t + 2, :].rearrange("p a b -> p (a b)")
                k.dve_steps(nc.vector.scalar_tensor_tensor(z[0:r, :], k.x[0:r, t, :], ALPHA, mixed, ALU.mult, ALU.add))
                norm_steps(k, z[0:r, :], stats[0:r, :], root, rooted, t + 1, k.x[0:r, t, :], g[0:r, :], b[0:r, :])

        @block.scalar
        def _(act):
            for t, r in enumerate(ROWS):
                act.wait_ge(root, t + 1)
                nc.scalar.activation(stats[0:r, 15:16], stats[0:r, 14:15], ACT.Sqrt).then_inc(rooted, 1)


def rotate(k, src, dst, tile_rows, heads, tmp):
    nc, step = k.nc, k.dve_steps
    t, r = tile_rows
    half = HD // 2
    cos, sin = bc(k.c("cos")[0:r, t, :], 1, heads), bc(k.c("sin")[0:r, t, :], 1, heads)
    s = src.rearrange("p (h d) -> p h d", d=HD)
    d = dst.rearrange("p (h d) -> p h d", d=HD)
    a, b, c, e = [tmp[0:r, i, 0:heads * half].rearrange("p (h d) -> p h d", d=half) for i in range(4)]
    nc.vector.tensor_tensor(a, s[:, :, 0:half], cos, ALU.mult)
    nc.vector.tensor_tensor(b, s[:, :, half:HD], sin, ALU.mult)
    nc.vector.tensor_tensor(c, s[:, :, 0:half], sin, ALU.mult)
    step(nc.vector.tensor_tensor(e, s[:, :, half:HD], cos, ALU.mult))
    nc.vector.tensor_tensor(d[:, :, 0:half], a, b, ALU.subtract)
    step(nc.vector.tensor_tensor(d[:, :, half:HD], c, e, ALU.add))




def attention(k, name, items):
    nc, step = k.nc, k.dve_steps
    n_items = len(items)
    scored, masked, expd, ready = [k.sem(f"{name}_{s}") for s in ("scored", "masked", "expd", "ready")]
    turned, copied, summed, left = [k.sem(f"{name}_{s}") for s in ("turned", "copied", "summed", "left")]
    rounds = [(i, j) for i, it in enumerate(items) for j in range(len(it["parts"]))]
    last_round = {i: max(r for r, (ii, _) in enumerate(rounds) if ii == i) for i in range(n_items)}
    leaving = [i for i, it in enumerate(items) if it["leave"]]
    first_round = {i: min(r for r, (ii, _) in enumerate(rounds) if ii == i) for i in range(n_items)}

    def left_before(i):
        need = 0
        for n, j in enumerate(leaving):
            if j < i and items[j]["bank"] == items[i]["bank"]:
                need = n + 1
        return need

    with ExitStack() as ctx:
        prob = k.sbuf(name + "_prob", [128, 3, 1024], ctx=ctx)
        probT = k.sbuf(name + "_probT", [128, 2, 512], ctx=ctx)
        top = k.sbuf(name + "_top", [128, 3, 4], ctx=ctx)
        low = k.sbuf(name + "_low", [128, 3, 4], ctx=ctx)
        den = k.sbuf(name + "_den", [128, 3, 4], ctx=ctx)
        inv = k.sbuf(name + "_inv", [128, 3, 4], ctx=ctx)
        block = ctx.enter_context(nc.Block())

        def flat(buf, i):
            it = items[i]
            return buf[0:it["rows"], i % 3, 0:it["groups"] * it["n"]]

        def view(buf, i):
            return flat(buf, i).rearrange("p (g n) -> p g n", n=items[i]["n"])

        def score_bank(i):
            return k.ps[:, 2 * (i % 2):2 * (i % 2) + 2, :].rearrange("p a b -> p (a b)")

        @block.tensor
        def _(pe):
            def scores(i):
                if i >= 2:
                    pe.wait_ge(masked, i - 1)
                for p0, pn, c0, cn, lhsT, rhs, start, stop in items[i]["scores"]:
                    last = nc.tensor.matmul(score_bank(i)[p0:p0 + pn, c0:c0 + cn], lhsT, rhs, start=start, stop=stop)
                last.then_inc(scored, 1)

            def turn(r):
                i, j = rounds[r]
                it = items[i]
                pe.wait_ge(ready, i + 1)
                if r >= 2:
                    pe.wait_ge(copied, r - 1)
                k0, kn, _ = it["parts"][j]
                for g in range(it["groups"]):
                    last = nc.tensor.transpose(k.bank(4 + r % 2)[0:kn, g * 128:g * 128 + it["rows"]],
                                               view(prob, i)[:, g, k0:k0 + kn], k.c("ident")[0:it["rows"], 0:it["rows"]])
                last.then_inc(turned, 1)

            def values(r):
                i, j = rounds[r]
                it = items[i]
                pe.wait_ge(copied, r + 1)
                if j == 0 and left_before(i):
                    pe.wait_ge(left, left_before(i))
                k0, kn, mms = it["parts"][j]
                for out, lhsT, pick, start, stop in mms:
                    last = nc.tensor.matmul(out, lhsT, pick(probT[0:kn, r % 2, :]), start=start, stop=stop,
                                            skip_group_check=True)
                last.then_inc(summed, 1)

            scores(0)
            for i in range(n_items):
                if i + 1 < n_items:
                    scores(i + 1)
                for r in range(first_round[i], last_round[i] + 1):
                    turn(r)
                    if r:
                        values(r - 1)
            values(len(rounds) - 1)

        @block.vector
        def _(dve):
            def mask_and_top(i):
                it = items[i]
                g, n, r = it["groups"], it["n"], it["rows"]
                dve.wait_ge(scored, i + 1)
                if i >= 3:
                    dve.wait_ge(turned, last_round[i - 3] + 1)
                apart = it.get("apart", n)
                sc = score_bank(i)[0:r, 0:g * apart].rearrange("p (g n) -> p g n", n=apart)[:, :, 0:n]
                if it["mask"] is None:
                    step(nc.vector.tensor_copy(view(prob, i), sc))
                else:
                    step(nc.vector.tensor_tensor(view(prob, i), sc, bc(it["mask"], 1, g), ALU.add))
                step(nc.vector.tensor_reduce(top[0:r, i % 3, 0:g], view(prob, i), AX, ALU.max))
                nc.vector.tensor_scalar(low[0:r, i % 3, 0:g], top[0:r, i % 3, 0:g], LEAST, -SCALE, ALU.max, ALU.mult)\
                    .then_inc(masked, 1)

            def normalise(i):
                it = items[i]
                g, n, r = it["groups"], it["n"], it["rows"]
                dve.wait_ge(expd, i + 1)
                d, v = den[0:r, i % 3, 0:g], inv[0:r, i % 3, 0:g]
                if it["count"] is not None:
                    step(nc.vector.tensor_tensor(view(prob, i), view(prob, i), bc(it["count"], 1, g), ALU.mult))
                    step(nc.vector.tensor_reduce(d, view(prob, i), AX, ALU.add))
                step(nc.vector.tensor_scalar(d, d, TINY, None, ALU.max))
                step(nc.vector.reciprocal(v, d))
                if it["gate"] is not None:
                    step(nc.vector.tensor_tensor(v, v, it["gate"], ALU.mult))
                nc.vector.tensor_tensor(view(prob, i), view(prob, i), bc(v, 2, n), ALU.mult).then_inc(ready, 1)

            def leave(i):
                if i in leaving:
                    dve.wait_ge(summed, last_round[i] + 1)
                    for dst, src in items[i]["leave"]:
                        last = nc.vector.tensor_copy(dst, src)
                    last.then_inc(left, 1)

            mask_and_top(0)
            for i in range(n_items):
                if i + 1 < n_items:
                    mask_and_top(i + 1)
                normalise(i)
                if i:
                    leave(i - 1)
            leave(n_items - 1)

        @block.scalar
        def _(act):
            def exps(i):
                it = items[i]
                r = it["rows"]
                act.wait_ge(masked, i + 1)
                for g in range(it["groups"]):
                    one = view(prob, i)[:, g, :]
                    if it["count"] is None:
                        last = nc.scalar.activation(one, one, ACT.Exp, bias=low[0:r, i % 3, g:g + 1], scale=SCALE,
                                                    accum_out=den[0:r, i % 3, g:g + 1])
                    else:
                        last = nc.scalar.activation(one, one, ACT.Exp, bias=low[0:r, i % 3, g:g + 1], scale=SCALE)
                last.then_inc(expd, 1)

            def copies(i):
                it = items[i]
                for r in range(first_round[i], last_round[i] + 1):
                    kn = it["parts"][r - first_round[i]][1]
                    act.wait_ge(turned, r + 1)
                    if r >= 2:
                        act.wait_ge(summed, r - 1)
                    w = (it["groups"] - 1) * 128 + it["rows"]
                    nc.scalar.copy(probT[0:kn, r % 2, 0:w], k.bank(4 + r % 2)[0:kn, 0:w]).then_inc(copied, 1)

            exps(0)
            for i in range(n_items):
                if i + 1 < n_items:
                    exps(i + 1)
                copies(i)




def recurrence(k, h, hT, cat, gamma, norm_g, state, state_prompt, state_sample):
    nc, step = k.nc, k.dve_steps
    C4 = 4
    pT = hT[:, 0:C4, :]
    fT = hT[:, C4:2 * C4, :]
    s = {n: k.sem("hg_" + n) for n in (
        "loaded", "gamma_turned", "gamma_read", "bounds_diff", "bounds_exp", "bounds_ready", "sigmoid", "factors", "products",
        "taken", "mask_landed", "keys_turned", "keys_out", "spread", "state_product", "out_product", "stored", "state_ready",
        "o_copied", "squares", "root", "gates")}
    with ExitStack() as ctx:
        masks = k.sbuf("level_masks", [128, len(LEVELS) + 1, 128], U32, ctx)
        key = k.sbuf("hg_key", [128, C4, NTOK], ctx=ctx)
        tot = [k.sbuf("hg_tot", [128, C4, NTOK], ctx=ctx) for _ in range(2)]
        sg = k.sbuf("hg_sigmoid", [128, 2 * C4, NTOK], ctx=ctx)
        att = k.sbuf("hg_att", [128, 2, HG, 128], ctx=ctx)
        cross = k.sbuf("hg_cross", [128, HG, 128], ctx=ctx)
        att_s = k.sbuf("hg_att_s", [NS, HG, NS], ctx=ctx)
        gam = k.sbuf("hg_gamma", [12, 128], ctx=ctx)
        small = k.sbuf("hg_small", [128, 48], ctx=ctx)
        s0 = k.sbuf("hg_state", [128, C4, DEC_B, HD], ctx=ctx)
        q_b = k.sbuf("hg_q_b", [128, C4, DEC_B, NS], ctx=ctx)
        keyT = k.sbuf("hg_keyT", [128, TILES, 512], ctx=ctx)
        v_b = k.sbuf("hg_v_b", [NS, 2, DEC_B, HD], ctx=ctx)
        fin = k.sbuf("hg_fin", [128, C4, HD], ctx=ctx)
        new = k.sbuf("hg_new", [128, C4, DEC_B, HD], ctx=ctx)

        with nc.Block() as block:
            @block.sync
            def _(sp):
                sp.dma_start(gam[:, :], gamma.rearrange("r (c p) -> (r c) p", p=128)).then_inc(s["loaded"], 16)
                sp.dma_start(masks[:, :, :], k.level_masks).then_inc(s["mask_landed"], 16)
                for c in range(C4):
                    src = state[0, :, 2 * c:2 * c + 2].rearrange("b h k v -> (h k) b v")
                    sp.dma_start(s0[:, c, :, :], src).then_inc(s["mask_landed"], 16)

            @block.tensor
            def _(pe):
                pe.wait_ge(s["loaded"], 16)
                nc.tensor.transpose(k.bank(0)[:, 0:12], gam[:, :], k.c("ident")[0:12, 0:12]).then_inc(s["gamma_turned"], 1)

            @block.scalar
            def _(act):
                nc.scalar.activation(sg[:, :, :], hT[:, :, :], ACT.Sigmoid).then_inc(s["sigmoid"], 1)
                act.wait_ge(s["bounds_diff"], 1)
                nc.scalar.activation(small[:, 16:28], small[:, 16:28], ACT.Exp).then_inc(s["bounds_exp"], 1)

            @block.vector
            def _(dve):
                dve.wait_ge(s["gamma_turned"], 1)
                step(nc.vector.tensor_copy(small[:, 0:12], k.bank(0)[:, 0:12]))
                step(nc.vector.tensor_tensor(small[:, 12:16], small[:, 0:4], small[:, 4:8], ALU.max))
                step(nc.vector.tensor_tensor(small[:, 12:16], small[:, 12:16], small[:, 8:12], ALU.max))
                nc.vector.tensor_tensor(small[:, 16:28].rearrange("p (r c) -> p r c", c=4),
                                        small[:, 0:12].rearrange("p (r c) -> p r c", c=4),
                                        bc(small[:, 12:16], 1, 3), ALU.subtract).then_inc(s["bounds_diff"], 1)
                dve.wait_ge(s["bounds_exp"], 1)
                step(nc.vector.tensor_tensor(small[:, 28:32], small[:, 16:20], small[:, 20:24], ALU.add))
                step(nc.vector.tensor_tensor(small[:, 28:32], small[:, 28:32], small[:, 24:28], ALU.add))
                step(nc.vector.reciprocal(small[:, 28:32], small[:, 28:32]))
                step(nc.vector.tensor_tensor(small[:, 32:36], small[:, 16:20], small[:, 28:32], ALU.mult))
                step(nc.vector.tensor_scalar(small[:, 36:40], small[:, 32:36], -1.0, 1.0, ALU.mult, ALU.add))
                dve.wait_ge(s["sigmoid"], 1)
                nc.vector.tensor_tensor(pT, pT, sg[:, 0:C4, :], ALU.mult)
                for c in range(C4):
                    step(nc.vector.tensor_scalar(fT[:, c, :], sg[:, C4 + c, :], small[:, 36 + c:37 + c],
                                                 small[:, 32 + c:33 + c], ALU.mult, ALU.add))
                nc.vector.tensor_scalar(key[:, :, :], fT, -1.0, 1.0, ALU.mult, ALU.add)
                nc.vector.memset(att[:, :, :, :], 0.0)
                nc.vector.memset(att_s[:, :, :], 0.0)
                step(nc.vector.tensor_copy(tot[0][:, :, :], fT))
            @block.gpsimd
            def _(pool):
                pool.wait_ge(s["mask_landed"], 16 * (1 + C4))

        def level_products(a, b):
            for t in range(2):
                for hd in range(HG):
                    p = slice(64 * (hd % 2), 64 * (hd % 2) + 64)
                    dst = k.bank(2 * t + hd % 2)[:, (hd // 2) * 128:(hd // 2 + 1) * 128]
                    last = nc.tensor.matmul(dst, a[p, hd // 2, cols(t)], b[p, hd // 2, cols(t)], start=True, stop=True,
                                            skip_group_check=True)
            return last

        def sample_products(a, b):
            for hd in range(HG):
                p = slice(64 * (hd % 2), 64 * (hd % 2) + 64)
                last = nc.tensor.matmul(k.bank(4 + hd % 2)[0:NS, (hd // 2) * NS:(hd // 2 + 1) * NS], a[p, hd // 2, cols(2)], b[p, hd // 2, cols(2)],
                                        start=True, stop=True, skip_group_check=True)
            return last

        s_levels = 3
        with nc.Block() as block:
            @block.tensor
            def _(pe):
                for n in range(len(LEVELS) + 1):
                    if n:
                        pe.wait_ge(s["factors"], n)
                    if n < s_levels:
                        sample_products(key, pT)
                    level_products(key, pT).then_inc(s["products"], 1)
                pe.wait_ge(s["factors"], len(LEVELS) + 1)
                for hd in range(HG):
                    p = slice(64 * (hd % 2), 64 * (hd % 2) + 64)
                    last = nc.tensor.matmul(k.bank(6 + hd % 2)[:, (hd // 2) * 128:(hd // 2 + 1) * 128], key[p, hd // 2, cols(0)],
                                            pT[p, hd // 2, cols(1)], start=True, stop=True, skip_group_check=True)
                last.then_inc(s["products"], 1)

            @block.vector
            def _(dve):
                def halves(x, a, b, m):
                    v = x[:, :, a:b].rearrange("p c (n z m) -> p c n z m", z=2, m=m)
                    return v[:, :, :, 0, :], v[:, :, :, 1, :]

                for n in range(len(LEVELS) + 1):
                    dve.wait_ge(s["products"], n + 1)
                    for t in range(2):
                        src = k.ps[:, 2 * t:2 * t + 2, :].rearrange("p a (b t) -> p (a b) t", t=128)
                        last = nc.vector.copy_predicated(att[:, t, :, :], bc(masks[:, n, :], 1, HG), src)
                    if n < s_levels:
                        for odd in range(2):
                            last = nc.vector.copy_predicated(att_s[:, C4 * odd:C4 * (odd + 1), :], bc(masks[0:NS, n, 0:NS], 1, C4),
                                                             k.bank(4 + odd)[0:NS, 0:C4 * NS].rearrange("p (h t) -> p h t", t=NS))
                    step(last)
                    if n == 0:
                        nc.vector.tensor_tensor(pT, pT, fT, ALU.mult).then_inc(s["factors"], 1)
                        continue
                    m = LEVELS[n - 1]
                    old, nxt = tot[(n - 1) % 2], tot[n % 2]
                    ranges = [(0, SEQ)] + ([(SEQ, NTOK)] if m < DEC_T else [])
                    for a, b in ranges:
                        cnt = (b - a) // (2 * m)
                        o = old[:, :, a:a + 2 * cnt].rearrange("p c (n z) -> p c n z", z=2)
                        k1, _ = halves(key, a, b, m)
                        _, q2 = halves(pT, a, b, m)
                        nc.vector.tensor_tensor(q2, q2, bc(o[:, :, :, 0], 3, m), ALU.mult)
                        nc.vector.tensor_tensor(k1, k1, bc(o[:, :, :, 1], 3, m), ALU.mult)
                        last = nc.vector.tensor_tensor(nxt[:, :, a:a + cnt], o[:, :, :, 0], o[:, :, :, 1], ALU.mult)
                    if m >= DEC_T:
                        last = nc.vector.tensor_copy(nxt[:, :, SEQ:SEQ + DEC_B], old[:, :, SEQ:SEQ + DEC_B])
                    step(last)
                    nc.vector.memset(small[:, 40:41], 0.0).then_inc(s["factors"], 1)
                dve.wait_ge(s["products"], len(LEVELS) + 2)
                step(nc.vector.tensor_copy(cross[:, :, :], k.ps[:, 6:8, :].rearrange("p a (b t) -> p (a b) t", t=128)))
                tN = tot[len(LEVELS) % 2]
                step(nc.vector.tensor_tensor(key[:, :, 0:128], key[:, :, 0:128], tN[:, :, 1:2].broadcast_to([128, C4, 128]), ALU.mult))
                for c in range(C4):
                    last = nc.vector.tensor_tensor(q_b[:, c, :, :], bc(pT[:, c, SEQ:NTOK], 1, DEC_B), k.c("batch_cols"), ALU.mult)
                step(last)
        tN = tot[len(LEVELS) % 2]

        transposes(k, "hg_keys", [([key[:, c, cols(t)] for c in range(C4)], keyT[0:ROWS[t], t, :].rearrange("p (c x) -> p c x", x=128))
                                  for t in range(TILES)])

        with nc.Block() as block:
            @block.vector
            def _(dve):
                for hd in range(HG):
                    if hd >= 2:
                        dve.wait_ge(s["state_product"], hd - 1)
                    vs = h[0:NS, 2, V0 + HD * hd:V0 + HD * (hd + 1)]
                    nc.vector.tensor_tensor(v_b[:, hd % 2, :, :], bc(vs, 1, DEC_B),
                                            bc(k.c("batch_rows")[0:NS, :], 2, HD), ALU.mult).then_inc(s["spread"], 1)
                dve.wait_ge(s["out_product"], 1)
                step(nc.vector.tensor_copy(fin[:, :, :], k.bank(3)[:, 256:512].rearrange("p (c v) -> p c v", v=HD)))
                dve.wait_ge(s["state_product"], HG)
                for c in range(C4):
                    step(nc.vector.tensor_tensor(new[:, c], s0[:, c], bc(tN[:, c, SEQ:SEQ + DEC_B], 2, HD), ALU.mult))
                    step(nc.vector.tensor_tensor(new[:, c], new[:, c], k.bank(4 + c).rearrange("p (b v) -> p b v", v=HD), ALU.add))
                nc.vector.memset(k.pad[:, :], 0.0).then_inc(s["state_ready"], 1)

            @block.tensor
            def _(pe):
                mm = lambda *a, **b: nc.tensor.matmul(*a, skip_group_check=True, **b)
                for hd in range(HG):
                    odd, c = hd % 2, hd // 2
                    p = slice(64 * odd, 64 * odd + 64)
                    hv = slice(V0 + HD * hd, V0 + HD * (hd + 1))
                    hk = slice(HD * hd, HD * (hd + 1))
                    place = C4 * odd + c
                    at = slice(HD * place, HD * (place + 1))
                    o = [k.bank(t)[0:ROWS[t], at] for t in range(TILES)]
                    mm(o[0], att[:, 0, place, :], h[:, 0, hv], start=True, stop=True)
                    mm(o[1], att[:, 1, place, :], h[:, 1, hv], start=True, stop=False)
                    mm(o[1], cross[:, place, :], h[:, 0, hv], start=False, stop=True)
                    mm(o[2], att_s[:, place, :], h[0:NS, 2, hv], start=True, stop=bool(odd))
                    own = k.bank(3)[0:NS, HD * c:HD * (c + 1)] if odd else o[2]
                    for b in range(DEC_B):
                        mm(own, q_b[p, c, b, :], s0[p, c, b, :], start=bool(odd and b == 0), stop=(b == DEC_B - 1))
                    last_state = k.bank(3)[p, 256 + HD * c:256 + HD * (c + 1)]
                    mm(last_state, keyT[:, 0, hk], h[:, 0, hv], start=True, stop=False)
                    last = mm(last_state, keyT[:, 1, hk], h[:, 1, hv], start=False, stop=True)
                last.then_inc(s["out_product"], 1)
                for hd in range(HG):
                    pe.wait_ge(s["spread"], hd + 1)
                    p = slice(64 * (hd % 2), 64 * (hd % 2) + 64)
                    mm(k.bank(4 + hd // 2)[p, :], keyT[0:NS, 2, HD * hd:HD * (hd + 1)],
                       v_b[:, hd % 2].rearrange("p b v -> p (b v)"), start=True, stop=True).then_inc(s["state_product"], 1)

            @block.sync
            def _(sp):
                sp.wait_ge(s["state_ready"], 1)
                sp.dma_start(state_prompt[0, 0].rearrange("(c e) k v -> (e k) c v", e=2), fin[:, :, :]).then_inc(s["stored"], 16)
                for c in range(C4):
                    dst = state_sample[0, :, 2 * c:2 * c + 2].rearrange("b h k v -> (h k) b v")
                    sp.dma_start(dst, new[:, c]).then_inc(s["stored"], 16)
                sp.wait_ge(s["stored"], 16 * (1 + C4))

    with ExitStack() as ctx:
        o = k.sbuf("hg_o", [128, 512], ctx=ctx)
        sq = k.sbuf("hg_sq", [128, 512], ctx=ctx)
        sgate = k.sbuf("hg_sgate", [128, TILES, 512], ctx=ctx)
        ms = k.sbuf("hg_ms", [128, 16], ctx=ctx)
        g = k.sbuf("hg_norm_g", [128, 512], ctx=ctx)
        row = k.sem("hg_row")
        block = ctx.enter_context(nc.Block())

        @block.sync
        def _(sp):
            sp.dma_start(g[:, :], norm_g.partition_broadcast(128)).then_inc(row, 16)

        @block.scalar
        def _(act):
            for t, r in enumerate(ROWS):
                nc.scalar.activation(sgate[0:r, t, :], h[0:r, t, G0:G0 + 512], ACT.Sigmoid).then_inc(s["gates"], 1)
            for t, r in enumerate(ROWS):
                act.wait_ge(s["squares"], t + 1)
                nc.scalar.activation(ms[0:r, 8:16], ms[0:r, 0:8], ACT.Sqrt).then_inc(s["root"], 1)

        @block.vector
        def _(dve):
            dve.wait_ge(row, 16)
            for t, r in enumerate(ROWS):
                dve.wait_ge(s["gates"], t + 1)
                per_head = lambda x: x.rearrange("p (h v) -> p h v", v=HD)
                for odd in range(2):
                    src = k.bank(t)[0:r, 256 * odd:256 * (odd + 1)].rearrange("p (c v) -> p c v", v=HD)
                    dst = o[0:r, :].rearrange("p (c e v) -> p c e v", e=2, v=HD)[:, :, odd, :]
                    step(nc.vector.tensor_copy(dst, src))
                if t == 2:
                    step(nc.vector.tensor_tensor(dst, dst, k.bank(3)[0:r, 0:256].rearrange("p (c v) -> p c v", v=HD), ALU.add))
                step(nc.vector.tensor_tensor(sq[0:r, :], o[0:r, :], o[0:r, :], ALU.mult))
                step(nc.vector.tensor_reduce(ms[0:r, 0:8], per_head(sq[0:r, :]), AX, ALU.add))
                step(nc.vector.tensor_scalar(ms[0:r, 0:8], ms[0:r, 0:8], 1.0 / HD, RMS_EPS, ALU.mult, ALU.add))
                nc.vector.memset(k.pad[0:r, :], 0.0).then_inc(s["squares"], 1)
                dve.wait_ge(s["root"], t + 1)
                step(nc.vector.reciprocal(ms[0:r, 8:16], ms[0:r, 8:16]))
                step(nc.vector.tensor_tensor(per_head(o[0:r, :]), per_head(o[0:r, :]), bc(ms[0:r, 8:16], 2, HD), ALU.mult))
                step(nc.vector.tensor_tensor(o[0:r, :], o[0:r, :], g[0:r, :], ALU.mult))
                step(nc.vector.tensor_tensor(sq[0:r, :], h[0:r, t, G0:G0 + 512], sgate[0:r, t, :], ALU.mult))
                step(nc.vector.tensor_tensor(cat[0:r, t, :], o[0:r, :], sq[0:r, :], ALU.mult))




def sparse_attention(k, h, catT, pages, cmp_cache, slc_cache, win_cache, pe_rows, outs):
    nc, step = k.nc, k.dve_steps
    stored = k.sem("kv_stored")
    (cmp_p, cmp_s, slc_p, slc_s, win_p, win_s) = outs
    with ExitStack() as outer:
        qn = k.sbuf("qn", [128, TILES, 512], ctx=outer)
        qr = k.sbuf("qr", [128, TILES, 512], ctx=outer)
        gates = k.sbuf("gates", [128, TILES, 24], ctx=outer)
        gates_s = k.sbuf("gates_s", [128, 6], ctx=outer)
        qT = {n: k.sbuf("q_T" + n, [128, GR, NTOK], ctx=outer) for n in ("nope", "rope")}
        kT = {n: k.sbuf("kT_" + n, [128, NTOK], ctx=outer) for n in ("slc", "win")}
        cache = {n: k.sbuf("cache_" + n, [128, DEC_B, NPG, 256], ctx=outer) for n in ("cmp", "slc", "win")}
        kTs = {n: k.sbuf("kTs_" + n, [128, DEC_B, PAST], ctx=outer) for n in ("slc", "win")}
        q_b = {n: k.sbuf("q_b" + n, [128, DEC_B, GR, NS], ctx=outer) for n in ("nope", "rope")}
        q_new = k.sbuf("q_new", [128, GR, NS], ctx=outer)
        kc = k.sbuf("kc", [128, 1 + DEC_B, NBLK], ctx=outer)
        vc = k.sbuf("vc", [NBLK, 1 + DEC_B, 128], ctx=outer)
        pe_sb = k.sbuf("cmp_pe", [32, 128], ctx=outer)
        pt = k.sbuf("pages", [128, 16], I32, outer)
        ptf = k.sbuf("pages_f", [128, 16], ctx=outer)
        idx = k.sbuf("page_rows", [128, 16], U32, outer)
        tmp = k.sbuf("rot_tmp", [128, 4, 256], ctx=outer)
        pt_landed, idx_ready, gathered, pe_landed = k.sem("pages_landed"), k.sem("page_rows_ready"), k.sem("pages_gathered"), k.sem("pe_landed")
        gate_done, rotated, regrouped = k.sem("gates_ready"), k.sem("rotated"), k.sem("regrouped")

        with nc.Block() as block:
            @block.sync
            def _(sp):
                sp.dma_start(pt[:, :], pages.rearrange("b n -> (b n)").partition_broadcast(128)).then_inc(pt_landed, 16)
                sp.dma_start(pe_sb[:, :], pe_rows[0].rearrange("r h d -> r (h d)")).then_inc(pe_landed, 16)
                for b in range(DEC_B):
                    sp.dma_start(cache["win"][:, b], win_cache[0, b].rearrange("(n p) x h d -> p n (x h d)", p=128)).then_inc(pe_landed, 16)
                sp.wait_ge(rotated, 1)
                for at, prompt, sample in ((CMP0, cmp_p, cmp_s), (SLC0, slc_p, slc_s), (WIN0, win_p, win_s)):
                    sp.dma_start(prompt[0, 0].rearrange("(t p) x h d -> p t (x h d)", p=128), h[:, 0:2, at:at + 256]).then_inc(stored, 16)
                    sp.dma_start(sample[0].rearrange("b t x h d -> (b t) (x h d)"), h[0:NS, 2, at:at + 256]).then_inc(stored, 16)
                sp.wait_ge(pe_landed, 16 * (1 + DEC_B))
                sp.wait_ge(stored, 16 * 6)

            @block.scalar
            def _(act):
                for t, r in enumerate(ROWS):
                    src = h[0:r, t, Q0:Q0 + 512].rearrange("p (kv g d) -> p g kv d", kv=KV, g=GR)
                    dst = qn[0:r, t, :].rearrange("p (g kv d) -> p g kv d", kv=KV, g=GR)
                    nc.scalar.copy(dst, src).then_inc(regrouped, 1)
                for t, r in enumerate(ROWS):
                    nc.scalar.activation(gates[0:r, t, :], h[0:r, t, GATE0:GATE0 + 24], ACT.Sigmoid).then_inc(gate_done, 1)

            @block.vector
            def _(dve):
                dve.wait_ge(pt_landed, 16)
                step(nc.vector.tensor_copy(ptf[:, :], pt[:, :]))
                step(nc.vector.tensor_scalar(ptf[:, :], ptf[:, :], float(PAGE), k.c("row"), ALU.mult, ALU.add))
                nc.vector.tensor_copy(idx[:, :], ptf[:, :]).then_inc(idx_ready, 1)
                for t, r in enumerate(ROWS):
                    dve.wait_ge(regrouped, t + 1)
                    rotate(k, qn[0:r, t, :], qr[0:r, t, :], (t, r), 8, tmp)
                    for at in (SLC0, WIN0):
                        rotate(k, h[0:r, t, at:at + 128], h[0:r, t, at:at + 128], (t, r), KV, tmp)
                nc.vector.memset(k.pad[:, :], 0.0).then_inc(rotated, 1)
                dve.wait_ge(gate_done, TILES)
                for g in range(GR):
                    src = gates[0:NS, 2, :].rearrange("p (a g) -> p a g", g=GR)[:, :, g]
                    last = nc.vector.tensor_copy(gates_s[NS * g:NS * (g + 1), :], src)
                step(last)

            @block.gpsimd
            def _(pool):
                pool.wait_ge(idx_ready, 1)
                for n, src in (("cmp", cmp_cache), ("slc", slc_cache)):
                    rows = src[0].rearrange("n p x h d -> (n p) (x h d)")
                    for j in range(DEC_B * NPG):
                        nc.gpsimd.indirect_dma_start(out=cache[n][:, j // NPG, j % NPG, :], out_offset=None, in_=rows,
                                                     in_offset=bass.IndirectOffsetOnAxis(ap=idx[:, j:j + 1], axis=0)).then_inc(gathered, 16)
                pool.wait_ge(gathered, 16 * 2 * DEC_B * NPG)

        groups = []
        for t, r in enumerate(ROWS):
            for n, x in (("nope", qn), ("rope", qr)):
                groups.append(([x[0:r, t, 128 * g:128 * (g + 1)] for g in range(GR)], qT[n][:, :, cols(t)]))
            for n, at in (("slc", SLC0), ("win", WIN0)):
                groups.append(([h[0:r, t, at:at + 128]], kT[n][:, cols(t)]))
        for n in ("slc", "win"):
            for b in range(0, DEC_B, 2):
                groups.append(([cache[n][:, b + j // NPG, j % NPG, 0:128] for j in range(2 * NPG)],
                               kTs[n][:, b:b + 2, :].rearrange("p b s -> p (b s)")))
        transposes(k, "nsa", groups)

        pooled = k.sem("pooled")
        with nc.Block() as block:
            @block.tensor
            def _(pe):
                pool, mean = k.c("pool"), k.c("mean32")
                mm = lambda *a, **b: nc.tensor.matmul(*a, skip_group_check=True, **b)
                for i in range(1 + DEC_B):
                    raw = (lambda t: h[:, t, CMP0:CMP0 + 256]) if i == 0 else (lambda t, b=i - 1: cache["cmp"][:, b, t, :])
                    kk, vv = k.bank(0)[:, NBLK * i:NBLK * (i + 1)], k.bank(1 + i // 4)[0:NBLK, 128 * (i % 4):128 * (i % 4 + 1)]
                    for t in range(NPG):
                        mm(kk, raw(t)[:, 0:128], pool[:, t, :], start=(t == 0), stop=False)
                        mm(vv, pool[:, t, :], raw(t)[:, 128:256], start=(t == 0), stop=(t == NPG - 1))
                    last = mm(kk, pe_sb[:, :], mean[0:32, :], start=False, stop=True)
                last.then_inc(pooled, 1)

            @block.vector
            def _(dve):
                for n in ("nope", "rope"):
                    for g in range(GR):
                        last = nc.vector.tensor_tensor(q_b[n][:, :, g, :], bc(qT[n][:, g, SEQ:NTOK], 1, DEC_B), k.c("batch_cols"), ALU.mult)
                nc.vector.tensor_copy(q_new[:, :, :], qT["rope"][:, :, SEQ:NTOK])
                dve.wait_ge(pooled, 1)
                nc.vector.tensor_copy(kc[:, :, :], k.bank(0)[:, 0:NBLK * (1 + DEC_B)].rearrange("p (i c) -> p i c", c=NBLK))
                step(nc.vector.tensor_copy(vc[:, :, :].rearrange("p i d -> p (i d)"),
                                           k.ps[0:NBLK, 1:4, :].rearrange("p a b -> p (a b)")[:, 0:128 * (1 + DEC_B)]))

        items = []
        for t in range(2):
            bank = 6 + t
            out = k.bank(bank).rearrange("p (g q) -> p g q", q=128)
            for br, n in ((1, "slc"), (2, "win"), (0, "cmp")):
                for kv in range(KV):
                    p = slice(64 * kv, 64 * kv + 64)
                    nk = NBLK if n == "cmp" else 128 * (t + 1)
                    q = qT["nope" if n == "cmp" else "rope"]
                    keys = kc[p, 0, :] if n == "cmp" else kT[n][p, 0:nk]
                    base = {"cmp": CMP0, "slc": SLC0, "win": WIN0}[n] + 128
                    parts = []
                    for j in range(1 if n == "cmp" else t + 1):
                        val = vc[:, 0, p] if n == "cmp" else h[:, j, base + 64 * kv:base + 64 * kv + 64]
                        kn = NBLK if n == "cmp" else 128
                        parts.append((128 * j, kn, [(k.bank(bank)[p, :], val, lambda pT: pT,
                                                     n == "slc" and j == 0, n == "cmp")]))
                    gate = gates[:, t, :].rearrange("p (a k g) -> p a k g", a=3, k=KV)[:, br, kv, :]
                    leave = [(catT[:, 4:8, cols(t)], out)] if (n, kv) == ("cmp", KV - 1) else []
                    items.append(dict(
                        rows=128, groups=GR, n=nk, mask=k.c("cmp_mask")[:, t, :] if n == "cmp" else k.c("causal")[:, t, 0:nk],
                        scores=[(0, 128, g * nk, nk, q[p, g, cols(t)], keys, True, True) for g in range(GR)],
                        count=None, gate=gate, parts=parts, bank=bank, leave=leave))
        out = k.bank(6)[:, 0:GR * NS]
        for br, n in ((1, "slc"), (2, "win"), (0, "cmp")):
            for kv in range(KV):
                p = slice(64 * kv, 64 * kv + 64)
                nk = NBLK if n == "cmp" else PAST + NS
                qb = q_b["nope" if n == "cmp" else "rope"]
                keys = (lambda b: kc[p, 1 + b, :]) if n == "cmp" else (lambda b: kTs[n][p, b, :])
                width = NBLK if n == "cmp" else PAST
                scores = [(0, 128, 0, width, qb[p, b].rearrange("p g t -> p (g t)"), keys(b), b == 0, b == DEC_B - 1) for b in range(DEC_B)]
                own = lambda b: (lambda pT: pT[:, 0:128].rearrange("p (g t) -> p g t", t=NS)[:, :, DEC_T * b:DEC_T * (b + 1)])
                dst = lambda b: out[p, :].rearrange("p (g t) -> p g t", t=NS)[:, :, DEC_T * b:DEC_T * (b + 1)]
                base = {"cmp": CMP0, "slc": SLC0, "win": WIN0}[n] + 128 + 64 * kv
                if n == "cmp":
                    parts = [(0, NBLK, [(dst(b), vc[:, 1 + b, p], own(b), False, True) for b in range(DEC_B)])]
                else:
                    scores.append((0, 128, PAST, NS, q_new[p].rearrange("p g t -> p (g t)"), kT[n][p, SEQ:NTOK], True, True))
                    parts = [(PAST, NS, [(out[p, :], h[0:NS, 2, base:base + 64], lambda pT: pT[:, 0:128], n == "slc", False)])]
                    parts += [(128 * j, 128, [(dst(b), cache[n][:, b, j, 128 + 64 * kv:192 + 64 * kv], own(b), False, False)
                                              for b in range(DEC_B)]) for j in range(NPG)]
                leave = [(catT[:, 4:8, SEQ:NTOK], out.rearrange("p (g t) -> p g t", t=NS))] if (n, kv) == ("cmp", KV - 1) else []
                items.append(dict(rows=128, groups=1, n=nk, mask=None if n == "cmp" else k.c("new_causal"), scores=scores, count=None,
                                  gate=gates_s[:, KV * br + kv:KV * br + kv + 1], parts=parts, bank=6, leave=leave))
        attention(k, "nsa", items)




def dilated_attention(k, h, catT, cache, out_p, out_s):
    nc, step = k.nc, k.dve_steps
    K0, VV0 = D, 2 * D
    stored, rotated = k.sem("dil_stored"), k.sem("dil_rotated")
    with ExitStack() as outer:
        qT = k.sbuf("dil_qT", [128, HP, NTOK], ctx=outer)
        kT = k.sbuf("dil_kT", [128, HP, NTOK], ctx=outer)
        with ExitStack() as ctx:
            tmp = k.sbuf("dil_tmp", [128, 4, 512], ctx=ctx)
            block = ctx.enter_context(nc.Block())

            @block.vector
            def _(dve):
                for t, r in enumerate(ROWS):
                    for at in (0, K0):
                        rotate(k, h[0:r, t, at:at + D], h[0:r, t, at:at + D], (t, r), HEADS, tmp)
                nc.vector.memset(k.pad[:, :], 0.0).then_inc(rotated, 1)

            @block.sync
            def _(sp):
                sp.wait_ge(rotated, 1)
                sp.dma_start(out_p[0, 0].rearrange("(t p) x h d -> p t (x h d)", p=128), h[:, 0:2, K0:K0 + 2 * D]).then_inc(stored, 16)
                sp.dma_start(out_s[0].rearrange("b t x h d -> (b t) (x h d)"), h[0:NS, 2, K0:K0 + 2 * D]).then_inc(stored, 16)
                sp.wait_ge(stored, 32)
        groups = []
        for t, r in enumerate(ROWS):
            for dst, at in ((qT, 0), (kT, K0)):
                for c in range(0, HP, 4):
                    groups.append(([h[0:r, t, at + 128 * (c + j):at + 128 * (c + j + 1)] for j in range(4)], dst[:, c:c + 4, cols(t)]))
        transposes(k, "dil", groups)

        items = []
        for t in range(2):
            nk = 128 * (t + 1)
            for q4 in range(HEADS // 4):
                bank = 6 + len(items) % 2
                head = [4 * q4 + g for g in (0, 2, 1, 3)]
                parts = []
                for j in range(t + 1):
                    parts.append((128 * j, 128, [
                        (k.bank(bank)[64 * (head[g] % 2):64 * (head[g] % 2) + 64, 128 * (g % 2):128 * (g % 2 + 1)],
                         h[:, j, VV0 + HD * head[g]:VV0 + HD * (head[g] + 1)], (lambda pT, g=g: pT[:, 128 * g:128 * (g + 1)]),
                         j == 0 and g % 2 == 0, j == t) for g in range(4)]))
                items.append(dict(
                    rows=128, groups=4, n=nk, apart=SEQ, mask=k.c("dil_mask")[:, t, 0:nk], count=k.c("dil_count")[:, t, 0:nk], gate=None,
                    scores=[(0, 128, g * SEQ, nk, qT[64 * (hd % 2):64 * (hd % 2) + 64, hd // 2, cols(t)],
                             kT[64 * (hd % 2):64 * (hd % 2) + 64, hd // 2, 0:nk], True, True) for g, hd in enumerate(head)],
                    parts=parts, bank=bank,
                    leave=[(catT[:, 2 * q4:2 * q4 + 2, cols(t)], k.bank(bank)[:, 0:256].rearrange("p (c q) -> p c q", q=128))]))
        attention(k, "dil_p", items)

        for q4 in range(HEADS // 4):
            with ExitStack() as ctx:
                kv = k.sbuf("dil_cache", [128, 2, DEC_B, NPG, 256], ctx=ctx)
                kTs = k.sbuf("dil_kTs", [128, 2, DEC_B, PAST], ctx=ctx)
                q_b = k.sbuf("dil_q_b", [128, 2, DEC_B, NS], ctx=ctx)
                landed = k.sem("dil_cache_landed")
                with nc.Block() as block:
                    @block.sync
                    def _(sp):
                        for x in range(2):
                            for b in range(DEC_B):
                                src = cache[0, b, :, x, 4 * q4:4 * q4 + 4].rearrange("(n p) h d -> p n (h d)", p=128)
                                sp.dma_start(kv[:, x, b], src).then_inc(landed, 16)
                        sp.wait_ge(landed, 32 * DEC_B)

                    @block.vector
                    def _(dve):
                        for c in range(2):
                            last = nc.vector.tensor_tensor(q_b[:, c], bc(qT[:, 2 * q4 + c, SEQ:NTOK], 1, DEC_B), k.c("batch_cols"), ALU.mult)
                        step(last)
                groups = []
                for c in range(2):
                    for b in range(0, DEC_B, 2):
                        groups.append(([kv[:, 0, b + j // NPG, j % NPG, 128 * c:128 * (c + 1)] for j in range(2 * NPG)],
                                       kTs[:, c, b:b + 2, :].rearrange("p b s -> p (b s)")))
                transposes(k, f"dil_s{q4}", groups)
                scores, new, old = [], [], [[] for _ in range(NPG)]
                out = lambda g: k.bank(6)[64 * (g % 2):64 * (g % 2) + 64, NS * (g // 2):NS * (g // 2 + 1)]
                for g in range(4):
                    p = slice(64 * (g % 2), 64 * (g % 2) + 64)
                    hd = 4 * q4 + g
                    for b in range(DEC_B):
                        scores.append((NS * g, NS, 0, PAST, q_b[p, g // 2, b, :], kTs[p, g // 2, b, :], b == 0, b == DEC_B - 1))
                        for j in range(NPG):
                            c0 = NS * g + DEC_T * b
                            old[j].append((out(g)[:, DEC_T * b:DEC_T * (b + 1)], kv[:, 1, b, j, HD * g:HD * (g + 1)],
                                           (lambda pT, c0=c0: pT[:, c0:c0 + DEC_T]), False, j == NPG - 1))
                    scores.append((NS * g, NS, PAST, NS, qT[p, hd // 2, SEQ:NTOK], kT[p, hd // 2, SEQ:NTOK], True, True))
                    new.append((out(g), h[0:NS, 2, VV0 + HD * hd:VV0 + HD * (hd + 1)],
                                (lambda pT, g=g: pT[:, NS * g:NS * (g + 1)]), g < 2, False))
                parts = [(PAST, NS, new)] + [(128 * j, 128, old[j]) for j in range(NPG)]
                attention(k, f"dil_s{q4}", [dict(
                    rows=128, groups=1, n=PAST + NS, mask=k.c("new_mask"), count=k.c("new_count"), gate=None, scores=scores,
                    parts=parts, bank=6, leave=[(catT[:, 2 * q4:2 * q4 + 2, SEQ:NTOK], k.bank(6)[:, 0:2 * NS].rearrange("p (c q) -> p c q", q=NS))])])




def route(k, name, layer, w_q, sub_keys, slots, gate):
    nc, step = k.nc, k.dve_steps
    HC = 2 * PH
    with ExitStack() as ctx:
        qT = k.sbuf(name + "_qT", [128, HC, NTOK], ctx=ctx)
        keysT = k.sbuf(name + "_keysT", [128, HC, NK], ctx=ctx)
        project_cols(k, name + "_q", w_q[layer], HC * 128, qT)
        with ExitStack() as load:
            keys = k.sbuf(name + "_keys", [128, HC, 128], ctx=load)
            landed = k.sem(name + "_keys_landed")
            with nc.Block() as block:
                @block.sync
                def _(sp):
                    sp.dma_start(keys[:, :, :], sub_keys[layer].rearrange("h c k d -> k (h c) d")).then_inc(landed, 16)
                    sp.wait_ge(landed, 16)
            transposes(k, name + "_keys", [([keys[:, 4 * i + j, :] for j in range(4)], keysT[:, 4 * i:4 * i + 4, :]) for i in range(4)])
        s = k.sbuf(name + "_s", [128, HC, NK], ctx=ctx)
        s2 = k.sbuf(name + "_s2", [128, HC, NK], ctx=ctx)
        val = k.sbuf(name + "_val", [128, HC, PK], ctx=ctx)
        at = k.sbuf(name + "_at", [128, HC, PK], U32, ctx)
        atf = k.sbuf(name + "_atf", [128, HC, PK], ctx=ctx)
        cand = k.sbuf(name + "_cand", [128, PH, PK * PK], ctx=ctx)
        cand2 = k.sbuf(name + "_cand2", [128, PH, PK * PK], ctx=ctx)
        top = k.sbuf(name + "_top", [128, PH, PK], ctx=ctx)
        sel = k.sbuf(name + "_sel", [128, PH, PK], U32, ctx)
        half = k.sbuf(name + "_half", [128, 2, PH, PK], U32, ctx)
        halff = k.sbuf(name + "_halff", [128, 2, PH, PK], ctx=ctx)
        ef = k.sbuf(name + "_ef", [128, 2, PH, PK], ctx=ctx)
        e = k.sbuf(name + "_e", [128, PH, PK], ctx=ctx)
        den = k.sbuf(name + "_den", [128, PH], ctx=ctx)
        scored, read, less, expd = k.sem(name + "_scored"), k.sem(name + "_read"), k.sem(name + "_less_top"), k.sem(name + "_expd")
        block = ctx.enter_context(nc.Block())

        @block.tensor
        def _(pe):
            for t, r in enumerate(ROWS):
                if t >= 2:
                    pe.wait_ge(read, t - 1)
                for i in range(HC):
                    last = nc.tensor.matmul(k.bank(4 * (t % 2) + i // 4)[0:r, 128 * (i % 4):128 * (i % 4 + 1)], qT[:, i, cols(t)],
                                            keysT[:, i, :], start=True, stop=True, skip_group_check=True)
                last.then_inc(scored, 1)

        @block.scalar
        def _(act):
            for t, r in enumerate(ROWS):
                act.wait_ge(less, t + 1)
                nc.scalar.activation(e[0:r], e[0:r], ACT.Exp).then_inc(expd, 1)

        @block.vector
        def _(dve):
            v = nc.vector
            for t, r in enumerate(ROWS):
                dve.wait_ge(scored, t + 1)
                src = k.ps[0:r, 4 * (t % 2):4 * (t % 2) + 4, :].rearrange("p a b -> p (a b)")
                step(v.tensor_copy(s[0:r].rearrange("p a b -> p (a b)"), src))

                def sixteen_best(x, y, best, where, n):
                    for i in range(n):
                        last = v.max(best[0:r, i, 0:8], x[0:r, i, :])
                    step(last)
                    for i in range(n):
                        v.max_index(where[0:r, i, 0:8], best[0:r, i, 0:8], x[0:r, i, :])
                        last = v.match_replace(y[0:r, i, :], best[0:r, i, 0:8], x[0:r, i, :], -3e38)
                    step(last)
                    for i in range(n):
                        last = v.max(best[0:r, i, 8:16], y[0:r, i, :])
                    step(last)
                    for i in range(n):
                        last = v.max_index(where[0:r, i, 8:16], best[0:r, i, 8:16], y[0:r, i, :])
                    step(last)

                sixteen_best(s, s2, val, at, HC)
                v.tensor_copy(atf[0:r], at[0:r]).then_inc(read, 1)
                pair = lambda x: x[0:r].rearrange("p (h c) k -> p h c k", c=2)
                for hd in range(PH):
                    last = v.tensor_tensor(cand[0:r, hd].rearrange("p (i j) -> p i j", j=PK), bc(val[0:r, 2 * hd, :], 2, PK),
                                           bc(val[0:r, 2 * hd + 1, :], 1, PK), ALU.add)
                step(last)
                sixteen_best(cand, cand2, top, sel, PH)
                v.tensor_scalar(half[0:r, 0], sel[0:r], 4, None, ALU.logical_shift_right)
                step(v.tensor_scalar(half[0:r, 1], sel[0:r], 15, None, ALU.bitwise_and))
                step(v.tensor_copy(halff[0:r], half[0:r]))
                for c in range(2):
                    for hd in range(PH):
                        eq = cand[0:r, hd].rearrange("p (k j) -> p k j", j=PK)
                        last = v.tensor_tensor(eq, bc(halff[0:r, c, hd, :], 2, PK), bc(k.c("iota16")[0:r, :], 1, PK), ALU.is_equal)
                    step(last)
                    for hd in range(PH):
                        eq = cand[0:r, hd].rearrange("p (k j) -> p k j", j=PK)
                        last = v.tensor_tensor(eq, eq, bc(atf[0:r, 2 * hd + c, :], 1, PK), ALU.mult)
                    step(last)
                    step(v.tensor_reduce(ef[0:r, c].rearrange("p h k -> p (h k)"), cand[0:r].rearrange("p h (k j) -> p (h k) j", j=PK),
                                         AX, ALU.add))
                step(v.scalar_tensor_tensor(ef[0:r, 0], ef[0:r, 0], float(NK), ef[0:r, 1], ALU.mult, ALU.add))
                step(v.tensor_scalar(ef[0:r, 0], ef[0:r, 0], float(layer * EXPERTS), None, ALU.add))
                v.tensor_tensor(e[0:r], top[0:r], top[0:r, :, 0:1].broadcast_to([r, PH, PK]), ALU.subtract).then_inc(less, 1)
                dve.wait_ge(expd, t + 1)
                step(v.tensor_reduce(den[0:r], e[0:r], AX, ALU.add))
                step(v.reciprocal(den[0:r], den[0:r]))
                step(v.tensor_tensor(e[0:r], e[0:r], bc(den[0:r], 2, PK), ALU.mult))
                if t < 2:
                    v.tensor_copy(slots[:, t, :], ef[:, 0].rearrange("p h k -> p (h k)"))
                    step(v.tensor_copy(gate[:, t, :], e[:].rearrange("p h k -> p (h k)")))
                else:
                    for q in range(4):
                        some = slice(NS * q, NS * (q + 1))
                        v.tensor_copy(slots[some, t, 0:NS], ef[0:r, 0].rearrange("p h k -> p (h k)")[:, some])
                        last = v.tensor_copy(gate[some, t, 0:NS], e[0:r].rearrange("p h k -> p (h k)")[:, some])
                    step(last)


def experts_and_norm(k, name, table, slots, gate, gain, bias, outs):
    nc, step = k.nc, k.dve_steps
    with ExitStack() as ctx:
        uv = k.sbuf(name + "_uv", [128, RING, 2 * D], ctx=ctx)
        xs = k.sbuf(name + "_xs", [128, D], ctx=ctx)
        rows = k.sbuf(name + "_rows", [128, RING], U32, ctx)
        dot = k.sbuf(name + "_dot", [128, 2, GROUP], ctx=ctx)
        act_ = k.sbuf(name + "_gelu", [128, 2, GROUP], ctx=ctx)
        wgt = k.sbuf(name + "_wgt", [128, 2, GROUP], ctx=ctx)
        diag = k.sbuf(name + "_diag", [128, RING, 128], ctx=ctx)
        g, b = k.sbuf(name + "_g", [128, D], ctx=ctx), k.sbuf(name + "_b", [128, D], ctx=ctx)
        z = k.sbuf(name + "_z", [128, D], ctx=ctx)
        stats = k.sbuf(name + "_stats", [128, 16], ctx=ctx)
        landed = [k.sem(f"{name}_row_landed{i}") for i in range(RING)]
        picked, dotted, gelued, weighed = [k.sem(f"{name}_{n}") for n in ("picked", "dotted", "gelued", "weighed")]
        spread, used, issued = [k.sem(f"{name}_{n}") for n in ("spread", "used", "issued")]
        root, rooted, rowl, ready, stored, released = [k.sem(f"{name}_{n}") for n in ("variance", "rooted", "rows_in", "y_ready", "stored", "sum_read")]
        steps_of = (SLOTS, SLOTS, SLOTS // 4)
        before = [0, SLOTS, 2 * SLOTS]
        GR_ = RING // GROUP
        block = ctx.enter_context(nc.Block())

        @block.gpsimd
        def _(pool):
            def eight(t, it, first):
                done = before[t] + it * RING
                for r in range(RING):
                    if not first:
                        pool.wait_ge(used, done + (r + 1 - RING))
                    at = slots[:, t, bass.ds(it * RING + r, 1)]
                    nc.gpsimd.tensor_copy(rows[:, r:r + 1], at).then_inc(picked, 1)
                    pool.wait_ge(picked, done + (r + 1))
                    pool.sem_inc(issued, 1)
                    nc.gpsimd.indirect_dma_start(out=uv[:, r, :], out_offset=None, in_=table,
                                                 in_offset=bass.IndirectOffsetOnAxis(ap=rows[:, r:r + 1], axis=0)).then_inc(landed[r], 16)

            for t in range(TILES):
                n = steps_of[t] // RING
                eight(t, 0, t == 0)
                with pool.Fori(1, n) as it:
                    eight(t, it, False)

        @block.vector
        def _(dve):
            dve.wait_ge(rowl, 32)
            for q in range(4):
                last = nc.vector.tensor_copy(xs[NS * q:NS * (q + 1), :], k.x[0:NS, 2, :])
            step(last)

            def eight(t, it, first):
                x = k.x[:, t, :] if t < 2 else xs[:, :]
                done = before[t] // RING + it
                for grp in range(GR_):
                    for r in range(GROUP * grp, GROUP * (grp + 1)):
                        dve.wait_ge(landed[r], (done + 1) * 16)
                        last = nc.vector.tensor_tensor_reduce(uv[:, r, 0:D], uv[:, r, 0:D], x, 1.0, 0.0, ALU.mult, ALU.add,
                                                              dot[:, grp, r % GROUP:r % GROUP + 1])
                    last.then_inc(dotted, 1)
                    dve.wait_ge(gelued, done * GR_ + (grp + 1))
                    if not first:
                        dve.wait_ge(spread, done * GR_ + (grp - 1))
                    nc.vector.tensor_tensor(wgt[:, grp, :], act_[:, grp, :], gate[:, t, bass.ds(it * RING + GROUP * grp, GROUP)],
                                            ALU.mult).then_inc(weighed, 1)

            for t, r in enumerate(ROWS):
                n = steps_of[t] // RING
                eight(t, 0, t == 0)
                with dve.Fori(1, n) as it:
                    eight(t, it, False)
                dve.wait_ge(used, before[t] + steps_of[t])
                out = k.ps[0:r, 2 * t:2 * t + 2, :].rearrange("p a b -> p (a b)")
                step(nc.vector.scalar_tensor_tensor(z[0:r, :], k.x[0:r, t, :], ALPHA, out, ALU.mult, ALU.add))
                norm_steps(k, z[0:r, :], stats[0:r, :], root, rooted, t + 1, k.x[0:r, t, :], g[0:r, :], b[0:r, :])
                nc.vector.memset(k.pad[:, :], 0.0).then_inc(ready, 1)

        @block.scalar
        def _(act):
            def eight(t, it, first):
                done = before[t] // RING + it
                for grp in range(GR_):
                    act.wait_ge(dotted, done * GR_ + (grp + 1))
                    nc.scalar.activation(act_[:, grp, :], dot[:, grp, :], ACT.Gelu).then_inc(gelued, 1)
                    act.wait_ge(weighed, done * GR_ + (grp + 1))
                    for r in range(GROUP * grp, GROUP * (grp + 1)):
                        if not first:
                            act.wait_ge(used, done * RING + (r + 1 - RING))
                        last = nc.scalar.activation(diag[:, r, :], k.c("ident"), ACT.Copy, scale=wgt[:, grp, r % GROUP:r % GROUP + 1])
                    last.then_inc(spread, 1)

            def sample_eight(it):
                done = before[2] // RING + it
                for grp in range(GR_):
                    act.wait_ge(dotted, done * GR_ + (grp + 1))
                    nc.scalar.activation(act_[:, grp, :], dot[:, grp, :], ACT.Gelu).then_inc(gelued, 1)
                    act.wait_ge(weighed, done * GR_ + (grp + 1))
                    for r in range(GROUP * grp, GROUP * (grp + 1)):
                        act.wait_ge(used, done * RING + (r + 1 - RING))
                        last = nc.scalar.activation(diag[:, r, 0:NS], k.c("fold"), ACT.Copy, scale=wgt[:, grp, r % GROUP:r % GROUP + 1])
                    last.then_inc(spread, 1)

            for t, r in enumerate(ROWS):
                n = steps_of[t] // RING
                if t < 2:
                    eight(t, 0, t == 0)
                    with act.Fori(1, n) as it:
                        eight(t, it, False)
                else:
                    with act.Fori(0, n) as it:
                        sample_eight(it)
                act.wait_ge(root, t + 1)
                nc.scalar.activation(stats[0:r, 15:16], stats[0:r, 14:15], ACT.Sqrt).then_inc(rooted, 1)

        @block.tensor
        def _(pe):
            def eight(t, it, start, stop):
                done = before[t] // RING + it
                m = ROWS[t]
                for r in range(RING):
                    if r % GROUP == 0:
                        pe.wait_ge(spread, done * GR_ + (r // GROUP + 1))
                    for c in range(2):
                        last = nc.tensor.matmul(k.bank(2 * t + c)[0:m, :], diag[:, r, 0:m], uv[:, r, D + 512 * c:D + 512 * (c + 1)],
                                                start=(start and r == 0), stop=(stop and r == RING - 1), skip_group_check=True)
                    last.then_inc(used, 1)

            for t in range(TILES):
                n = steps_of[t] // RING
                eight(t, 0, True, False)
                with pe.Fori(1, n - 1) as it:
                    eight(t, it, False, False)
                eight(t, n - 1, False, True)

        @block.sync
        def _(sp):
            sp.dma_start(g[:, :], gain.partition_broadcast(128)).then_inc(rowl, 16)
            sp.dma_start(b[:, :], bias.partition_broadcast(128)).then_inc(rowl, 16)
            if outs is not None:
                y_prompt, y_sample = outs
                for t in range(TILES):
                    sp.wait_ge(ready, t + 1)
                    dst = y_prompt[0, 128 * t:128 * (t + 1), :] if t < 2 else y_sample.rearrange("b t d -> (b t) d")
                    sp.dma_start(dst, k.x[0:ROWS[t], t, :]).then_inc(stored, 16)
                sp.wait_ge(stored, 16 * TILES)


def peer(k, name, layer, w_q, sub_keys, table, gain, bias, outs):
    transpose_x(k, name + "_x")
    with ExitStack() as ctx:
        slots = k.sbuf(name + "_slots", [128, TILES, SLOTS], U32, ctx)
        gate = k.sbuf(name + "_gate", [128, TILES, SLOTS], ctx=ctx)
        route(k, name, layer, w_q, sub_keys, slots, gate)
        experts_and_norm(k, name + "_ex", table, slots, gate, gain[layer], bias[layer], outs)


def build(nc, a, o):
    with ExitStack() as whole:
        k = Core(nc, whole)
        k.pad = k.sbuf("progress", [128, 1])
        k.level_masks = a["level_masks"]
        load_inputs(k, a["x_prompt"], a["x_sample"], a["const"])
        transpose_x(k, "x0")
        with ExitStack() as ctx:
            catT = k.sbuf("catT", [128, KC, NTOK], ctx=ctx)
            with ExitStack() as inner:
                h = k.sbuf("h", [128, TILES, EVEN_ROWS], ctx=inner)
                w_in = a["even_w_in"][0]
                project_rows(k, "even", w_in[:, 1024:], [512, 512, 512, 512, 280], h)
                with ExitStack() as hg:
                    cat = k.sbuf("cat", [128, TILES, 512], ctx=hg)
                    hT = k.sbuf("hT", [128, 8, NTOK], ctx=hg)
                    project_cols(k, "even_T", w_in, 1024, hT)
                    recurrence(k, h, hT, cat, a["hg_gamma"], a["hg_norm_g"][0], a["state_hgrn"], o["state_prompt"], o["state_sample"])
                    transposes(k, "cat", [([cat[0:r, t, 128 * c:128 * (c + 1)] for c in range(4)], catT[:, 0:4, cols(t)])
                                          for t, r in enumerate(ROWS)])
                sparse_attention(k, h, catT, a["page_table"], a["cache_cmp_kv"], a["cache_slc_kv"], a["cache_win_kv"], a["nsa_cmp_pe"],
                                 [o[n] for n in ("cmp_p", "cmp_s", "slc_p", "slc_s", "win_p", "win_s")])
            w_out = a["even_w_out"][0]
            project_out_and_norm(k, "even_out", catT, lambda w: [
                (w[:, 0:4, :], w_out[0:512].rearrange("(c p) n -> p c n", p=128)),
                (w[0:64, 4:8, :], w_out[512:768].rearrange("(g d) n -> d g n", d=HD)),
                (w[64:128, 4:8, :], w_out[768:1024].rearrange("(g d) n -> d g n", d=HD))], a["ln_mix_g"][0], a["ln_mix_b"][0])
        peer(k, "peer0", 0, a["peer_w_q"], a["peer_sub_keys"], a["experts"], a["ln_ffn_g"], a["ln_ffn_b"], None)
        k.fresh_semaphores()
        transpose_x(k, "x1")
        with ExitStack() as ctx:
            catT = k.sbuf("catT1", [128, KC, NTOK], ctx=ctx)
            with ExitStack() as inner:
                h = k.sbuf("h1", [128, TILES, 3 * D], ctx=inner)
                project_rows(k, "odd", a["odd_w_in"][0], [512] * 6, h)
                dilated_attention(k, h, catT, a["cache_dil_kv"], o["dil_p"], o["dil_s"])
            project_out_and_norm(k, "odd_out", catT, lambda w: [(w[:, :, :], a["odd_w_out"][0].rearrange("(c p) n -> p c n", p=128))],
                                 a["ln_mix_g"][1], a["ln_mix_b"][1])
        peer(k, "peer1", 1, a["peer_w_q"], a["peer_sub_keys"], a["experts"], a["ln_ffn_g"], a["ln_ffn_b"], (o["y_prompt"], o["y_sample"]))


_OUTS = [("y_prompt", (1, SEQ, D)), ("y_sample", (DEC_B, DEC_T, D)), ("state_prompt", (1, 1, HG, 64, 64)),
         ("state_sample", (1, DEC_B, HG, 64, 64))]
for _n in ("cmp", "slc", "win"):
    _OUTS += [(_n + "_p", (1, 1, SEQ, 2, KV, HD)), (_n + "_s", (1, DEC_B, DEC_T, 2, KV, HD))]
_OUTS += [("dil_p", (1, 1, SEQ, 2, HEADS, HD)), ("dil_s", (1, DEC_B, DEC_T, 2, HEADS, HD))]


def kernel(**inputs):
    import numpy as _np
    import concourse.bacc as _bacc
    from concourse import mybir as _mybir
    from concourse.bass_utils import run_bass_kernel_spmd as _run

    nc = _bacc.Bacc("TRN2", target_bir_lowering=False, num_devices=1)
    given = {n: _np.ascontiguousarray(x) for n, x in inputs.items() if n not in ("peer_u", "peer_v")}
    u, v = _np.asarray(inputs["peer_u"]), _np.asarray(inputs["peer_v"])
    given["experts"] = _np.concatenate([u, v], axis=2).reshape(DEPTH * EXPERTS, 2 * D)
    given["const"], given["level_masks"] = CONST, LEVEL_MASKS
    arrays = {f"in_{n}_dram": x for n, x in given.items()}
    a = {n: nc.dram_tensor(f"in_{n}_dram", x.shape, _mybir.dt.from_np(x.dtype), kind="ExternalInput").ap() for n, x in given.items()}
    o = {n: nc.dram_tensor(f"out_{n}_dram", shape, F32, kind="ExternalOutput").ap() for n, shape in _OUTS}
    build(nc, a, o)
    r = _run(nc, [arrays], core_ids=[0])
    return tuple(r.results[0][f"out_{n}_dram"] for n, _ in _OUTS)
```

```python
from contextlib import ExitStack

import numpy as np

import concourse.bass as bass
from concourse import mybir

F32 = mybir.dt.float32
U32 = mybir.dt.uint32
I32 = mybir.dt.int32
ALU = mybir.AluOpType
ACT = mybir.ActivationFunctionType
AX = mybir.AxisListType.X

D = 1024
KC = D // 128
SEQ = 256
DEC_B, DEC_T = 8, 4
NS = DEC_B * DEC_T
PAST = 256
PAGE = 128
NPG = PAST // PAGE
NTOK = SEQ + NS
ROWS = (128, 128, NS)
TILES = len(ROWS)
DEPTH = 2
ALPHA = float((2 * DEPTH) ** 0.25)
LN_EPS, RMS_EPS, TINY = 1e-5, 1e-6, 1e-30
HD = 64
SCALE = HD ** -0.5
HG = 8
KV, GR = 2, 4
NBLK = PAST // 32
MASKED = -1e30
LEAST = -1e28
HEADS = 16
HP = HEADS // 2
DIL = ((128, 1), (512, 4), (2048, 16))
PH, PK, NK = 8, 16, 128
EXPERTS = NK * NK
SLOTS = PH * PK
RING = 7
GROUP = 2
LAG = 3
LEVELS = (1, 2, 4, 8, 16, 32, 64)

V0, G0, Q0, CMP0, SLC0, WIN0, GATE0, EVEN_ROWS = 0, 512, 1024, 1536, 1792, 2048, 2304, 2328


def shape_constants():
    half = HD // 2
    inv = np.float32(10000.0) ** (-np.arange(half, dtype=np.float32) / np.float32(half))
    cos = np.zeros((128, TILES, half), np.float32)
    sin = np.zeros((128, TILES, half), np.float32)
    for t in range(TILES):
        pos = np.arange(128) + 128 * t if t < 2 else PAST + np.arange(128) % DEC_T
        ang = pos.astype(np.float32)[:, None] * inv[None, :].astype(np.float32)
        cos[:, t], sin[:, t] = np.cos(ang.astype(np.float64)), np.sin(ang.astype(np.float64))

    def reach(qpos, kpos):
        dist = qpos[:, None] - kpos[None, :]
        count = np.zeros(dist.shape, np.float32)
        for window, dil in DIL:
            count += (dist >= 0) & (dist <= window // dil * dil) & (dist % dil == 0)
        return (dist >= 0), count

    p = np.arange(128)
    causal = np.zeros((128, 2, SEQ), np.float32)
    dil_mask = np.zeros((128, 2, SEQ), np.float32)
    dil_count = np.zeros((128, 2, SEQ), np.float32)
    cmp_mask = np.zeros((128, 2, NBLK), np.float32)
    for t in range(2):
        seen, count = reach(p + 128 * t, np.arange(SEQ))
        causal[:, t] = np.where(seen, 0, MASKED)
        dil_mask[:, t] = np.where(count > 0, 0, MASKED)
        dil_count[:, t] = count
        cmp_mask[:, t] = np.where((np.arange(NBLK) + 1)[None] * 32 - 1 <= (p + 128 * t)[:, None], 0, MASKED)
    tok = p % NS
    seen, count = reach(PAST + tok % DEC_T, np.concatenate([np.arange(PAST), PAST + np.arange(NS) % DEC_T]))
    own = np.concatenate([np.ones((128, PAST), bool), tok[:, None] // DEC_T == np.arange(NS)[None] // DEC_T], 1)
    new_causal = np.where(seen & own, 0, MASKED).astype(np.float32)
    new_mask = np.where((count > 0) & own, 0, MASKED).astype(np.float32)
    new_count = np.where(own, count, 0).astype(np.float32)
    batch_cols = np.broadcast_to((np.arange(NS)[None] // DEC_T == np.arange(DEC_B)[:, None]), (128, DEC_B, NS))
    batch_rows = tok[:, None] // DEC_T == np.arange(DEC_B)[None]
    pool = np.zeros((128, NPG, NBLK), np.float32)
    for t in range(NPG):
        pool[p, t, 4 * t + p // 32] = 1 / 32
    fold = tok[:, None] == np.arange(NS)[None]
    parts = dict(
        ident=np.eye(128), cos=cos, sin=sin, causal=causal, dil_mask=dil_mask, dil_count=dil_count,
        cmp_mask=cmp_mask, new_causal=new_causal, new_mask=new_mask, new_count=new_count,
        batch_cols=batch_cols, batch_rows=batch_rows, pool=pool, mean32=np.full((128, NBLK), 1 / 32), fold=fold,
        iota16=np.broadcast_to(np.arange(PK), (128, PK)), row=p[:, None],
    )
    at, cols = {}, []
    for name, a in parts.items():
        a = np.asarray(a, np.float32)
        n = sum(c.shape[1] for c in cols)
        at[name] = (n, a.shape[1:])
        cols.append(a.reshape(128, -1))
    s, t = p[:, None], p[None, :]
    levels = [s == t] + [(s // (2 * m) == t // (2 * m)) & (s // m % 2 == 0) & (t // m % 2 == 1) for m in LEVELS]
    return np.concatenate(cols, 1), at, np.stack(levels, 1).astype(np.uint32)


CONST, CONST_AT, LEVEL_MASKS = shape_constants()


class Steps:

    def __init__(self, k, eng, name):
        self.sem, self.eng, self.n = k.sem(name), eng, 0

    def __call__(self, ins):
        self.n += 1
        ins.then_inc(self.sem, 1)
        self.eng.wait_ge(self.sem, self.n)


class Core:

    def __init__(self, nc, ctx):
        self.nc, self.ctx, self.serial, self.stage_sems = nc, ctx, 0, []
        self.stored, self.n_stored = nc.alloc_semaphore("stored"), 0
        self.side, self.side_set, self.side_sems, self.side_taken = False, 0, {}, []
        self.dve_steps = Steps(self, nc.vector, "dve_steps")
        self.x = self.sbuf("x", [128, TILES, D])
        self.xT = self.sbuf("xT", [128, KC, NTOK])
        self.const = self.sbuf("const", list(CONST.shape))
        self.ps = ctx.enter_context(nc.psum_tensor("ps", [128, 8, 512], F32))

    def sem(self, name, role=None):
        if self.side and role:
            key = (role, self.side_set)
            if key not in self.side_sems:
                self.side_sems[key] = self.nc.alloc_semaphore(f"side{self.side_set}_{role}")
                self.stage_sems.append(self.side_sems[key])
            self.side_taken.append(self.side_sems[key])
            return self.side_sems[key]
        name = f"{name}_{role}" if role else name
        self.serial += 1
        self.stage_sems.append(self.nc.alloc_semaphore(f"{name}_{self.serial}"))
        return self.stage_sems[-1]

    def store(self, sp, dst, src):
        self.n_stored += 1
        sp.dma_start(dst, src).then_inc(self.stored, 16)

    def wait_for_stores(self, sp):
        sp.wait_ge(self.stored, 16 * self.n_stored)

    def take_side_sems(self):
        taken, self.side_taken = self.side_taken, []
        if self.side:
            self.side_set = 1 - self.side_set
        return taken

    def fresh_semaphores(self):
        self.nc.clear_and_free_semaphores(self.stage_sems)
        self.stage_sems = []
        self.nc.all_engine_barrier()
        self.dve_steps.n = 0
        self.dve_steps.sem = self.sem("dve_steps")

    def sbuf(self, name, shape, dt=F32, ctx=None):
        self.serial += 1
        return (ctx or self.ctx).enter_context(self.nc.sbuf_tensor(f"{name}_{self.serial}", shape, dt))

    def c(self, name):
        n, shape = CONST_AT[name]
        size = int(np.prod(shape))
        flat = self.const[:, n:n + size]
        if len(shape) == 2:
            return flat.rearrange("p (a b) -> p a b", b=shape[1])
        return flat

    def bank(self, b):
        return self.ps[:, b, :]


def bc(ap, axis, n):
    ap = ap.unsqueeze(axis)
    shape = list(ap.shape)
    shape[axis] = n
    return ap.broadcast_to(shape)


COL0 = (NS, NS + 128, 0)
SMP = slice(0, NS)


def cols(t):
    return slice(COL0[t], COL0[t] + ROWS[t])




def load_inputs(k, x_prompt, x_sample, const):
    nc = k.nc
    loaded = k.sem("loaded")
    with nc.Block() as block:
        @block.sync
        def _(sp):
            sp.dma_start(k.const[:, :], const).then_inc(loaded, 16)
            sp.dma_start(k.x[:, 0:2, :], x_prompt.rearrange("o (t p) d -> p (o t) d", p=128)).then_inc(loaded, 16)
            sp.dma_start(k.x[0:NS, 2, :], x_sample.rearrange("b t d -> (b t) d")).then_inc(loaded, 16)
            sp.wait_ge(loaded, 48)


class Stage:

    def __init__(self, k, ticks):
        self.ticks, self.parts, self.sems = ticks, {}, k.take_side_sems()

    def on(self, engine):
        def keep(part):
            self.parts[engine] = part
        return keep

    def run(self, name, eng):
        count = 0
        if name in self.parts:
            for _ in self.parts[name](eng):
                count += 1
                yield
            assert count == self.ticks, (count, self.ticks)
        else:
            for _ in range(self.ticks):
                yield


def alone(k, stage):
    with k.nc.Block() as block:
        @block.tensor
        def _(pe):
            for _ in stage.run("tensor", pe):
                pass

        @block.vector
        def _(dve):
            for _ in stage.run("vector", dve):
                pass

        @block.scalar
        def _(act):
            for _ in stage.run("scalar", act):
                pass

        @block.sync
        def _(sp):
            if "sync" in stage.parts:
                stage.parts["sync"](sp)


ALL_BANKS = tuple(range(8))
SIDE_BANKS = tuple(range(2, 8))


def transposes(k, name, groups, banks=ALL_BANKS, loads=()):
    nc, nb = k.nc, len(banks)
    turned, v_out, s_out, loaded = [k.sem(name, n) for n in ("turned", "v_out", "s_out", "loaded")]
    ident = k.c("ident")
    stage = Stage(k, len(groups) + 1)
    sizes = [(srcs[0].shape[0], int(np.prod(srcs[0].shape[1:]))) for srcs, _ in groups]
    outs = ((v_out, nc.vector.tensor_copy), (s_out, nc.scalar.copy))

    def out_view(i):
        (rows, width), (srcs, dst) = sizes[i], groups[i]
        flat = k.bank(banks[i % nb])[0:width, 0:rows * len(srcs)]
        if len(dst.shape) == 3:
            return flat.rearrange("p (a b) -> p a b", b=dst.shape[2])
        return flat

    @stage.on("sync")
    def _(sp):
        for dst, src in loads:
            sp.dma_start(dst, src).then_inc(loaded, 16)

    @stage.on("tensor")
    def _(pe):
        if loads:
            pe.wait_ge(loaded, 16 * len(loads))
        for i, (srcs, dst) in enumerate(groups):
            rows, width = sizes[i]
            j = i - nb
            if j >= 0:
                pe.wait_ge((v_out, s_out)[j % 2], j // 2 + 1)
            for n, src in enumerate(srcs):
                last = nc.tensor.transpose(k.bank(banks[i % nb])[0:width, n * rows:(n + 1) * rows], src, ident[0:rows, 0:rows])
            last.then_inc(turned, 1)
            yield
        yield

    def take_out(eng, side):
        done, copy = outs[side]
        yield
        for i in range(len(groups)):
            if i % 2 == side:
                eng.wait_ge(turned, i + 1)
                copy(groups[i][1], out_view(i)).then_inc(done, 1)
            yield

    stage.on("vector")(lambda dve: take_out(dve, 0))
    stage.on("scalar")(lambda act: take_out(act, 1))
    return stage


def transpose_x(k, name, tiles=(0, 1, 2), banks=ALL_BANKS):
    groups = []
    for t in tiles:
        for c in range(0, KC, 4):
            groups.append(([k.x[0:ROWS[t], t, (c + j) * 128:(c + j + 1) * 128] for j in range(4)],
                           k.xT[:, c:c + 4, cols(t)]))
    return transposes(k, name, groups, banks)


def project_rows(k, name, w, widths, out, wbuf, tiles=(0, 1, 2), banks=ALL_BANKS):
    nc, nb, slots = k.nc, len(banks), wbuf.shape[1]
    starts = [sum(widths[:i]) for i in range(len(widths))]
    w_v = w.rearrange("(c p) n -> p c n", p=128)
    landed = [k.sem(name, f"w_landed{i}") for i in range(slots)]
    half_done, product, v_out, s_out = [k.sem(name, n) for n in ("half_done", "product", "v_out", "s_out")]
    n_t = len(tiles)
    loads = [(j, half) for j in range(len(widths)) for half in range(2)]
    jobs = [(j, t) for j in range(len(widths)) for t in tiles]
    ticks = []
    for j in range(len(widths)):
        for half in range(2):
            for t in tiles:
                ticks += [[("multiply", j, half, t, sub)] for sub in range(2)]
        for t in tiles:
            ticks[-1].append(("leave", jobs.index((j, t))))
    stage = Stage(k, len(ticks))

    @stage.on("sync")
    def _(sp):
        for i, (j, half) in enumerate(loads):
            if i >= slots:
                sp.wait_ge(half_done, n_t * (i - slots + 1))
            sp.dma_start(wbuf[:, i % slots, :, 0:widths[j]], w_v[:, 4 * half:4 * half + 4, starts[j]:starts[j] + widths[j]])\
              .then_inc(landed[i % slots], 16)

    @stage.on("tensor")
    def _(pe):
        for tick in ticks:
            for what, *rest in tick:
                if what == "multiply":
                    j, half, t, sub = rest
                    i, load = jobs.index((j, t)), 2 * j + half
                    if sub == 0:
                        pe.wait_ge(landed[load % slots], 16 * (load // slots + 1))
                        if half == 0 and i >= nb:
                            pe.wait_ge((v_out, s_out)[(i - nb) % 2], (i - nb) // 2 + 1)
                    for c in (2 * sub, 2 * sub + 1):
                        last = nc.tensor.matmul(k.bank(banks[i % nb])[0:ROWS[t], 0:widths[j]], k.xT[:, 4 * half + c, cols(t)],
                                                wbuf[:, load % slots, c, 0:widths[j]],
                                                start=(half == 0 and c == 0), stop=(half == 1 and c == 3))
                    if sub == 1:
                        last.then_inc(half_done, 1)
            yield

    def take_out(eng, side, done, copy):
        for tick in ticks:
            for what, *rest in tick:
                if what == "leave" and rest[0] % 2 == side:
                    i = rest[0]
                    j, t = jobs[i]
                    eng.wait_ge(half_done, 2 * n_t * j + n_t + i % n_t + 1)
                    copy(out(j, t), k.bank(banks[i % nb])[0:ROWS[t], 0:widths[j]]).then_inc(done, 1)
            yield

    stage.on("vector")(lambda dve: take_out(dve, 0, v_out, nc.vector.tensor_copy))
    stage.on("scalar")(lambda act: take_out(act, 1, s_out, nc.scalar.copy))
    return stage


def project_cols(k, name, w, n, outT, wbuf, tok=slice(0, NTOK), banks=ALL_BANKS):
    nc, nb, slots = k.nc, len(banks), wbuf.shape[1]
    w_v = w.rearrange("(c p) n -> p c n", p=128)
    n_tok = tok.stop - tok.start
    landed = [k.sem(name, f"w_landed{i}") for i in range(slots)]
    product, v_out, s_out = [k.sem(name, n) for n in ("product", "v_out", "s_out")]
    n_cols = n // 128
    stage = Stage(k, 2 * n_cols + 1)

    @stage.on("sync")
    def _(sp):
        for j in range(n // 256):
            if j >= slots:
                sp.wait_ge(product, 2 * (j - slots + 1))
            sp.dma_start(wbuf[:, j % slots, :, :], w_v[:, :, 256 * j:256 * (j + 1)]).then_inc(landed[j % slots], 16)

    @stage.on("tensor")
    def _(pe):
        for i in range(n_cols):
            j = i // 2
            if i % 2 == 0:
                pe.wait_ge(landed[j % slots], 16 * (j // slots + 1))
            if i >= nb:
                pe.wait_ge((v_out, s_out)[(i - nb) % 2], (i - nb) // 2 + 1)
            for c in range(KC):
                last = nc.tensor.matmul(k.bank(banks[i % nb])[:, 0:n_tok], wbuf[:, j % slots, c, 128 * (i % 2):128 * (i % 2 + 1)],
                                        k.xT[:, c, tok], start=(c == 0), stop=(c == KC - 1))
                if c == KC // 2 - 1:
                    yield
            last.then_inc(product, 1)
            yield
        yield

    def take_out(eng, side, done, copy):
        for _ in range(2):
            yield
        for i in range(n_cols):
            if i % 2 == side:
                eng.wait_ge(product, i + 1)
                copy(outT[:, i, tok], k.bank(banks[i % nb])[:, 0:n_tok]).then_inc(done, 1)
            yield
            if i < n_cols - 1:
                yield

    stage.on("vector")(lambda dve: take_out(dve, 0, v_out, nc.vector.tensor_copy))
    stage.on("scalar")(lambda act: take_out(act, 1, s_out, nc.scalar.copy))
    return stage


def norm_first(k, z, stats, variance):
    nc, step = k.nc, k.dve_steps
    for h in range(2):
        step(nc.vector.bn_stats(stats[:, 6 * h:6 * h + 6], z[:, 512 * h:512 * (h + 1)]))
    step(nc.vector.bn_aggr(stats[:, 12:14], stats[:, 0:12]))
    nc.vector.tensor_scalar(stats[:, 14:15], stats[:, 13:14], LN_EPS, None, ALU.add).then_inc(variance, 1)


def norm_second(k, z, stats):
    nc, step = k.nc, k.dve_steps
    step(nc.vector.reciprocal(stats[:, 15:16], stats[:, 15:16]))
    step(nc.vector.tensor_scalar(z, z, stats[:, 12:13], stats[:, 15:16], ALU.subtract, ALU.mult))


def norm_third(k, z, out, gain, bias):
    nc, step = k.nc, k.dve_steps
    step(nc.vector.tensor_tensor(z, z, gain, ALU.mult))
    step(nc.vector.tensor_tensor(out, z, bias, ALU.add))


def project_out_and_norm(k, name, catT, w_piece, gain, bias, w, gb, z, stats, tiles=(0, 1, 2), banks=ALL_BANKS):
    nc, slots = k.nc, w.shape[1]
    landed = [k.sem(name, f"w_landed{i}") for i in range(slots)]
    row_landed, used, variance, rooted = [k.sem(name, n) for n in ("rows_landed", "w_used", "variance", "rooted")]
    n_t, pieces = len(tiles), KC // 2
    per = [len(w_piece(i, w[:, 0])) for i in range(pieces)]
    stage = Stage(k, pieces * n_t * 2 + 3 * n_t)

    def bank(n, h):
        return k.bank(banks[2 * n + h])

    @stage.on("sync")
    def _(sp):
        sp.dma_start(gb[:, 0, :], gain.partition_broadcast(128)).then_inc(row_landed, 16)
        sp.dma_start(gb[:, 1, :], bias.partition_broadcast(128)).then_inc(row_landed, 16)
        for i in range(pieces):
            if i >= slots:
                sp.wait_ge(used, i - slots + 1)
            for dst, src in w_piece(i, w[:, i % slots]):
                sp.dma_start(dst, src).then_inc(landed[i % slots], 16)

    @stage.on("tensor")
    def _(pe):
        for i in range(pieces):
            pe.wait_ge(landed[i % slots], 16 * sum(per[j] for j in range(i % slots, i + 1, slots)))
            for n, t in enumerate(tiles):
                for h in range(2):
                    for c in range(2):
                        last = nc.tensor.matmul(bank(n, h)[0:ROWS[t], :], catT[:, 2 * i + c, cols(t)],
                                                w[:, i % slots, c, 512 * h:512 * (h + 1)],
                                                start=(i == 0 and c == 0), stop=(i == pieces - 1 and c == 1))
                    if (n, h) == (n_t - 1, 1):
                        last.then_inc(used, 1)
                    yield
        for _ in range(3 * n_t):
            yield

    @stage.on("vector")
    def _(dve):
        for _ in range(pieces * n_t * 2):
            yield
        dve.wait_ge(row_landed, 32)
        dve.wait_ge(used, pieces)
        for n, t in enumerate(tiles):
            r = ROWS[t]
            b = banks[2 * n]
            mixed = k.ps[0:r, b:b + 2, :].rearrange("p a b -> p (a b)")
            k.dve_steps(nc.vector.scalar_tensor_tensor(z[0:r, :], k.x[0:r, t, :], ALPHA, mixed, ALU.mult, ALU.add))
            norm_first(k, z[0:r, :], stats[0:r, :], variance)
            yield
            dve.wait_ge(rooted, n + 1)
            norm_second(k, z[0:r, :], stats[0:r, :])
            yield
            norm_third(k, z[0:r, :], k.x[0:r, t, :], gb[0:r, 0, :], gb[0:r, 1, :])
            yield

    @stage.on("scalar")
    def _(act):
        for _ in range(pieces * n_t * 2):
            yield
        for n, t in enumerate(tiles):
            act.wait_ge(variance, n + 1)
            nc.scalar.activation(stats[0:ROWS[t], 15:16], stats[0:ROWS[t], 14:15], ACT.Sqrt).then_inc(rooted, 1)
            for _ in range(3):
                yield
    return stage


def rotate(k, src, dst, tile_rows, heads, tmp):
    nc, step = k.nc, k.dve_steps
    t, r = tile_rows
    half = HD // 2
    cos, sin = bc(k.c("cos")[0:r, t, :], 1, heads), bc(k.c("sin")[0:r, t, :], 1, heads)
    s = src.rearrange("p (h d) -> p h d", d=HD)
    d = dst.rearrange("p (h d) -> p h d", d=HD)
    a, b, c, e = [tmp[0:r, i, 0:heads * half].rearrange("p (h d) -> p h d", d=half) for i in range(4)]
    nc.vector.tensor_tensor(a, s[:, :, 0:half], cos, ALU.mult)
    nc.vector.tensor_tensor(b, s[:, :, half:HD], sin, ALU.mult)
    nc.vector.tensor_tensor(c, s[:, :, 0:half], sin, ALU.mult)
    step(nc.vector.tensor_tensor(e, s[:, :, half:HD], cos, ALU.mult))
    nc.vector.tensor_tensor(d[:, :, 0:half], a, b, ALU.subtract)
    step(nc.vector.tensor_tensor(d[:, :, half:HD], c, e, ALU.add))




def attention(k, name, items, bufs, pairs=(0, 2), turn_banks=(4, 5)):
    nc, step = k.nc, k.dve_steps
    n_items = len(items)
    prob, probT, small = bufs
    scored, masked, expd, ready, turned, copied, summed, left = [
        k.sem(name, s) for s in ("scored", "masked", "expd", "ready", "turned", "copied", "summed", "left")]
    n_tb = len(turn_banks)
    rounds = [(i, j) for i, it in enumerate(items) for j in range(len(it["parts"]))]
    rounds_of = {i: [r for r, (ii, _) in enumerate(rounds) if ii == i] for i in range(n_items)}
    leaving = [i for i, it in enumerate(items) if it["leave"]]

    ticks = []

    def scores_and_exps(i):
        count = len(items[i]["scores"])
        for at in range(0, count, 3):
            ticks.append([("scores", i, at, min(at + 3, count))])
        ticks.append([("mask", i), ("exp", i)])

    scores_and_exps(0)
    for i in range(n_items):
        if i + 1 < n_items:
            scores_and_exps(i + 1)
        ticks.append([("normalise", i)])
        ticks.append([("turn", rounds_of[i][0]), ("copy", rounds_of[i][0])])
        for r in rounds_of[i]:
            count = len(items[i]["parts"][rounds[r][1]][2])
            for at in range(0, count, 8):
                ticks.append([("values", r, at, min(at + 8, count))])
                if at == 0 and r != rounds_of[i][-1]:
                    ticks[-1] = [("turn", r + 1), ("copy", r + 1)] + ticks[-1]
        ticks.append([("leave", i)])
    stage = Stage(k, len(ticks))

    def view(i):
        it = items[i]
        return prob[0:it["rows"], i % 3, 0:it["groups"] * it["n"]].rearrange("p (g n) -> p g n", n=it["n"])

    def score_bank(i):
        b = pairs[i % 2]
        return k.ps[:, b:b + 2, :].rearrange("p a b -> p (a b)")

    def top(i):
        return small[0:items[i]["rows"], 0, i % 3, 0:items[i]["groups"]]

    def low(i):
        return small[0:items[i]["rows"], 1, i % 3, 0:items[i]["groups"]]

    def den(i):
        return small[0:items[i]["rows"], 2, i % 3, 0:items[i]["groups"]]

    def inv(i):
        return small[0:items[i]["rows"], 3, i % 3, 0:items[i]["groups"]]

    @stage.on("tensor")
    def _(pe):
        def scores(i, a, b):
            if a == 0 and i >= 2:
                pe.wait_ge(masked, i - 1)
            for p0, pn, c0, cn, lhsT, rhs, start, stop in items[i]["scores"][a:b]:
                last = nc.tensor.matmul(score_bank(i)[p0:p0 + pn, c0:c0 + cn], lhsT, rhs, start=start, stop=stop)
            if b == len(items[i]["scores"]):
                last.then_inc(scored, 1)

        def turn(r):
            i, j = rounds[r]
            it = items[i]
            pe.wait_ge(ready, i + 1)
            if r >= n_tb:
                pe.wait_ge(copied, r - n_tb + 1)
            k0, kn, _ = it["parts"][j]
            for g in range(it["groups"]):
                last = nc.tensor.transpose(k.bank(turn_banks[r % n_tb])[0:kn, g * 128:g * 128 + it["rows"]],
                                           view(i)[:, g, k0:k0 + kn], k.c("ident")[0:it["rows"], 0:it["rows"]])
            last.then_inc(turned, 1)

        def values(r, a, b):
            i, j = rounds[r]
            k0, kn, mms = items[i]["parts"][j]
            if a == 0:
                pe.wait_ge(copied, r + 1)
                before = sum(1 for n in leaving if n < i)
                if j == 0 and before:
                    pe.wait_ge(left, before)
            for out, lhsT, pick, start, stop in mms[a:b]:
                last = nc.tensor.matmul(out, lhsT, pick(probT[0:kn, r % 2, :]), start=start, stop=stop, skip_group_check=True)
            if b == len(mms):
                last.then_inc(summed, 1)

        for tick in ticks:
            for what, *rest in tick:
                if what == "scores":
                    scores(*rest)
                elif what == "turn":
                    turn(*rest)
                elif what == "values":
                    values(*rest)
            yield

    @stage.on("vector")
    def _(dve):
        def mask_and_top(i):
            it = items[i]
            g, n, r = it["groups"], it["n"], it["rows"]
            dve.wait_ge(scored, i + 1)
            if i >= 3:
                dve.wait_ge(turned, rounds_of[i - 3][-1] + 1)
            apart = it.get("apart", n)
            sc = score_bank(i)[0:r, 0:g * apart].rearrange("p (g n) -> p g n", n=apart)[:, :, 0:n]
            if it["mask"] is None:
                step(nc.vector.tensor_copy(view(i), sc))
            else:
                step(nc.vector.tensor_tensor(view(i), sc, bc(it["mask"], 1, g), ALU.add))
            step(nc.vector.tensor_reduce(top(i), view(i), AX, ALU.max))
            nc.vector.tensor_scalar(low(i), top(i), LEAST, -SCALE, ALU.max, ALU.mult).then_inc(masked, 1)

        def normalise(i):
            it = items[i]
            g, n = it["groups"], it["n"]
            dve.wait_ge(expd, i + 1)
            if it["count"] is not None:
                step(nc.vector.tensor_tensor(view(i), view(i), bc(it["count"], 1, g), ALU.mult))
                step(nc.vector.tensor_reduce(den(i), view(i), AX, ALU.add))
            step(nc.vector.tensor_scalar(den(i), den(i), TINY, None, ALU.max))
            step(nc.vector.reciprocal(inv(i), den(i)))
            if it["gate"] is not None:
                step(nc.vector.tensor_tensor(inv(i), inv(i), it["gate"], ALU.mult))
            nc.vector.tensor_tensor(view(i), view(i), bc(inv(i), 2, n), ALU.mult).then_inc(ready, 1)

        for tick in ticks:
            for what, *rest in tick:
                if what == "mask":
                    mask_and_top(*rest)
                elif what == "normalise":
                    normalise(*rest)
                elif what == "leave" and rest[0] in leaving:
                    i = rest[0]
                    dve.wait_ge(summed, rounds_of[i][-1] + 1)
                    for dst, src in items[i]["leave"]:
                        last = nc.vector.tensor_copy(dst, src)
                    last.then_inc(left, 1)
            yield

    @stage.on("scalar")
    def _(act):
        def exps(i):
            act.wait_ge(masked, i + 1)
            for g in range(items[i]["groups"]):
                one = view(i)[:, g, :]
                total = {} if items[i]["count"] is not None else dict(accum_out=den(i)[:, g:g + 1])
                last = nc.scalar.activation(one, one, ACT.Exp, bias=low(i)[:, g:g + 1], scale=SCALE, **total)
            last.then_inc(expd, 1)

        def copy(r):
            i, j = rounds[r]
            it = items[i]
            kn, w = it["parts"][j][1], (it["groups"] - 1) * 128 + it["rows"]
            act.wait_ge(turned, r + 1)
            if r >= 2:
                act.wait_ge(summed, r - 1)
            nc.scalar.copy(probT[0:kn, r % 2, 0:w], k.bank(turn_banks[r % n_tb])[0:kn, 0:w]).then_inc(copied, 1)

        for tick in ticks:
            for what, *rest in tick:
                if what == "exp":
                    exps(*rest)
                elif what == "copy":
                    copy(*rest)
            yield
    return stage


def attention_buffers(k, name, width, turned, ctx):
    return (k.sbuf(name + "_prob", [128, 3, width], ctx=ctx), k.sbuf(name + "_probT", [128, 2, turned], ctx=ctx),
            k.sbuf(name + "_small", [128, 4, 3, 4], ctx=ctx))




def recurrence(k, h, hT, cat, gamma, norm_g, state, state_prompt, state_sample):
    nc, step = k.nc, k.dve_steps
    C4 = 4
    pT = hT[:, 0:C4, :]
    fT = hT[:, C4:2 * C4, :]
    s = {n: k.sem("hg_" + n) for n in (
        "loaded", "gamma_turned", "gamma_read", "bounds_diff", "bounds_exp", "bounds_ready", "sigmoid", "factors", "products",
        "taken", "mask_landed", "keys_turned", "keys_out", "spread", "state_product", "out_product", "state_ready",
        "o_copied", "squares", "root", "gates")}
    with ExitStack() as ctx:
        masks = k.sbuf("level_masks", [128, len(LEVELS) + 1, 128], U32, ctx)
        key = k.sbuf("hg_key", [128, C4, NTOK], ctx=ctx)
        tot = [k.sbuf("hg_tot", [128, C4, NTOK], ctx=ctx) for _ in range(2)]
        sg = k.sbuf("hg_sigmoid", [128, 2 * C4, NTOK], ctx=ctx)
        att = k.sbuf("hg_att", [128, 2, HG, 128], ctx=ctx)
        cross = k.sbuf("hg_cross", [128, HG, 128], ctx=ctx)
        att_s = k.sbuf("hg_att_s", [NS, HG, NS], ctx=ctx)
        gam = k.sbuf("hg_gamma", [12, 128], ctx=ctx)
        small = k.sbuf("hg_small", [128, 48], ctx=ctx)
        s0 = k.sbuf("hg_state", [128, C4, DEC_B, HD], ctx=ctx)
        q_b = k.sbuf("hg_q_b", [128, C4, DEC_B, NS], ctx=ctx)
        keyT = k.sbuf("hg_keyT", [128, TILES, 512], ctx=ctx)
        v_b = k.sbuf("hg_v_b", [NS, 2, DEC_B, HD], ctx=ctx)
        fin = k.sbuf("hg_fin", [128, C4, HD], ctx=ctx)
        new = k.sbuf("hg_new", [128, C4, DEC_B, HD], ctx=ctx)

        with nc.Block() as block:
            @block.sync
            def _(sp):
                sp.dma_start(gam[:, :], gamma.rearrange("r (c p) -> (r c) p", p=128)).then_inc(s["loaded"], 16)
                sp.dma_start(masks[:, :, :], k.level_masks).then_inc(s["mask_landed"], 16)
                for c in range(C4):
                    src = state[0, :, 2 * c:2 * c + 2].rearrange("b h k v -> (h k) b v")
                    sp.dma_start(s0[:, c, :, :], src).then_inc(s["mask_landed"], 16)

            @block.tensor
            def _(pe):
                pe.wait_ge(s["loaded"], 16)
                nc.tensor.transpose(k.bank(0)[:, 0:12], gam[:, :], k.c("ident")[0:12, 0:12]).then_inc(s["gamma_turned"], 1)

            @block.scalar
            def _(act):
                nc.scalar.activation(sg[:, :, :], hT[:, :, :], ACT.Sigmoid).then_inc(s["sigmoid"], 1)
                act.wait_ge(s["bounds_diff"], 1)
                nc.scalar.activation(small[:, 16:28], small[:, 16:28], ACT.Exp).then_inc(s["bounds_exp"], 1)

            @block.vector
            def _(dve):
                dve.wait_ge(s["gamma_turned"], 1)
                step(nc.vector.tensor_copy(small[:, 0:12], k.bank(0)[:, 0:12]))
                step(nc.vector.tensor_tensor(small[:, 12:16], small[:, 0:4], small[:, 4:8], ALU.max))
                step(nc.vector.tensor_tensor(small[:, 12:16], small[:, 12:16], small[:, 8:12], ALU.max))
                nc.vector.tensor_tensor(small[:, 16:28].rearrange("p (r c) -> p r c", c=4),
                                        small[:, 0:12].rearrange("p (r c) -> p r c", c=4),
                                        bc(small[:, 12:16], 1, 3), ALU.subtract).then_inc(s["bounds_diff"], 1)
                dve.wait_ge(s["bounds_exp"], 1)
                step(nc.vector.tensor_tensor(small[:, 28:32], small[:, 16:20], small[:, 20:24], ALU.add))
                step(nc.vector.tensor_tensor(small[:, 28:32], small[:, 28:32], small[:, 24:28], ALU.add))
                step(nc.vector.reciprocal(small[:, 28:32], small[:, 28:32]))
                step(nc.vector.tensor_tensor(small[:, 32:36], small[:, 16:20], small[:, 28:32], ALU.mult))
                step(nc.vector.tensor_scalar(small[:, 36:40], small[:, 32:36], -1.0, 1.0, ALU.mult, ALU.add))
                dve.wait_ge(s["sigmoid"], 1)
                nc.vector.tensor_tensor(pT, pT, sg[:, 0:C4, :], ALU.mult)
                for c in range(C4):
                    step(nc.vector.tensor_scalar(fT[:, c, :], sg[:, C4 + c, :], small[:, 36 + c:37 + c],
                                                 small[:, 32 + c:33 + c], ALU.mult, ALU.add))
                nc.vector.tensor_scalar(key[:, :, :], fT, -1.0, 1.0, ALU.mult, ALU.add)
                nc.vector.memset(att[:, :, :, :], 0.0)
                nc.vector.memset(att_s[:, :, :], 0.0)
                step(nc.vector.tensor_copy(tot[0][:, :, :], fT))
            @block.gpsimd
            def _(pool):
                pool.wait_ge(s["mask_landed"], 16 * (1 + C4))

        def level_products(a, b):
            for t in range(2):
                for hd in range(HG):
                    p = slice(64 * (hd % 2), 64 * (hd % 2) + 64)
                    dst = k.bank(2 * t + hd % 2)[:, (hd // 2) * 128:(hd // 2 + 1) * 128]
                    last = nc.tensor.matmul(dst, a[p, hd // 2, cols(t)], b[p, hd // 2, cols(t)], start=True, stop=True,
                                            skip_group_check=True)
            return last

        def sample_products(a, b):
            for hd in range(HG):
                p = slice(64 * (hd % 2), 64 * (hd % 2) + 64)
                last = nc.tensor.matmul(k.bank(4 + hd % 2)[0:NS, (hd // 2) * NS:(hd // 2 + 1) * NS], a[p, hd // 2, cols(2)], b[p, hd // 2, cols(2)],
                                        start=True, stop=True, skip_group_check=True)
            return last

        s_levels = 3
        with nc.Block() as block:
            @block.tensor
            def _(pe):
                for n in range(len(LEVELS) + 1):
                    if n:
                        pe.wait_ge(s["factors"], n)
                    if n < s_levels:
                        sample_products(key, pT)
                    level_products(key, pT).then_inc(s["products"], 1)
                pe.wait_ge(s["factors"], len(LEVELS) + 1)
                for hd in range(HG):
                    p = slice(64 * (hd % 2), 64 * (hd % 2) + 64)
                    last = nc.tensor.matmul(k.bank(6 + hd % 2)[:, (hd // 2) * 128:(hd // 2 + 1) * 128], key[p, hd // 2, cols(0)],
                                            pT[p, hd // 2, cols(1)], start=True, stop=True, skip_group_check=True)
                last.then_inc(s["products"], 1)

            @block.vector
            def _(dve):
                def halves(x, a, b, m):
                    v = x[:, :, a:b].rearrange("p c (n z m) -> p c n z m", z=2, m=m)
                    return v[:, :, :, 0, :], v[:, :, :, 1, :]

                for n in range(len(LEVELS) + 1):
                    dve.wait_ge(s["products"], n + 1)
                    for t in range(2):
                        src = k.ps[:, 2 * t:2 * t + 2, :].rearrange("p a (b t) -> p (a b) t", t=128)
                        last = nc.vector.copy_predicated(att[:, t, :, :], bc(masks[:, n, :], 1, HG), src)
                    if n < s_levels:
                        for odd in range(2):
                            last = nc.vector.copy_predicated(att_s[:, C4 * odd:C4 * (odd + 1), :], bc(masks[0:NS, n, 0:NS], 1, C4),
                                                             k.bank(4 + odd)[0:NS, 0:C4 * NS].rearrange("p (h t) -> p h t", t=NS))
                    step(last)
                    if n == 0:
                        nc.vector.tensor_tensor(pT, pT, fT, ALU.mult).then_inc(s["factors"], 1)
                        continue
                    m = LEVELS[n - 1]
                    old, nxt = tot[(n - 1) % 2], tot[n % 2]
                    ranges = [(NS, NTOK)] + ([(0, NS)] if m < DEC_T else [])
                    for a, b in ranges:
                        cnt = (b - a) // (2 * m)
                        o = old[:, :, a:a + 2 * cnt].rearrange("p c (n z) -> p c n z", z=2)
                        k1, _ = halves(key, a, b, m)
                        _, q2 = halves(pT, a, b, m)
                        nc.vector.tensor_tensor(q2, q2, bc(o[:, :, :, 0], 3, m), ALU.mult)
                        nc.vector.tensor_tensor(k1, k1, bc(o[:, :, :, 1], 3, m), ALU.mult)
                        last = nc.vector.tensor_tensor(nxt[:, :, a:a + cnt], o[:, :, :, 0], o[:, :, :, 1], ALU.mult)
                    if m >= DEC_T:
                        last = nc.vector.tensor_copy(nxt[:, :, 0:DEC_B], old[:, :, 0:DEC_B])
                    step(last)
                    nc.vector.memset(small[:, 40:41], 0.0).then_inc(s["factors"], 1)
                dve.wait_ge(s["products"], len(LEVELS) + 2)
                step(nc.vector.tensor_copy(cross[:, :, :], k.ps[:, 6:8, :].rearrange("p a (b t) -> p (a b) t", t=128)))
                tN = tot[len(LEVELS) % 2]
                step(nc.vector.tensor_tensor(key[:, :, cols(0)], key[:, :, cols(0)],
                                             tN[:, :, NS + 1:NS + 2].broadcast_to([128, C4, 128]), ALU.mult))
                for c in range(C4):
                    last = nc.vector.tensor_tensor(q_b[:, c, :, :], bc(pT[:, c, SMP], 1, DEC_B), k.c("batch_cols"), ALU.mult)
                step(last)
        tN = tot[len(LEVELS) % 2]

        alone(k, transposes(k, "hg_keys", [
            ([key[:, c, cols(t)] for c in range(C4)], keyT[0:ROWS[t], t, :].rearrange("p (c x) -> p c x", x=128))
            for t in range(TILES)]))

        with nc.Block() as block:
            @block.vector
            def _(dve):
                for hd in range(HG):
                    if hd >= 2:
                        dve.wait_ge(s["state_product"], hd - 1)
                    vs = h[0:NS, 2, V0 + HD * hd:V0 + HD * (hd + 1)]
                    nc.vector.tensor_tensor(v_b[:, hd % 2, :, :], bc(vs, 1, DEC_B),
                                            bc(k.c("batch_rows")[0:NS, :], 2, HD), ALU.mult).then_inc(s["spread"], 1)
                dve.wait_ge(s["out_product"], 1)
                step(nc.vector.tensor_copy(fin[:, :, :], k.bank(3)[:, 256:512].rearrange("p (c v) -> p c v", v=HD)))
                dve.wait_ge(s["state_product"], HG)
                for c in range(C4):
                    step(nc.vector.tensor_tensor(new[:, c], s0[:, c], bc(tN[:, c, 0:DEC_B], 2, HD), ALU.mult))
                    step(nc.vector.tensor_tensor(new[:, c], new[:, c], k.bank(4 + c).rearrange("p (b v) -> p b v", v=HD), ALU.add))
                nc.vector.memset(k.pad[:, :], 0.0).then_inc(s["state_ready"], 1)

            @block.tensor
            def _(pe):
                mm = lambda *a, **b: nc.tensor.matmul(*a, skip_group_check=True, **b)
                for hd in range(HG):
                    odd, c = hd % 2, hd // 2
                    p = slice(64 * odd, 64 * odd + 64)
                    hv = slice(V0 + HD * hd, V0 + HD * (hd + 1))
                    hk = slice(HD * hd, HD * (hd + 1))
                    place = C4 * odd + c
                    at = slice(HD * place, HD * (place + 1))
                    o = [k.bank(t)[0:ROWS[t], at] for t in range(TILES)]
                    mm(o[0], att[:, 0, place, :], h[:, 0, hv], start=True, stop=True)
                    mm(o[1], att[:, 1, place, :], h[:, 1, hv], start=True, stop=False)
                    mm(o[1], cross[:, place, :], h[:, 0, hv], start=False, stop=True)
                    mm(o[2], att_s[:, place, :], h[0:NS, 2, hv], start=True, stop=bool(odd))
                    own = k.bank(3)[0:NS, HD * c:HD * (c + 1)] if odd else o[2]
                    for b in range(DEC_B):
                        mm(own, q_b[p, c, b, :], s0[p, c, b, :], start=bool(odd and b == 0), stop=(b == DEC_B - 1))
                    last_state = k.bank(3)[p, 256 + HD * c:256 + HD * (c + 1)]
                    mm(last_state, keyT[:, 0, hk], h[:, 0, hv], start=True, stop=False)
                    last = mm(last_state, keyT[:, 1, hk], h[:, 1, hv], start=False, stop=True)
                last.then_inc(s["out_product"], 1)
                for hd in range(HG):
                    pe.wait_ge(s["spread"], hd + 1)
                    p = slice(64 * (hd % 2), 64 * (hd % 2) + 64)
                    mm(k.bank(4 + hd // 2)[p, :], keyT[0:NS, 2, HD * hd:HD * (hd + 1)],
                       v_b[:, hd % 2].rearrange("p b v -> p (b v)"), start=True, stop=True).then_inc(s["state_product"], 1)

            @block.sync
            def _(sp):
                sp.wait_ge(s["state_ready"], 1)
                k.store(sp, state_prompt[0, 0].rearrange("(c e) k v -> (e k) c v", e=2), fin[:, :, :])
                for c in range(C4):
                    dst = state_sample[0, :, 2 * c:2 * c + 2].rearrange("b h k v -> (h k) b v")
                    k.store(sp, dst, new[:, c])
                k.wait_for_stores(sp)

    with ExitStack() as ctx:
        o = k.sbuf("hg_o", [128, 512], ctx=ctx)
        sq = k.sbuf("hg_sq", [128, 512], ctx=ctx)
        sgate = k.sbuf("hg_sgate", [128, TILES, 512], ctx=ctx)
        ms = k.sbuf("hg_ms", [128, 16], ctx=ctx)
        g = k.sbuf("hg_norm_g", [128, 512], ctx=ctx)
        row = k.sem("hg_row")
        block = ctx.enter_context(nc.Block())

        @block.sync
        def _(sp):
            sp.dma_start(g[:, :], norm_g.partition_broadcast(128)).then_inc(row, 16)

        @block.scalar
        def _(act):
            for t, r in enumerate(ROWS):
                nc.scalar.activation(sgate[0:r, t, :], h[0:r, t, G0:G0 + 512], ACT.Sigmoid).then_inc(s["gates"], 1)
            for t, r in enumerate(ROWS):
                act.wait_ge(s["squares"], t + 1)
                nc.scalar.activation(ms[0:r, 8:16], ms[0:r, 0:8], ACT.Sqrt).then_inc(s["root"], 1)

        @block.vector
        def _(dve):
            dve.wait_ge(row, 16)
            for t, r in enumerate(ROWS):
                dve.wait_ge(s["gates"], t + 1)
                per_head = lambda x: x.rearrange("p (h v) -> p h v", v=HD)
                for odd in range(2):
                    src = k.bank(t)[0:r, 256 * odd:256 * (odd + 1)].rearrange("p (c v) -> p c v", v=HD)
                    dst = o[0:r, :].rearrange("p (c e v) -> p c e v", e=2, v=HD)[:, :, odd, :]
                    step(nc.vector.tensor_copy(dst, src))
                if t == 2:
                    step(nc.vector.tensor_tensor(dst, dst, k.bank(3)[0:r, 0:256].rearrange("p (c v) -> p c v", v=HD), ALU.add))
                step(nc.vector.tensor_tensor(sq[0:r, :], o[0:r, :], o[0:r, :], ALU.mult))
                step(nc.vector.tensor_reduce(ms[0:r, 0:8], per_head(sq[0:r, :]), AX, ALU.add))
                step(nc.vector.tensor_scalar(ms[0:r, 0:8], ms[0:r, 0:8], 1.0 / HD, RMS_EPS, ALU.mult, ALU.add))
                nc.vector.memset(k.pad[0:r, :], 0.0).then_inc(s["squares"], 1)
                dve.wait_ge(s["root"], t + 1)
                step(nc.vector.reciprocal(ms[0:r, 8:16], ms[0:r, 8:16]))
                step(nc.vector.tensor_tensor(per_head(o[0:r, :]), per_head(o[0:r, :]), bc(ms[0:r, 8:16], 2, HD), ALU.mult))
                step(nc.vector.tensor_tensor(o[0:r, :], o[0:r, :], g[0:r, :], ALU.mult))
                step(nc.vector.tensor_tensor(sq[0:r, :], h[0:r, t, G0:G0 + 512], sgate[0:r, t, :], ALU.mult))
                step(nc.vector.tensor_tensor(cat[0:r, t, :], o[0:r, :], sq[0:r, :], ALU.mult))




def sparse_attention(k, h, catT, pages, cmp_cache, slc_cache, win_cache, pe_rows, outs):
    nc, step = k.nc, k.dve_steps
    (cmp_p, cmp_s, slc_p, slc_s, win_p, win_s) = outs
    with ExitStack() as outer:
        qn = k.sbuf("qn", [128, TILES, 512], ctx=outer)
        qr = k.sbuf("qr", [128, TILES, 512], ctx=outer)
        gates = k.sbuf("gates", [128, TILES, 24], ctx=outer)
        gates_s = k.sbuf("gates_s", [128, 6], ctx=outer)
        qT = {n: k.sbuf("q_T" + n, [128, GR, NTOK], ctx=outer) for n in ("nope", "rope")}
        kT = {n: k.sbuf("kT_" + n, [128, NTOK], ctx=outer) for n in ("slc", "win")}
        cache = {n: k.sbuf("cache_" + n, [128, DEC_B, NPG, 256], ctx=outer) for n in ("cmp", "slc", "win")}
        kTs = {n: k.sbuf("kTs_" + n, [128, DEC_B, PAST], ctx=outer) for n in ("slc", "win")}
        q_b = {n: k.sbuf("q_b" + n, [128, DEC_B, GR, NS], ctx=outer) for n in ("nope", "rope")}
        q_new = k.sbuf("q_new", [128, GR, NS], ctx=outer)
        kc = k.sbuf("kc", [128, 1 + DEC_B, NBLK], ctx=outer)
        vc = k.sbuf("vc", [NBLK, 1 + DEC_B, 128], ctx=outer)
        pe_sb = k.sbuf("cmp_pe", [32, 128], ctx=outer)
        pt = k.sbuf("pages", [128, 16], I32, outer)
        ptf = k.sbuf("pages_f", [128, 16], ctx=outer)
        idx = k.sbuf("page_rows", [128, 16], U32, outer)
        tmp = k.sbuf("rot_tmp", [128, 4, 256], ctx=outer)
        pt_landed, idx_ready, gathered, pe_landed = k.sem("pages_landed"), k.sem("page_rows_ready"), k.sem("pages_gathered"), k.sem("pe_landed")
        gate_done, rotated, regrouped = k.sem("gates_ready"), k.sem("rotated"), k.sem("regrouped")

        with nc.Block() as block:
            @block.sync
            def _(sp):
                sp.dma_start(pt[:, :], pages.rearrange("b n -> (b n)").partition_broadcast(128)).then_inc(pt_landed, 16)
                sp.dma_start(pe_sb[:, :], pe_rows[0].rearrange("r h d -> r (h d)")).then_inc(pe_landed, 16)
                for b in range(DEC_B):
                    sp.dma_start(cache["win"][:, b], win_cache[0, b].rearrange("(n p) x h d -> p n (x h d)", p=128)).then_inc(pe_landed, 16)
                sp.wait_ge(rotated, 1)
                for at, prompt, sample in ((CMP0, cmp_p, cmp_s), (SLC0, slc_p, slc_s), (WIN0, win_p, win_s)):
                    k.store(sp, prompt[0, 0].rearrange("(t p) x h d -> p t (x h d)", p=128), h[:, 0:2, at:at + 256])
                    k.store(sp, sample[0].rearrange("b t x h d -> (b t) (x h d)"), h[0:NS, 2, at:at + 256])
                sp.wait_ge(pe_landed, 16 * (1 + DEC_B))
                k.wait_for_stores(sp)

            @block.scalar
            def _(act):
                for t, r in enumerate(ROWS):
                    src = h[0:r, t, Q0:Q0 + 512].rearrange("p (kv g d) -> p g kv d", kv=KV, g=GR)
                    dst = qn[0:r, t, :].rearrange("p (g kv d) -> p g kv d", kv=KV, g=GR)
                    nc.scalar.copy(dst, src).then_inc(regrouped, 1)
                for t, r in enumerate(ROWS):
                    nc.scalar.activation(gates[0:r, t, :], h[0:r, t, GATE0:GATE0 + 24], ACT.Sigmoid).then_inc(gate_done, 1)

            @block.vector
            def _(dve):
                dve.wait_ge(pt_landed, 16)
                step(nc.vector.tensor_copy(ptf[:, :], pt[:, :]))
                step(nc.vector.tensor_scalar(ptf[:, :], ptf[:, :], float(PAGE), k.c("row"), ALU.mult, ALU.add))
                nc.vector.tensor_copy(idx[:, :], ptf[:, :]).then_inc(idx_ready, 1)
                for t, r in enumerate(ROWS):
                    dve.wait_ge(regrouped, t + 1)
                    rotate(k, qn[0:r, t, :], qr[0:r, t, :], (t, r), 8, tmp)
                    for at in (SLC0, WIN0):
                        rotate(k, h[0:r, t, at:at + 128], h[0:r, t, at:at + 128], (t, r), KV, tmp)
                nc.vector.memset(k.pad[:, :], 0.0).then_inc(rotated, 1)
                dve.wait_ge(gate_done, TILES)
                for g in range(GR):
                    src = gates[0:NS, 2, :].rearrange("p (a g) -> p a g", g=GR)[:, :, g]
                    last = nc.vector.tensor_copy(gates_s[NS * g:NS * (g + 1), :], src)
                step(last)

            @block.gpsimd
            def _(pool):
                pool.wait_ge(idx_ready, 1)
                for n, src in (("cmp", cmp_cache), ("slc", slc_cache)):
                    rows = src[0].rearrange("n p x h d -> (n p) (x h d)")
                    for j in range(DEC_B * NPG):
                        nc.gpsimd.indirect_dma_start(out=cache[n][:, j // NPG, j % NPG, :], out_offset=None, in_=rows,
                                                     in_offset=bass.IndirectOffsetOnAxis(ap=idx[:, j:j + 1], axis=0)).then_inc(gathered, 16)
                pool.wait_ge(gathered, 16 * 2 * DEC_B * NPG)

        groups = []
        for t, r in enumerate(ROWS):
            for n, x in (("nope", qn), ("rope", qr)):
                groups.append(([x[0:r, t, 128 * g:128 * (g + 1)] for g in range(GR)], qT[n][:, :, cols(t)]))
            for n, at in (("slc", SLC0), ("win", WIN0)):
                groups.append(([h[0:r, t, at:at + 128]], kT[n][:, cols(t)]))
        for n in ("slc", "win"):
            for b in range(0, DEC_B, 2):
                groups.append(([cache[n][:, b + j // NPG, j % NPG, 0:128] for j in range(2 * NPG)],
                               kTs[n][:, b:b + 2, :].rearrange("p b s -> p (b s)")))
        alone(k, transposes(k, "nsa", groups))

        pooled = k.sem("pooled")
        with nc.Block() as block:
            @block.tensor
            def _(pe):
                pool, mean = k.c("pool"), k.c("mean32")
                mm = lambda *a, **b: nc.tensor.matmul(*a, skip_group_check=True, **b)
                for i in range(1 + DEC_B):
                    raw = (lambda t: h[:, t, CMP0:CMP0 + 256]) if i == 0 else (lambda t, b=i - 1: cache["cmp"][:, b, t, :])
                    kk, vv = k.bank(0)[:, NBLK * i:NBLK * (i + 1)], k.bank(1 + i // 4)[0:NBLK, 128 * (i % 4):128 * (i % 4 + 1)]
                    for t in range(NPG):
                        mm(kk, raw(t)[:, 0:128], pool[:, t, :], start=(t == 0), stop=False)
                        mm(vv, pool[:, t, :], raw(t)[:, 128:256], start=(t == 0), stop=(t == NPG - 1))
                    last = mm(kk, pe_sb[:, :], mean[0:32, :], start=False, stop=True)
                last.then_inc(pooled, 1)

            @block.vector
            def _(dve):
                for n in ("nope", "rope"):
                    for g in range(GR):
                        last = nc.vector.tensor_tensor(q_b[n][:, :, g, :], bc(qT[n][:, g, SMP], 1, DEC_B), k.c("batch_cols"), ALU.mult)
                nc.vector.tensor_copy(q_new[:, :, :], qT["rope"][:, :, SMP])
                dve.wait_ge(pooled, 1)
                nc.vector.tensor_copy(kc[:, :, :], k.bank(0)[:, 0:NBLK * (1 + DEC_B)].rearrange("p (i c) -> p i c", c=NBLK))
                step(nc.vector.tensor_copy(vc[:, :, :].rearrange("p i d -> p (i d)"),
                                           k.ps[0:NBLK, 1:4, :].rearrange("p a b -> p (a b)")[:, 0:128 * (1 + DEC_B)]))

        items = []
        for t in range(2):
            bank = 6 + t
            out = k.bank(bank).rearrange("p (g q) -> p g q", q=128)
            for br, n in ((1, "slc"), (2, "win"), (0, "cmp")):
                for kv in range(KV):
                    p = slice(64 * kv, 64 * kv + 64)
                    nk = NBLK if n == "cmp" else 128 * (t + 1)
                    q = qT["nope" if n == "cmp" else "rope"]
                    keys = kc[p, 0, :] if n == "cmp" else kT[n][p, NS:NS + nk]
                    base = {"cmp": CMP0, "slc": SLC0, "win": WIN0}[n] + 128
                    parts = []
                    for j in range(1 if n == "cmp" else t + 1):
                        val = vc[:, 0, p] if n == "cmp" else h[:, j, base + 64 * kv:base + 64 * kv + 64]
                        kn = NBLK if n == "cmp" else 128
                        parts.append((128 * j, kn, [(k.bank(bank)[p, :], val, lambda pT: pT,
                                                     n == "slc" and j == 0, n == "cmp")]))
                    gate = gates[:, t, :].rearrange("p (a k g) -> p a k g", a=3, k=KV)[:, br, kv, :]
                    leave = [(catT[:, 4:8, cols(t)], out)] if (n, kv) == ("cmp", KV - 1) else []
                    items.append(dict(
                        rows=128, groups=GR, n=nk, mask=k.c("cmp_mask")[:, t, :] if n == "cmp" else k.c("causal")[:, t, 0:nk],
                        scores=[(0, 128, g * nk, nk, q[p, g, cols(t)], keys, True, True) for g in range(GR)],
                        count=None, gate=gate, parts=parts, leave=leave))
        out = k.bank(6)[:, 0:GR * NS]
        for br, n in ((1, "slc"), (2, "win"), (0, "cmp")):
            for kv in range(KV):
                p = slice(64 * kv, 64 * kv + 64)
                nk = NBLK if n == "cmp" else PAST + NS
                qb = q_b["nope" if n == "cmp" else "rope"]
                keys = (lambda b: kc[p, 1 + b, :]) if n == "cmp" else (lambda b: kTs[n][p, b, :])
                width = NBLK if n == "cmp" else PAST
                scores = [(0, 128, 0, width, qb[p, b].rearrange("p g t -> p (g t)"), keys(b), b == 0, b == DEC_B - 1) for b in range(DEC_B)]
                own = lambda b: (lambda pT: pT[:, 0:128].rearrange("p (g t) -> p g t", t=NS)[:, :, DEC_T * b:DEC_T * (b + 1)])
                dst = lambda b: out[p, :].rearrange("p (g t) -> p g t", t=NS)[:, :, DEC_T * b:DEC_T * (b + 1)]
                base = {"cmp": CMP0, "slc": SLC0, "win": WIN0}[n] + 128 + 64 * kv
                if n == "cmp":
                    parts = [(0, NBLK, [(dst(b), vc[:, 1 + b, p], own(b), False, True) for b in range(DEC_B)])]
                else:
                    scores.append((0, 128, PAST, NS, q_new[p].rearrange("p g t -> p (g t)"), kT[n][p, SMP], True, True))
                    parts = [(PAST, NS, [(out[p, :], h[0:NS, 2, base:base + 64], lambda pT: pT[:, 0:128], n == "slc", False)])]
                    parts += [(128 * j, 128, [(dst(b), cache[n][:, b, j, 128 + 64 * kv:192 + 64 * kv], own(b), False, False)
                                              for b in range(DEC_B)]) for j in range(NPG)]
                leave = [(catT[:, 4:8, SMP], out.rearrange("p (g t) -> p g t", t=NS))] if (n, kv) == ("cmp", KV - 1) else []
                items.append(dict(rows=128, groups=1, n=nk, mask=None if n == "cmp" else k.c("new_causal"), scores=scores, count=None,
                                  gate=gates_s[:, KV * br + kv:KV * br + kv + 1], parts=parts, leave=leave))
        alone(k, attention(k, "nsa", items, attention_buffers(k, "nsa", 1024, 512, outer)))




def rotate_and_store(k, name, qk, val, tiles, out_p, out_s, tmp):
    nc = k.nc
    rotated = k.sem(name, "rotated")
    stage = Stage(k, 4 * len(tiles))

    @stage.on("vector")
    def _(dve):
        for n, t in enumerate(tiles):
            r = ROWS[t]
            for at in (0, 512, 1024, 1536):
                rotate(k, qk[0:r, n, at:at + 512], qk[0:r, n, at:at + 512], (t, r), HEADS // 2, tmp)
                if at == 1536:
                    nc.vector.memset(k.pad[:, :], 0.0).then_inc(rotated, 1)
                yield

    @stage.on("sync")
    def _(sp):
        for n, t in enumerate(tiles):
            sp.wait_ge(rotated, n + 1)
            dst = out_s[0].rearrange("b t x h d -> (b t) x (h d)") if t == 2 else \
                out_p[0, 0, 128 * t:128 * (t + 1)].rearrange("p x h d -> p x (h d)")
            k.store(sp, dst[:, 0, :], qk[0:ROWS[t], n, D:2 * D])
            k.store(sp, dst[:, 1, :], val[0:ROWS[t], t, :])
        k.wait_for_stores(sp)
    return stage


def dilated_prompt(k, name, t, qT, kT, val, catT, bufs, pairs, turn_banks, out_bank):
    items = []
    nk = 128 * (t + 1)
    for q4 in range(HEADS // 4):
        head = [4 * q4 + g for g in (0, 2, 1, 3)]
        parts = []
        for j in range(t + 1):
            parts.append((128 * j, 128, [
                (k.bank(out_bank)[64 * (head[g] % 2):64 * (head[g] % 2) + 64, 128 * (g % 2):128 * (g % 2 + 1)],
                 val[:, j, HD * head[g]:HD * (head[g] + 1)], (lambda pT, g=g: pT[:, 128 * g:128 * (g + 1)]),
                 j == 0 and g % 2 == 0, j == t) for g in range(4)]))
        items.append(dict(
            rows=128, groups=4, n=nk, apart=SEQ, mask=k.c("dil_mask")[:, t, 0:nk], count=k.c("dil_count")[:, t, 0:nk], gate=None,
            scores=[(0, 128, g * SEQ, nk, qT[64 * (hd % 2):64 * (hd % 2) + 64, hd // 2, cols(t)],
                     kT[64 * (hd % 2):64 * (hd % 2) + 64, hd // 2, NS:NS + nk], True, True) for g, hd in enumerate(head)],
            parts=parts,
            leave=[(catT[:, 2 * q4:2 * q4 + 2, cols(t)], k.bank(out_bank)[:, 0:256].rearrange("p (c q) -> p c q", q=128))]))
    return attention(k, name, items, bufs, pairs, turn_banks)


def dilated_sample(k, name, q4, cache, qT, kT, val, catT, ctx, banks, pairs, turn_banks, out_bank):
    nc = k.nc
    kv = k.sbuf(name + "_cache", [128, 2, DEC_B, NPG, 256], ctx=ctx)
    kTs = k.sbuf(name + "_kTs", [128, 2, DEC_B, PAST], ctx=ctx)
    q_b = k.sbuf(name + "_q_b", [128, 2, DEC_B, NS], ctx=ctx)
    bufs = attention_buffers(k, name, PAST + NS, 128, ctx)
    loads = [(kv[:, x, b], cache[0, b, :, x, 4 * q4:4 * q4 + 4].rearrange("(n p) h d -> p n (h d)", p=128))
             for x in range(2) for b in range(DEC_B)]
    groups = []
    for c in range(2):
        for b in range(0, DEC_B, 2):
            groups.append(([kv[:, 0, b + j // NPG, j % NPG, 128 * c:128 * (c + 1)] for j in range(2 * NPG)],
                           kTs[:, c, b:b + 2, :].rearrange("p b s -> p (b s)")))
    turn_keys = transposes(k, name + "_k", groups, banks, loads)
    spread = Stage(k, 1)

    @spread.on("vector")
    def _(dve):
        for c in range(2):
            last = nc.vector.tensor_tensor(q_b[:, c], bc(qT[:, 2 * q4 + c, SMP], 1, DEC_B), k.c("batch_cols"), ALU.mult)
        k.dve_steps(last)
        yield
    scores, new, old = [], [], [[] for _ in range(NPG)]
    out = lambda g: k.bank(out_bank)[64 * (g % 2):64 * (g % 2) + 64, NS * (g // 2):NS * (g // 2 + 1)]
    for g in range(4):
        p = slice(64 * (g % 2), 64 * (g % 2) + 64)
        hd = 4 * q4 + g
        for b in range(DEC_B):
            scores.append((NS * g, NS, 0, PAST, q_b[p, g // 2, b, :], kTs[p, g // 2, b, :], b == 0, b == DEC_B - 1))
            for j in range(NPG):
                c0 = NS * g + DEC_T * b
                old[j].append((out(g)[:, DEC_T * b:DEC_T * (b + 1)], kv[:, 1, b, j, HD * g:HD * (g + 1)],
                               (lambda pT, c0=c0: pT[:, c0:c0 + DEC_T]), False, j == NPG - 1))
        scores.append((NS * g, NS, PAST, NS, qT[p, hd // 2, SMP], kT[p, hd // 2, SMP], True, True))
        new.append((out(g), val[0:NS, 2, HD * hd:HD * (hd + 1)],
                    (lambda pT, g=g: pT[:, NS * g:NS * (g + 1)]), g < 2, False))
    parts = [(PAST, NS, new)] + [(128 * j, 128, old[j]) for j in range(NPG)]
    item = dict(rows=128, groups=1, n=PAST + NS, mask=k.c("new_mask"), count=k.c("new_count"), gate=None, scores=scores, parts=parts,
                leave=[(catT[:, 2 * q4:2 * q4 + 2, SMP], k.bank(out_bank)[:, 0:2 * NS].rearrange("p (c q) -> p c q", q=NS))])
    return [turn_keys, spread, attention(k, name, [item], bufs, pairs, turn_banks)]




def turn_keys(k, name, sub_keys, keys, keysT, banks):
    return transposes(k, name, [([keys[:, 4 * i + j, :] for j in range(4)], keysT[:, 4 * i:4 * i + 4, :]) for i in range(4)],
                      banks, [(keys[:, :, :], sub_keys.rearrange("h c k d -> k (h c) d"))])


def route(k, name, layer, t, qT, keysT, slots, gate, xs, ctx, bank0, routed=None):
    nc, step = k.nc, k.dve_steps
    HC, r, v = 2 * PH, ROWS[t], k.nc.vector
    s = k.sbuf(name + "_s", [128, HC, NK], ctx=ctx)
    val = k.sbuf(name + "_val", [128, HC, PK], ctx=ctx)
    at = k.sbuf(name + "_at", [128, HC, PK], U32, ctx)
    atf = k.sbuf(name + "_atf", [128, HC, PK], ctx=ctx)
    top = k.sbuf(name + "_top", [128, PH, PK], ctx=ctx)
    sel = k.sbuf(name + "_sel", [128, PH, PK], U32, ctx)
    half = k.sbuf(name + "_half", [128, 2, PH, PK], U32, ctx)
    halff = k.sbuf(name + "_halff", [128, 2, PH, PK], ctx=ctx)
    ef = k.sbuf(name + "_ef", [128, 2, PH, PK], ctx=ctx)
    e = k.sbuf(name + "_e", [128, PH, PK], ctx=ctx)
    den = k.sbuf(name + "_den", [128, PH], ctx=ctx)
    scored, less, expd = k.sem(name, "scored"), k.sem(name, "less_top"), k.sem(name, "expd")
    cand = s[:, :, :].rearrange("p (h x) n -> p h (x n)", x=2)
    PIECE = 4
    SCORE_TICKS, EXP_TICK = 4, 50
    TICKS = 54
    stage = Stage(k, TICKS)

    @stage.on("tensor")
    def _(pe):
        for i in range(HC):
            last = nc.tensor.matmul(k.bank(bank0 + i // 4)[0:r, 128 * (i % 4):128 * (i % 4 + 1)], qT[:, i, cols(t)],
                                    keysT[:, i, :], start=True, stop=True, skip_group_check=True)
            if i == HC - 1:
                last.then_inc(scored, 1)
            if i % 4 == 3:
                yield
        for _ in range(TICKS - SCORE_TICKS):
            yield

    @stage.on("scalar")
    def _(act):
        for _ in range(EXP_TICK):
            yield
        act.wait_ge(less, 1)
        nc.scalar.activation(e[0:r], e[0:r], ACT.Exp).then_inc(expd, 1)
        for _ in range(TICKS - EXP_TICK):
            yield

    @stage.on("vector")
    def _(dve):
        count = 0
        for _ in range(SCORE_TICKS):
            count += 1
            yield
        dve.wait_ge(scored, 1)
        for b in range(0, 4, 2):
            step(v.tensor_copy(s[0:r, 4 * b:4 * b + 8].rearrange("p a b -> p (a b)"),
                               k.ps[0:r, bank0 + b:bank0 + b + 2, :].rearrange("p a b -> p (a b)")))
            count += 1
            yield

        def sixteen_best(x, best, where, n):
            for i0 in range(0, n, PIECE):
                some = range(i0, i0 + PIECE)
                for i in some:
                    last = v.max(best[0:r, i, 0:8], x[0:r, i, :])
                step(last)
                for i in some:
                    last = v.max_index(where[0:r, i, 0:8], best[0:r, i, 0:8], x[0:r, i, :])
                step(last)
                yield
                for i in some:
                    last = v.match_replace(x[0:r, i, :], best[0:r, i, 0:8], x[0:r, i, :], -3e38)
                step(last)
                for i in some:
                    last = v.max(best[0:r, i, 8:16], x[0:r, i, :])
                step(last)
                yield
                for i in some:
                    last = v.max_index(where[0:r, i, 8:16], best[0:r, i, 8:16], x[0:r, i, :])
                step(last)
                yield

        for _ in sixteen_best(s, val, at, HC):
            count += 1
            yield
        v.tensor_copy(atf[0:r], at[0:r])
        for hd in range(PH):
            last = v.tensor_tensor(cand[0:r, hd].rearrange("p (i j) -> p i j", j=PK), bc(val[0:r, 2 * hd, :], 2, PK),
                                   bc(val[0:r, 2 * hd + 1, :], 1, PK), ALU.add)
            if hd % 4 == 3:
                step(last)
                count += 1
                yield
        for _ in sixteen_best(cand, top, sel, PH):
            count += 1
            yield
        v.tensor_scalar(half[0:r, 0], sel[0:r], 4, None, ALU.logical_shift_right)
        step(v.tensor_scalar(half[0:r, 1], sel[0:r], 15, None, ALU.bitwise_and))
        step(v.tensor_copy(halff[0:r], half[0:r]))
        for c in range(2):
            for op in (ALU.is_equal, ALU.mult):
                for hd in range(PH):
                    eq = cand[0:r, hd].rearrange("p (k j) -> p k j", j=PK)
                    if op == ALU.is_equal:
                        last = v.tensor_tensor(eq, bc(halff[0:r, c, hd, :], 2, PK), bc(k.c("iota16")[0:r, :], 1, PK), op)
                    else:
                        last = v.tensor_tensor(eq, eq, bc(atf[0:r, 2 * hd + c, :], 1, PK), op)
                    if hd % 4 == 3:
                        step(last)
                        count += 1
                        yield
            step(v.tensor_reduce(ef[0:r, c].rearrange("p h k -> p (h k)"), cand[0:r].rearrange("p h (k j) -> p (h k) j", j=PK),
                                 AX, ALU.add))
            count += 1
            yield
        step(v.scalar_tensor_tensor(ef[0:r, 0], ef[0:r, 0], float(NK), ef[0:r, 1], ALU.mult, ALU.add))
        step(v.tensor_scalar(ef[0:r, 0], ef[0:r, 0], float(layer * EXPERTS), None, ALU.add))
        v.tensor_tensor(e[0:r], top[0:r], top[0:r, :, 0:1].broadcast_to([r, PH, PK]), ALU.subtract).then_inc(less, 1)
        assert count <= EXP_TICK, count
        while count < EXP_TICK + 1:
            count += 1
            yield
        dve.wait_ge(expd, 1)
        step(v.tensor_reduce(den[0:r], e[0:r], AX, ALU.add))
        step(v.reciprocal(den[0:r], den[0:r]))
        step(v.tensor_tensor(e[0:r], e[0:r], bc(den[0:r], 2, PK), ALU.mult))
        count += 1
        yield
        if t < 2:
            v.tensor_copy(slots, ef[:, 0].rearrange("p h k -> p (h k)"))
            last = v.tensor_copy(gate, e[:].rearrange("p h k -> p (h k)"))
        else:
            for q in range(4):
                some = slice(NS * q, NS * (q + 1))
                v.tensor_copy(slots[some, 0:NS], ef[0:r, 0].rearrange("p h k -> p (h k)")[:, some])
                v.tensor_copy(xs[some, :], k.x[0:NS, 2, :])
                last = v.tensor_copy(gate[some, 0:NS], e[0:r].rearrange("p h k -> p (h k)")[:, some])
        step(last)
        if routed is not None:
            v.memset(k.pad[:, :], 0.0).then_inc(routed, 1)
        while count < TICKS:
            count += 1
            yield
    return stage


ORDER = (2, 0, 1)
VISITS = [(layer, t) for layer in range(DEPTH) for t in ORDER]
STEPS = [SLOTS // 4 if t == 2 else SLOTS for _, t in VISITS]
FIRST = [sum(STEPS[:i]) for i in range(len(STEPS) + 1)]


class Experts:

    def __init__(self, k, table, slots, gate, xs, gain, bias, outs, ctx):
        self.k, self.table, self.slots, self.gate, self.xs, self.outs = k, table, slots, gate, xs, outs
        self.gain, self.bias = gain, bias
        self.uv = k.sbuf("uv", [128, RING, 2 * D], ctx=ctx)
        self.dot, self.gelu, self.wgt = [k.sbuf(n, [128, 2, GROUP], ctx=ctx) for n in ("dot", "gelu", "wgt")]
        self.diag = k.sbuf("diag", [128, RING, 128], ctx=ctx)
        self.gb = k.sbuf("ffn_gb", [128, DEPTH, 2, D], ctx=ctx)
        self.z = k.sbuf("ffn_z", [128, D], ctx=ctx)
        self.stats = k.sbuf("ffn_stats", [128, 16], ctx=ctx)
        self.landed = [k.sem(f"row_landed{i}") for i in range(RING)]
        (self.dotted, self.gelued, self.weighed, self.spread, self.used, self.variance, self.rooted, self.rows_in, self.sum_read,
         self.normed, self.routed) = [k.sem(n) for n in (
             "dotted", "gelued", "weighed", "spread", "row_used", "ffn_variance", "ffn_rooted", "ffn_rows_in", "sum_read", "normed",
             "routed")]
        self.n = FIRST[-1]
        self.ticks = self.n + LAG + 3

    def visit(self, s):
        return max(i for i in range(len(VISITS)) if FIRST[i] <= s)

    def at(self, s):
        i = self.visit(s)
        return VISITS[i][1], s - FIRST[i]

    def pool(self, pool):
        for s in range(self.n):
            t, j = self.at(s)
            i = self.visit(s)
            if j == 0 and i:
                pool.wait_ge(self.routed, i)
            if s >= RING:
                pool.wait_ge(self.used, s - RING + 1)
            self.k.nc.gpsimd.indirect_dma_start(
                out=self.uv[:, s % RING, :], out_offset=None, in_=self.table,
                in_offset=bass.IndirectOffsetOnAxis(ap=self.slots[:, t, j:j + 1], axis=0)).then_inc(self.landed[s % RING], 16)

    def vector(self, dve):
        k, nc = self.k, self.k.nc
        dve.wait_ge(self.rows_in, 16 * 2 * DEPTH)

        def ending(s):
            return next((i for i in range(len(VISITS)) if FIRST[i + 1] - 1 + LAG == s), None)

        for s in range(self.ticks):
            if s < self.n:
                t, j = self.at(s)
                x = k.x[:, t, :] if t < 2 else self.xs[:, :]
                grp = s // GROUP
                dve.wait_ge(self.landed[s % RING], 16 * (s // RING + 1))
                if s % GROUP == 0 and grp >= 2:
                    dve.wait_ge(self.gelued, grp - 1)
                ins = nc.vector.tensor_tensor_reduce(self.uv[:, s % RING, 0:D], self.uv[:, s % RING, 0:D], x, 1.0, 0.0, ALU.mult, ALU.add,
                                                     self.dot[:, grp % 2, s % GROUP:s % GROUP + 1])
                if s % GROUP == GROUP - 1:
                    ins.then_inc(self.dotted, 1)
            if s % GROUP == 0 and 0 < s <= self.n:
                grp = s // GROUP - 1
                t, j = self.at(s - GROUP)
                dve.wait_ge(self.gelued, grp + 1)
                if grp >= 2:
                    dve.wait_ge(self.spread, grp - 1)
                nc.vector.tensor_tensor(self.wgt[:, grp % 2, :], self.gelu[:, grp % 2, :], self.gate[:, t, j:j + GROUP], ALU.mult)\
                    .then_inc(self.weighed, 1)
            for later in range(3):
                i = ending(s - later)
                if i is None:
                    continue
                layer, t = VISITS[i]
                r = ROWS[t]
                z, stats = self.z[0:r, :], self.stats[0:r, :]
                if later == 0:
                    dve.wait_ge(self.used, FIRST[i + 1])
                    out = k.ps[0:r, 0:2, :].rearrange("p a b -> p (a b)")
                    nc.vector.scalar_tensor_tensor(z, k.x[0:r, t, :], ALPHA, out, ALU.mult, ALU.add).then_inc(self.sum_read, 1)
                    dve.wait_ge(self.sum_read, i + 1)
                    norm_first(k, z, stats, self.variance)
                elif later == 1:
                    dve.wait_ge(self.rooted, i + 1)
                    norm_second(k, z, stats)
                else:
                    norm_third(k, z, k.x[0:r, t, :], self.gb[0:r, layer, 0, :], self.gb[0:r, layer, 1, :])
                    nc.vector.memset(k.pad[:, :], 0.0).then_inc(self.normed, 1)
            yield

    def scalar(self, act):
        k, nc = self.k, self.k.nc
        for s in range(self.ticks):
            if s < self.n and s % GROUP == GROUP - 1:
                grp = s // GROUP
                act.wait_ge(self.dotted, grp + 1)
                if grp >= 2:
                    act.wait_ge(self.weighed, grp - 1)
                nc.scalar.activation(self.gelu[:, grp % 2, :], self.dot[:, grp % 2, :], ACT.Gelu).then_inc(self.gelued, 1)
            if s % GROUP == 0 and 0 < s <= self.n:
                grp = s // GROUP - 1
                act.wait_ge(self.weighed, grp + 1)
                for g in range(GROUP):
                    step = s - GROUP + g
                    if step >= RING:
                        act.wait_ge(self.used, step - RING + 1)
                    t, _ = self.at(step)
                    shape, w = ("ident", 128) if t < 2 else ("fold", NS)
                    last = nc.scalar.activation(self.diag[:, step % RING, 0:w], k.c(shape), ACT.Copy,
                                                scale=self.wgt[:, grp % 2, g:g + 1])
                last.then_inc(self.spread, 1)
            i = next((i for i in range(len(VISITS)) if FIRST[i + 1] - 1 + LAG == s), None)
            if i is not None:
                r = ROWS[VISITS[i][1]]
                act.wait_ge(self.variance, i + 1)
                nc.scalar.activation(self.stats[0:r, 15:16], self.stats[0:r, 14:15], ACT.Sqrt).then_inc(self.rooted, 1)
            yield

    def tensor(self, pe):
        k, nc = self.k, self.k.nc
        for tick in range(self.ticks):
            s = tick - LAG
            if 0 <= s < self.n:
                i = self.visit(s)
                t, j = self.at(s)
                m = ROWS[t]
                if s % GROUP == 0:
                    pe.wait_ge(self.spread, s // GROUP + 1)
                if j == 0 and i:
                    pe.wait_ge(self.sum_read, i)
                for c in range(2):
                    last = nc.tensor.matmul(k.bank(c)[0:m, :], self.diag[:, s % RING, 0:m], self.uv[:, s % RING, D + 512 * c:D + 512 * (c + 1)],
                                            start=(j == 0), stop=(j == STEPS[i] - 1), skip_group_check=True)
                last.then_inc(self.used, 1)
            yield

    def loads(self, sp):
        for layer in range(DEPTH):
            sp.dma_start(self.gb[:, layer, 0, :], self.gain[layer].partition_broadcast(128)).then_inc(self.rows_in, 16)
            sp.dma_start(self.gb[:, layer, 1, :], self.bias[layer].partition_broadcast(128)).then_inc(self.rows_in, 16)

    def stores(self, sp):
        y_prompt, y_sample = self.outs
        for i in range(len(ORDER)):
            t = ORDER[i]
            sp.wait_ge(self.normed, len(ORDER) + i + 1)
            dst = y_prompt[0, 128 * t:128 * (t + 1), :] if t < 2 else y_sample.rearrange("b t d -> (b t) d")
            self.k.store(sp, dst, self.k.x[0:ROWS[t], t, :])
        self.k.wait_for_stores(sp)


def side_ticks(k, stages, name, eng, ended, base):
    for n, stage in enumerate([Stage(k, 0)] + stages):
        yield from stage.run(name, eng)
        eng.drain().then_inc(ended, 1)
        yield
        eng.wait_ge(ended, 4 * (base + n + 1))
        yield


def experts_and_side_work(k, experts, windows):
    ended = k.sem("side_stage_ended")
    spans = []
    for i in range(len(VISITS)):
        a, b = FIRST[i], FIRST[i + 1] if i + 1 < len(VISITS) else experts.ticks
        spans.append((a, b))

    def both(name, eng):
        main = {"tensor": experts.tensor, "vector": experts.vector, "scalar": experts.scalar}[name](eng)
        base = 0
        for (a, b), (delay, stages) in zip(spans, windows):
            side = side_ticks(k, stages, name, eng, ended, base) if stages else iter(())
            total = sum(st.ticks + 2 for st in stages) + 2 if stages else 0
            base += len(stages) + 1 if stages else 0
            done = 0
            for n in range(b - a):
                next(main)
                share = total * max(0, n + 1 - delay) // (b - a - delay)
                while done < share:
                    next(side)
                    done += 1
            for _ in side:
                raise AssertionError("side work left over")
        for _ in main:
            raise AssertionError("steps left over")

    with k.nc.Block() as block:
        @block.gpsimd
        def _(pool):
            experts.pool(pool)

        @block.tensor
        def _(pe):
            both("tensor", pe)

        @block.vector
        def _(dve):
            both("vector", dve)

        @block.scalar
        def _(act):
            both("scalar", act)

        @block.sync
        def _(sp):
            experts.loads(sp)
            n = 0
            for _, stages in windows:
                if not stages:
                    continue
                for stage in [Stage(k, 0)] + stages:
                    if "sync" in stage.parts:
                        stage.parts["sync"](sp)
                    n += 1
                    sp.sem_inc(ended, 1)
                    sp.wait_ge(ended, 4 * n)
                    for sem in stage.sems:
                        sp.sem_clear(sem)
            experts.stores(sp)


def dilated_layer(k, name, tiles, a, o, val, kT):
    tok = slice(min(cols(t).start for t in tiles), max(cols(t).stop for t in tiles))
    stages = [transpose_x(k, name + "_x", tiles, SIDE_BANKS)]
    outer = ExitStack()
    catT = k.sbuf(name + "_catT", [128, KC, tok.stop], ctx=outer)
    with ExitStack() as ctx:
        qT = k.sbuf(name + "_qT", [128, HP, tok.stop], ctx=ctx)
        with ExitStack() as inner:
            qk = k.sbuf(name + "_qk", [128, len(tiles), 2 * D], ctx=inner)
            with ExitStack() as load:
                wbuf = k.sbuf(name + "_w", [128, 2, 4, 512], ctx=load)
                out = lambda j, t: qk[0:ROWS[t], tiles.index(t), 512 * j:512 * (j + 1)] if j < 4 else \
                    val[0:ROWS[t], t, 512 * (j - 4):512 * (j - 3)]
                stages.append(project_rows(k, name + "_in", a["odd_w_in"][0], [512] * 6, out, wbuf, tiles, SIDE_BANKS))
            with ExitStack() as rot:
                tmp = k.sbuf(name + "_tmp", [128, 4, 256], ctx=rot)
                stages.append(rotate_and_store(k, name + "_rot", qk, val, tiles, o["dil_p"], o["dil_s"], tmp))
            groups = []
            for n, t in enumerate(tiles):
                for dst, at in ((qT, 0), (kT, D)):
                    for c in range(0, HP, 4):
                        groups.append(([qk[0:ROWS[t], n, at + 128 * (c + j):at + 128 * (c + j + 1)] for j in range(4)],
                                       dst[:, c:c + 4, cols(t)]))
            stages.append(transposes(k, name + "_qk", groups, SIDE_BANKS))
        for t in tiles:
            if t == 2:
                for q4 in range(HEADS // 4):
                    with ExitStack() as inner:
                        stages += dilated_sample(k, f"{name}_s{q4}", q4, a["cache_dil_kv"], qT, kT, val, catT, inner, SIDE_BANKS,
                                                 (2, 4), (6,), 7)
            else:
                with ExitStack() as inner:
                    bufs = attention_buffers(k, f"{name}_p{t}", 512 * (t + 1), 512, inner)
                    stages.append(dilated_prompt(k, f"{name}_p{t}", t, qT, kT, val, catT, bufs, (2, 4), (6,), 7))
    with ExitStack() as inner:
        w = k.sbuf(name + "_w_out", [128, 2, 2, D], ctx=inner)
        gb = k.sbuf(name + "_gb", [128, 2, D], ctx=inner)
        z, stats = k.sbuf(name + "_z", [128, D], ctx=inner), k.sbuf(name + "_stats", [128, 16], ctx=inner)
        w_v = a["odd_w_out"][0].rearrange("(c p) n -> p c n", p=128)
        stages.append(project_out_and_norm(k, name + "_out", catT, lambda i, dst: [(dst, w_v[:, 2 * i:2 * i + 2, :])], a["ln_mix_g"][1],
                                           a["ln_mix_b"][1], w, gb, z, stats, tiles, SIDE_BANKS))
    outer.close()
    stages.append(transpose_x(k, name + "_y", tiles, SIDE_BANKS))
    return stages, tok


def build(nc, a, o):
    with ExitStack() as whole:
        k = Core(nc, whole)
        k.pad = k.sbuf("progress", [128, 1])
        k.level_masks = a["level_masks"]
        load_inputs(k, a["x_prompt"], a["x_sample"], a["const"])
        alone(k, transpose_x(k, "x0"))
        with ExitStack() as ctx:
            catT = k.sbuf("catT", [128, KC, NTOK], ctx=ctx)
            with ExitStack() as inner:
                h = k.sbuf("h", [128, TILES, EVEN_ROWS], ctx=inner)
                w_in = a["even_w_in"][0]
                widths = [512, 512, 512, 512, 280]
                with ExitStack() as load:
                    wbuf = k.sbuf("even_w", [128, 6, 4, 512], ctx=load)
                    out = lambda j, t: h[0:ROWS[t], t, 512 * j:512 * j + widths[j]]
                    alone(k, project_rows(k, "even", w_in[:, 1024:], widths, out, wbuf))
                with ExitStack() as hg:
                    cat = k.sbuf("cat", [128, TILES, 512], ctx=hg)
                    hT = k.sbuf("hT", [128, 8, NTOK], ctx=hg)
                    with ExitStack() as load:
                        wbuf = k.sbuf("even_wT", [128, 4, 8, 256], ctx=load)
                        alone(k, project_cols(k, "even_T", w_in, 1024, hT, wbuf))
                    recurrence(k, h, hT, cat, a["hg_gamma"], a["hg_norm_g"][0], a["state_hgrn"], o["state_prompt"], o["state_sample"])
                    alone(k, transposes(k, "cat", [([cat[0:r, t, 128 * c:128 * (c + 1)] for c in range(4)], catT[:, 0:4, cols(t)])
                                                   for t, r in enumerate(ROWS)]))
                sparse_attention(k, h, catT, a["page_table"], a["cache_cmp_kv"], a["cache_slc_kv"], a["cache_win_kv"], a["nsa_cmp_pe"],
                                 [o[n] for n in ("cmp_p", "cmp_s", "slc_p", "slc_s", "win_p", "win_s")])
            w_out = a["even_w_out"][0]

            def even_piece(i, dst):
                if i < 2:
                    return [(dst, w_out[256 * i:256 * (i + 1)].rearrange("(c p) n -> p c n", p=128))]
                return [(dst[64 * kv:64 * kv + 64], w_out[512 + 256 * kv + 128 * (i - 2):512 + 256 * kv + 128 * (i - 1)]
                         .rearrange("(g d) n -> d g n", d=HD)) for kv in range(KV)]

            w = k.sbuf("even_w_out", [128, 4, 2, D], ctx=ctx)
            gb = k.sbuf("even_gb", [128, 2, D], ctx=ctx)
            z, stats = k.sbuf("even_z", [128, D], ctx=ctx), k.sbuf("even_stats", [128, 16], ctx=ctx)
            alone(k, project_out_and_norm(k, "even_out", catT, even_piece, a["ln_mix_g"][0], a["ln_mix_b"][0], w, gb, z, stats))
        alone(k, transpose_x(k, "x1"))
        k.fresh_semaphores()
        with ExitStack() as ctx:
            slots = k.sbuf("slots", [128, TILES, SLOTS], U32, ctx)
            gate = k.sbuf("gate", [128, TILES, SLOTS], ctx=ctx)
            xs = k.sbuf("xs", [128, D], ctx=ctx)
            experts = Experts(k, a["experts"], slots, gate, xs, a["ln_ffn_g"], a["ln_ffn_b"], (o["y_prompt"], o["y_sample"]), ctx)
            r = lambda layer, t, qT, keysT, inner, routed=experts.routed: route(
                k, f"route{layer}{t}", layer, t, qT, keysT, slots[:, t], gate[:, t], xs, inner, 2, routed)
            with ExitStack() as first:
                qT = k.sbuf("peer_qT", [128, 2 * PH, NTOK], ctx=first)
                keysT = k.sbuf("peer_keysT", [128, 2 * PH, NK], ctx=first)
                with ExitStack() as load:
                    wbuf = k.sbuf("peer_w", [128, 2, 8, 256], ctx=load)
                    alone(k, project_cols(k, "peer_q", a["peer_w_q"][0], 2 * PH * 128, qT, wbuf))
                with ExitStack() as load:
                    keys = k.sbuf("peer_keys", [128, 2 * PH, 128], ctx=load)
                    alone(k, turn_keys(k, "peer_keys", a["peer_sub_keys"][0], keys, keysT, ALL_BANKS))
                with ExitStack() as inner:
                    alone(k, r(0, 2, qT, keysT, inner, None))
                k.side = True
                with ExitStack() as inner:
                    window0 = [r(0, 0, qT, keysT, inner)]
                with ExitStack() as inner:
                    window1 = [r(0, 1, qT, keysT, inner)]
            with ExitStack() as second:
                val = k.sbuf("dil_val", [128, TILES, D], ctx=second)
                kT = k.sbuf("dil_kT", [128, HP, NTOK], ctx=second)

                window2, tok = dilated_layer(k, "first", (2, 0), a, o, val, kT)
                with ExitStack() as late:
                    qT = k.sbuf("peer1_qT", [128, 2 * PH, NTOK], ctx=late)
                    keysT = k.sbuf("peer1_keysT", [128, 2 * PH, NK], ctx=late)
                    with ExitStack() as load:
                        keys = k.sbuf("peer1_keys", [128, 2 * PH, 128], ctx=load)
                        window2.append(turn_keys(k, "peer1_keys", a["peer_sub_keys"][1], keys, keysT, SIDE_BANKS))
                    with ExitStack() as load:
                        wbuf = k.sbuf("peer1_w", [128, 1, 8, 256], ctx=load)
                        window2.append(project_cols(k, "peer1_qa", a["peer_w_q"][1], 2 * PH * 128, qT, wbuf, tok, SIDE_BANKS))
                    with ExitStack() as inner:
                        window2.append(r(1, 2, qT, keysT, inner))
                    with ExitStack() as inner:
                        window3 = [r(1, 0, qT, keysT, inner)]
                window4, tok = dilated_layer(k, "second", (1,), a, o, val, kT)
                with ExitStack() as late:
                    qT = k.sbuf("peer2_qT", [128, 2 * PH, NTOK], ctx=late)
                    keysT = k.sbuf("peer2_keysT", [128, 2 * PH, NK], ctx=late)
                    with ExitStack() as load:
                        keys = k.sbuf("peer2_keys", [128, 2 * PH, 128], ctx=load)
                        window4.append(turn_keys(k, "peer2_keys", a["peer_sub_keys"][1], keys, keysT, SIDE_BANKS))
                    with ExitStack() as load:
                        wbuf = k.sbuf("peer2_w", [128, 1, 8, 256], ctx=load)
                        window4.append(project_cols(k, "peer1_qb", a["peer_w_q"][1], 2 * PH * 128, qT, wbuf, tok, SIDE_BANKS))
                    with ExitStack() as inner:
                        window4.append(r(1, 1, qT, keysT, inner))
            k.side = False
            experts_and_side_work(k, experts, [(0, window0), (0, window1), (8, window2), (0, window3), (0, window4), (0, [])])


_OUTS = [("y_prompt", (1, SEQ, D)), ("y_sample", (DEC_B, DEC_T, D)), ("state_prompt", (1, 1, HG, 64, 64)),
         ("state_sample", (1, DEC_B, HG, 64, 64))]
for _n in ("cmp", "slc", "win"):
    _OUTS += [(_n + "_p", (1, 1, SEQ, 2, KV, HD)), (_n + "_s", (1, DEC_B, DEC_T, 2, KV, HD))]
_OUTS += [("dil_p", (1, 1, SEQ, 2, HEADS, HD)), ("dil_s", (1, DEC_B, DEC_T, 2, HEADS, HD))]


def kernel(**inputs):
    import numpy as _np
    import concourse.bacc as _bacc
    from concourse import mybir as _mybir
    from concourse.bass_utils import run_bass_kernel_spmd as _run

    nc = _bacc.Bacc("TRN2", target_bir_lowering=False, num_devices=1)
    given = {n: _np.ascontiguousarray(x) for n, x in inputs.items() if n not in ("peer_u", "peer_v")}
    u, v = _np.asarray(inputs["peer_u"]), _np.asarray(inputs["peer_v"])
    given["experts"] = _np.concatenate([u, v], axis=2).reshape(DEPTH * EXPERTS, 2 * D)
    given["const"], given["level_masks"] = CONST, LEVEL_MASKS
    arrays = {f"in_{n}_dram": x for n, x in given.items()}
    a = {n: nc.dram_tensor(f"in_{n}_dram", x.shape, _mybir.dt.from_np(x.dtype), kind="ExternalInput").ap() for n, x in given.items()}
    o = {n: nc.dram_tensor(f"out_{n}_dram", shape, F32, kind="ExternalOutput").ap() for n, shape in _OUTS}
    build(nc, a, o)
    r = _run(nc, [arrays], core_ids=[0])
    return tuple(r.results[0][f"out_{n}_dram"] for n, _ in _OUTS)
```

```python
from contextlib import ExitStack

import numpy as np

import concourse.bass as bass
from concourse import mybir

F32 = mybir.dt.float32
U32 = mybir.dt.uint32
I32 = mybir.dt.int32
ALU = mybir.AluOpType
ACT = mybir.ActivationFunctionType
AX = mybir.AxisListType.X

D = 1024
KC = D // 128
SEQ = 256
DEC_B, DEC_T = 8, 4
NS = DEC_B * DEC_T
PAST = 256
PAGE = 128
NPG = PAST // PAGE
NTOK = SEQ + NS
ROWS = (128, 128, NS)
TILES = len(ROWS)
DEPTH = 2
ALPHA = float((2 * DEPTH) ** 0.25)
LN_EPS, RMS_EPS, TINY = 1e-5, 1e-6, 1e-30
HD = 64
SCALE = HD ** -0.5
HG = 8
KV, GR = 2, 4
NBLK = PAST // 32
MASKED = -1e30
LEAST = -1e28
HEADS = 16
HP = HEADS // 2
DIL = ((128, 1), (512, 4), (2048, 16))
PH, PK, NK = 8, 16, 128
EXPERTS = NK * NK
SLOTS = PH * PK
RING = 8
GROUP = 2
LAG = 3
LEVELS = (1, 2, 4, 8, 16, 32, 64)

V0, G0, Q0, CMP0, SLC0, WIN0, GATE0, EVEN_ROWS = 0, 512, 1024, 1536, 1792, 2048, 2304, 2328


def shape_constants():
    half = HD // 2
    inv = np.float32(10000.0) ** (-np.arange(half, dtype=np.float32) / np.float32(half))
    cos = np.zeros((128, TILES, half), np.float32)
    sin = np.zeros((128, TILES, half), np.float32)
    for t in range(TILES):
        pos = np.arange(128) + 128 * t if t < 2 else PAST + np.arange(128) % DEC_T
        ang = pos.astype(np.float32)[:, None] * inv[None, :].astype(np.float32)
        cos[:, t], sin[:, t] = np.cos(ang.astype(np.float64)), np.sin(ang.astype(np.float64))

    def reach(qpos, kpos):
        dist = qpos[:, None] - kpos[None, :]
        count = np.zeros(dist.shape, np.float32)
        for window, dil in DIL:
            count += (dist >= 0) & (dist <= window // dil * dil) & (dist % dil == 0)
        return (dist >= 0), count

    p = np.arange(128)
    causal = np.zeros((128, 2, SEQ), np.float32)
    dil_mask = np.zeros((128, 2, SEQ), np.float32)
    dil_count = np.zeros((128, 2, SEQ), np.float32)
    cmp_mask = np.zeros((128, 2, NBLK), np.float32)
    for t in range(2):
        seen, count = reach(p + 128 * t, np.arange(SEQ))
        causal[:, t] = np.where(seen, 0, MASKED)
        dil_mask[:, t] = np.where(count > 0, 0, MASKED)
        dil_count[:, t] = count
        cmp_mask[:, t] = np.where((np.arange(NBLK) + 1)[None] * 32 - 1 <= (p + 128 * t)[:, None], 0, MASKED)
    tok = p % NS
    seen, count = reach(PAST + tok % DEC_T, np.concatenate([np.arange(PAST), PAST + np.arange(NS) % DEC_T]))
    own = np.concatenate([np.ones((128, PAST), bool), tok[:, None] // DEC_T == np.arange(NS)[None] // DEC_T], 1)
    new_causal = np.where(seen & own, 0, MASKED).astype(np.float32)
    new_mask = np.where((count > 0) & own, 0, MASKED).astype(np.float32)
    new_count = np.where(own, count, 0).astype(np.float32)
    batch_cols = np.broadcast_to((np.arange(NS)[None] // DEC_T == np.arange(DEC_B)[:, None]), (128, DEC_B, NS))
    batch_rows = tok[:, None] // DEC_T == np.arange(DEC_B)[None]
    pool = np.zeros((128, NPG, NBLK), np.float32)
    for t in range(NPG):
        pool[p, t, 4 * t + p // 32] = 1 / 32
    fold = tok[:, None] == np.arange(NS)[None]
    parts = dict(
        ident=np.eye(128), cos=cos, sin=sin, causal=causal, dil_mask=dil_mask, dil_count=dil_count,
        cmp_mask=cmp_mask, new_causal=new_causal, new_mask=new_mask, new_count=new_count,
        batch_cols=batch_cols, batch_rows=batch_rows, pool=pool, mean32=np.full((128, NBLK), 1 / 32), fold=fold,
        iota16=np.broadcast_to(np.arange(PK), (128, PK)), row=p[:, None],
    )
    at, cols = {}, []
    for name, a in parts.items():
        a = np.asarray(a, np.float32)
        n = sum(c.shape[1] for c in cols)
        at[name] = (n, a.shape[1:])
        cols.append(a.reshape(128, -1))
    s, t = p[:, None], p[None, :]
    levels = [s == t] + [(s // (2 * m) == t // (2 * m)) & (s // m % 2 == 0) & (t // m % 2 == 1) for m in LEVELS]
    return np.concatenate(cols, 1), at, np.stack(levels, 1).astype(np.uint32)


CONST, CONST_AT, LEVEL_MASKS = shape_constants()


class Steps:

    def __init__(self, k, eng, name):
        self.sem, self.eng, self.n = k.sem(name), eng, 0

    def __call__(self, ins):
        self.n += 1
        ins.then_inc(self.sem, 1)
        self.eng.wait_ge(self.sem, self.n)


class Core:

    def __init__(self, nc, ctx):
        self.nc, self.ctx, self.serial, self.stage_sems = nc, ctx, 0, []
        self.stored, self.n_stored = nc.alloc_semaphore("stored"), 0
        self.side, self.side_set, self.side_sems, self.side_taken = False, 0, {}, []
        self.dve_steps = Steps(self, nc.vector, "dve_steps")
        self.x = self.sbuf("x", [128, TILES, D])
        self.xT = self.sbuf("xT", [128, KC, NTOK])
        self.const = self.sbuf("const", list(CONST.shape))
        self.ps = ctx.enter_context(nc.psum_tensor("ps", [128, 8, 512], F32))

    def sem(self, name, role=None):
        if self.side and role:
            key = (role, self.side_set)
            if key not in self.side_sems:
                self.side_sems[key] = self.nc.alloc_semaphore(f"side{self.side_set}_{role}")
                self.stage_sems.append(self.side_sems[key])
            self.side_taken.append(self.side_sems[key])
            return self.side_sems[key]
        name = f"{name}_{role}" if role else name
        self.serial += 1
        self.stage_sems.append(self.nc.alloc_semaphore(f"{name}_{self.serial}"))
        return self.stage_sems[-1]

    def store(self, sp, dst, src):
        self.n_stored += 1
        sp.dma_start(dst, src).then_inc(self.stored, 16)

    def wait_for_stores(self, sp):
        sp.wait_ge(self.stored, 16 * self.n_stored)

    def take_side_sems(self):
        taken, self.side_taken = self.side_taken, []
        if self.side:
            self.side_set = 1 - self.side_set
        return taken

    def fresh_semaphores(self):
        self.nc.clear_and_free_semaphores(self.stage_sems)
        self.stage_sems = []
        self.nc.all_engine_barrier()
        self.dve_steps.n = 0
        self.dve_steps.sem = self.sem("dve_steps")

    def sbuf(self, name, shape, dt=F32, ctx=None):
        self.serial += 1
        return (ctx or self.ctx).enter_context(self.nc.sbuf_tensor(f"{name}_{self.serial}", shape, dt))

    def c(self, name):
        n, shape = CONST_AT[name]
        size = int(np.prod(shape))
        flat = self.const[:, n:n + size]
        if len(shape) == 2:
            return flat.rearrange("p (a b) -> p a b", b=shape[1])
        return flat

    def bank(self, b):
        return self.ps[:, b, :]


def bc(ap, axis, n):
    ap = ap.unsqueeze(axis)
    shape = list(ap.shape)
    shape[axis] = n
    return ap.broadcast_to(shape)


COL0 = (NS, NS + 128, 0)
SMP = slice(0, NS)


def cols(t):
    return slice(COL0[t], COL0[t] + ROWS[t])




def load_inputs(k, x_prompt, x_sample, const):
    nc = k.nc
    loaded = k.sem("loaded")
    with nc.Block() as block:
        @block.sync
        def _(sp):
            sp.dma_start(k.const[:, :], const).then_inc(loaded, 16)
            sp.dma_start(k.x[:, 0:2, :], x_prompt.rearrange("o (t p) d -> p (o t) d", p=128)).then_inc(loaded, 16)
            sp.dma_start(k.x[0:NS, 2, :], x_sample.rearrange("b t d -> (b t) d")).then_inc(loaded, 16)
            sp.wait_ge(loaded, 48)


class Stage:

    def __init__(self, k, ticks, weight=1.0):
        self.ticks, self.parts, self.sems = ticks, {}, k.take_side_sems()
        self.weights = [weight] * ticks

    def on(self, engine):
        def keep(part):
            self.parts[engine] = part
        return keep

    def run(self, name, eng):
        count = 0
        if name in self.parts:
            for _ in self.parts[name](eng):
                count += 1
                yield
            assert count == self.ticks, (count, self.ticks)
        else:
            for _ in range(self.ticks):
                yield


def alone(k, *stages, scalar=None, following=()):
    with k.nc.Block() as block:
        @block.tensor
        def _(pe):
            for stage in stages:
                for _ in stage.run("tensor", pe):
                    pass

        @block.vector
        def _(dve):
            for stage in stages:
                for _ in stage.run("vector", dve):
                    pass

        @block.scalar
        def _(act):
            for stage in scalar or stages:
                for _ in stage.run("scalar", act):
                    pass

        @block.gpsimd
        def _(pool):
            for stage in stages:
                if "gpsimd" in stage.parts:
                    stage.parts["gpsimd"](pool)

        @block.sync
        def _(sp):
            for part in ("early loads", "sync"):
                for stage in stages:
                    if part in stage.parts:
                        stage.parts[part](sp)
            for stage in following:
                stage.parts.pop("early loads")(sp)


ALL_BANKS = tuple(range(8))
SIDE_BANKS = tuple(range(2, 8))


def transposes(k, name, groups, banks=ALL_BANKS, loads=(), early=False):
    nc, nb = k.nc, len(banks)
    turned, v_out, s_out, loaded = [k.sem(name, n) for n in ("turned", "v_out", "s_out", "loaded")]
    ident = k.c("ident")
    stage = Stage(k, len(groups) + 1, 1.5)
    sizes = [(srcs[0].shape[0], int(np.prod(srcs[0].shape[1:]))) for srcs, _ in groups]
    outs = ((v_out, nc.vector.tensor_copy), (s_out, nc.scalar.copy))

    def out_view(i):
        (rows, width), (srcs, dst) = sizes[i], groups[i]
        flat = k.bank(banks[i % nb])[0:width, 0:rows * len(srcs)]
        if len(dst.shape) == 3:
            return flat.rearrange("p (a b) -> p a b", b=dst.shape[2])
        return flat

    @stage.on("early loads" if early else "sync")
    def _(sp):
        for dst, src in loads:
            sp.dma_start(dst, src).then_inc(loaded, 16)

    @stage.on("tensor")
    def _(pe):
        if loads:
            pe.wait_ge(loaded, 16 * len(loads))
        for i, (srcs, dst) in enumerate(groups):
            rows, width = sizes[i]
            j = i - nb
            if j >= 0:
                pe.wait_ge((v_out, s_out)[j % 2], j // 2 + 1)
            for n, src in enumerate(srcs):
                last = nc.tensor.transpose(k.bank(banks[i % nb])[0:width, n * rows:(n + 1) * rows], src, ident[0:rows, 0:rows])
            last.then_inc(turned, 1)
            yield
        yield

    def take_out(eng, side):
        done, copy = outs[side]
        yield
        for i in range(len(groups)):
            if i % 2 == side:
                eng.wait_ge(turned, i + 1)
                copy(groups[i][1], out_view(i)).then_inc(done, 1)
            yield

    stage.on("vector")(lambda dve: take_out(dve, 0))
    stage.on("scalar")(lambda act: take_out(act, 1))
    return stage


def transpose_x(k, name, tiles=(0, 1, 2), banks=ALL_BANKS):
    groups = []
    for t in tiles:
        for c in range(0, KC, 4):
            groups.append(([k.x[0:ROWS[t], t, (c + j) * 128:(c + j + 1) * 128] for j in range(4)],
                           k.xT[:, c:c + 4, cols(t)]))
    return transposes(k, name, groups, banks)


def project_rows(k, name, w, widths, out, wbuf, tiles=(0, 1, 2), banks=ALL_BANKS):
    nc, nb, slots = k.nc, len(banks), wbuf.shape[1]
    starts = [sum(widths[:i]) for i in range(len(widths))]
    w_v = w.rearrange("(c p) n -> p c n", p=128)
    landed = [k.sem(name, f"w_landed{i}") for i in range(slots)]
    half_done, product, v_out, s_out = [k.sem(name, n) for n in ("half_done", "product", "v_out", "s_out")]
    n_t = len(tiles)
    loads = [(j, half) for j in range(len(widths)) for half in range(2)]
    jobs = [(j, t) for j in range(len(widths)) for t in tiles]
    ticks = []
    for j in range(len(widths)):
        for half in range(2):
            for t in tiles:
                ticks += [[("multiply", j, half, t, sub)] for sub in range(2)]
        for t in tiles:
            ticks[-1].append(("leave", jobs.index((j, t))))
    stage = Stage(k, len(ticks), 1.0)

    def load(sp, i):
        j, half = loads[i]
        sp.dma_start(wbuf[:, i % slots, :, 0:widths[j]], w_v[:, 4 * half:4 * half + 4, starts[j]:starts[j] + widths[j]])\
          .then_inc(landed[i % slots], 16)

    @stage.on("early loads")
    def _(sp):
        for i in range(slots):
            load(sp, i)

    @stage.on("sync")
    def _(sp):
        for i in range(slots, len(loads)):
            sp.wait_ge(half_done, n_t * (i - slots + 1))
            load(sp, i)

    @stage.on("tensor")
    def _(pe):
        for tick in ticks:
            for what, *rest in tick:
                if what == "multiply":
                    j, half, t, sub = rest
                    i, load = jobs.index((j, t)), 2 * j + half
                    if sub == 0:
                        pe.wait_ge(landed[load % slots], 16 * (load // slots + 1))
                        if half == 0 and i >= nb:
                            pe.wait_ge((v_out, s_out)[(i - nb) % 2], (i - nb) // 2 + 1)
                    for c in (2 * sub, 2 * sub + 1):
                        last = nc.tensor.matmul(k.bank(banks[i % nb])[0:ROWS[t], 0:widths[j]], k.xT[:, 4 * half + c, cols(t)],
                                                wbuf[:, load % slots, c, 0:widths[j]],
                                                start=(half == 0 and c == 0), stop=(half == 1 and c == 3))
                    if sub == 1:
                        last.then_inc(half_done, 1)
            yield

    def take_out(eng, side, done, copy):
        for tick in ticks:
            for what, *rest in tick:
                if what == "leave" and rest[0] % 2 == side:
                    i = rest[0]
                    j, t = jobs[i]
                    eng.wait_ge(half_done, 2 * n_t * j + n_t + i % n_t + 1)
                    copy(out(j, t), k.bank(banks[i % nb])[0:ROWS[t], 0:widths[j]]).then_inc(done, 1)
            yield

    stage.on("vector")(lambda dve: take_out(dve, 0, v_out, nc.vector.tensor_copy))
    stage.on("scalar")(lambda act: take_out(act, 1, s_out, nc.scalar.copy))
    return stage


def project_cols(k, name, w, n, outT, wbuf, tok=slice(0, NTOK), banks=ALL_BANKS, by=("vector", "scalar")):
    nc, nb, slots = k.nc, len(banks), wbuf.shape[1]
    w_v = w.rearrange("(c p) n -> p c n", p=128)
    n_tok = tok.stop - tok.start
    landed = [k.sem(name, f"w_landed{i}") for i in range(slots)]
    product = k.sem(name, "product")
    outs = [k.sem(name, {"vector": "v_out", "scalar": "s_out"}[engine]) for engine in by]
    n_cols, n_by = n // 128, len(by)
    stage = Stage(k, 2 * n_cols + 1, 0.7 + n_tok / 256)

    def load(sp, j):
        sp.dma_start(wbuf[:, j % slots, :, :], w_v[:, :, 256 * j:256 * (j + 1)]).then_inc(landed[j % slots], 16)

    @stage.on("early loads")
    def _(sp):
        for j in range(slots):
            load(sp, j)

    @stage.on("sync")
    def _(sp):
        for j in range(slots, n // 256):
            sp.wait_ge(product, 2 * (j - slots + 1))
            load(sp, j)

    @stage.on("tensor")
    def _(pe):
        for i in range(n_cols):
            j = i // 2
            if i % 2 == 0:
                pe.wait_ge(landed[j % slots], 16 * (j // slots + 1))
            if i >= nb:
                pe.wait_ge(outs[(i - nb) % n_by], (i - nb) // n_by + 1)
            for c in range(KC):
                last = nc.tensor.matmul(k.bank(banks[i % nb])[:, 0:n_tok], wbuf[:, j % slots, c, 128 * (i % 2):128 * (i % 2 + 1)],
                                        k.xT[:, c, tok], start=(c == 0), stop=(c == KC - 1))
                if c == KC // 2 - 1:
                    yield
            last.then_inc(product, 1)
            yield
        yield

    def take_out(eng, side, done, copy):
        for _ in range(2):
            yield
        for i in range(n_cols):
            if i % n_by == side:
                eng.wait_ge(product, i + 1)
                copy(outT[:, i, tok], k.bank(banks[i % nb])[:, 0:n_tok]).then_inc(done, 1)
            yield
            if i < n_cols - 1:
                yield

    copies = {"vector": nc.vector.tensor_copy, "scalar": nc.scalar.copy}
    for side, engine in enumerate(by):
        stage.on(engine)(lambda eng, side=side, engine=engine: take_out(eng, side, outs[side], copies[engine]))
    return stage


def norm_first(k, z, stats, variance):
    nc, step = k.nc, k.dve_steps
    for h in range(2):
        step(nc.vector.bn_stats(stats[:, 6 * h:6 * h + 6], z[:, 512 * h:512 * (h + 1)]))
    step(nc.vector.bn_aggr(stats[:, 12:14], stats[:, 0:12]))
    nc.vector.tensor_scalar(stats[:, 14:15], stats[:, 13:14], LN_EPS, None, ALU.add).then_inc(variance, 1)


def norm_second(k, z, stats):
    nc, step = k.nc, k.dve_steps
    step(nc.vector.reciprocal(stats[:, 15:16], stats[:, 15:16]))
    step(nc.vector.tensor_scalar(z, z, stats[:, 12:13], stats[:, 15:16], ALU.subtract, ALU.mult))


def norm_third(k, z, out, gain, bias):
    nc, step = k.nc, k.dve_steps
    step(nc.vector.tensor_tensor(z, z, gain, ALU.mult))
    step(nc.vector.tensor_tensor(out, z, bias, ALU.add))


def project_out_and_norm(k, name, catT, w_piece, gain, bias, w, gb, z, stats, tiles=(0, 1, 2), banks=ALL_BANKS):
    nc, slots = k.nc, w.shape[1]
    landed = [k.sem(name, f"w_landed{i}") for i in range(slots)]
    row_landed, used, variance, rooted = [k.sem(name, n) for n in ("rows_landed", "w_used", "variance", "rooted")]
    n_t, pieces = len(tiles), KC // 2
    per = [len(w_piece(i, w[:, 0])) for i in range(pieces)]
    stage = Stage(k, pieces * n_t * 2 + 3 * n_t, 1.2)
    stage.weights[pieces * n_t * 2:] = [3.5] * (3 * n_t)

    by_tile = slots >= pieces
    order = [(i, n) for n in range(n_t) for i in range(pieces)] if by_tile else [(i, n) for i in range(pieces) for n in range(n_t)]

    def bank(n, h):
        return k.bank(banks[2 * n + h])

    def load(sp, i):
        for dst, src in w_piece(i, w[:, i % slots]):
            sp.dma_start(dst, src).then_inc(landed[i % slots], 16)

    @stage.on("early loads")
    def _(sp):
        for i in range(slots):
            load(sp, i)

    @stage.on("sync")
    def _(sp):
        sp.dma_start(gb[:, 0, :], gain.partition_broadcast(128)).then_inc(row_landed, 16)
        sp.dma_start(gb[:, 1, :], bias.partition_broadcast(128)).then_inc(row_landed, 16)
        for i in range(slots, pieces):
            sp.wait_ge(used, i - slots + 1)
            load(sp, i)

    @stage.on("tensor")
    def _(pe):
        for i, n in order:
            t = tiles[n]
            if n == 0:
                pe.wait_ge(landed[i % slots], 16 * sum(per[j] for j in range(i % slots, i + 1, slots)))
            for h in range(2):
                for c in range(2):
                    last = nc.tensor.matmul(bank(n, h)[0:ROWS[t], :], catT[:, 2 * i + c, cols(t)],
                                            w[:, i % slots, c, 512 * h:512 * (h + 1)],
                                            start=(i == 0 and c == 0), stop=(i == pieces - 1 and c == 1))
                if h == 1 and (by_tile or n == n_t - 1):
                    last.then_inc(used, 1)
                yield
        for _ in range(3 * n_t):
            yield

    @stage.on("vector")
    def _(dve):
        for _ in range(pieces * n_t * 2):
            yield
        dve.wait_ge(row_landed, 32)
        for n, t in enumerate(tiles):
            dve.wait_ge(used, pieces * (n + 1) if by_tile else pieces)
            r = ROWS[t]
            b = banks[2 * n]
            mixed = k.ps[0:r, b:b + 2, :].rearrange("p a b -> p (a b)")
            k.dve_steps(nc.vector.scalar_tensor_tensor(z[0:r, :], k.x[0:r, t, :], ALPHA, mixed, ALU.mult, ALU.add))
            norm_first(k, z[0:r, :], stats[0:r, :], variance)
            yield
            dve.wait_ge(rooted, n + 1)
            norm_second(k, z[0:r, :], stats[0:r, :])
            yield
            norm_third(k, z[0:r, :], k.x[0:r, t, :], gb[0:r, 0, :], gb[0:r, 1, :])
            yield

    @stage.on("scalar")
    def _(act):
        for _ in range(pieces * n_t * 2):
            yield
        for n, t in enumerate(tiles):
            act.wait_ge(variance, n + 1)
            nc.scalar.activation(stats[0:ROWS[t], 15:16], stats[0:ROWS[t], 14:15], ACT.Sqrt).then_inc(rooted, 1)
            for _ in range(3):
                yield
    return stage


def rotate(k, src, dst, tile_rows, heads, tmp):
    nc, step = k.nc, k.dve_steps
    t, r = tile_rows
    half = HD // 2
    cos, sin = bc(k.c("cos")[0:r, t, :], 1, heads), bc(k.c("sin")[0:r, t, :], 1, heads)
    s = src.rearrange("p (h d) -> p h d", d=HD)
    d = dst.rearrange("p (h d) -> p h d", d=HD)
    a, b, c, e = [tmp[0:r, i, 0:heads * half].rearrange("p (h d) -> p h d", d=half) for i in range(4)]
    nc.vector.tensor_tensor(a, s[:, :, 0:half], cos, ALU.mult)
    nc.vector.tensor_tensor(b, s[:, :, half:HD], sin, ALU.mult)
    nc.vector.tensor_tensor(c, s[:, :, 0:half], sin, ALU.mult)
    step(nc.vector.tensor_tensor(e, s[:, :, half:HD], cos, ALU.mult))
    nc.vector.tensor_tensor(d[:, :, 0:half], a, b, ALU.subtract)
    step(nc.vector.tensor_tensor(d[:, :, half:HD], c, e, ALU.add))




def attention(k, name, items, bufs, pairs=(0, 2), turn_banks=(4, 5)):
    nc, step = k.nc, k.dve_steps
    n_items = len(items)
    prob, probT, small = bufs
    scored, masked, expd, ready, turned, copied, summed, left = [
        k.sem(name, s) for s in ("scored", "masked", "expd", "ready", "turned", "copied", "summed", "left")]
    n_tb = len(turn_banks)
    rounds = [(i, j) for i, it in enumerate(items) for j in range(len(it["parts"]))]
    rounds_of = {i: [r for r, (ii, _) in enumerate(rounds) if ii == i] for i in range(n_items)}
    leaving = [i for i, it in enumerate(items) if it["leave"]]

    ticks = []

    def scores(i):
        if i < n_items:
            count = len(items[i]["scores"])
            for at in range(0, count, 3):
                ticks.append([("scores", i, at, min(at + 3, count))])

    def mask_and_exp(i):
        if i < n_items:
            ticks.append([("mask", i), ("exp", i)])

    for i in range(2):
        scores(i)
        mask_and_exp(i)
    for i in range(n_items):
        ticks.append([("normalise", i)])
        scores(i + 2)
        ticks.append([("turn", rounds_of[i][0]), ("copy", rounds_of[i][0])])
        mask_and_exp(i + 2)
        for r in rounds_of[i]:
            count = len(items[i]["parts"][rounds[r][1]][2])
            for at in range(0, count, 8):
                ticks.append([("values", r, at, min(at + 8, count))])
                if at == 0 and r != rounds_of[i][-1]:
                    ticks[-1] = [("turn", r + 1), ("copy", r + 1)] + ticks[-1]
        ticks.append([("leave", i)])
    stage = Stage(k, len(ticks), 1.0)

    def view(i):
        it = items[i]
        return prob[0:it["rows"], i % 3, 0:it["groups"] * it["n"]].rearrange("p (g n) -> p g n", n=it["n"])

    def score_bank(i):
        b = pairs[i % 2]
        return k.ps[:, b:b + 2, :].rearrange("p a b -> p (a b)")

    def top(i):
        return small[0:items[i]["rows"], 0, i % 3, 0:items[i]["groups"]]

    def low(i):
        return small[0:items[i]["rows"], 1, i % 3, 0:items[i]["groups"]]

    def den(i):
        return small[0:items[i]["rows"], 2, i % 3, 0:items[i]["groups"]]

    def inv(i):
        return small[0:items[i]["rows"], 3, i % 3, 0:items[i]["groups"]]

    @stage.on("tensor")
    def _(pe):
        def scores(i, a, b):
            if a == 0 and i >= 2:
                pe.wait_ge(masked, i - 1)
            for p0, pn, c0, cn, lhsT, rhs, start, stop in items[i]["scores"][a:b]:
                last = nc.tensor.matmul(score_bank(i)[p0:p0 + pn, c0:c0 + cn], lhsT, rhs, start=start, stop=stop)
            if b == len(items[i]["scores"]):
                last.then_inc(scored, 1)

        def turn(r):
            i, j = rounds[r]
            it = items[i]
            pe.wait_ge(ready, i + 1)
            if r >= n_tb:
                pe.wait_ge(copied, r - n_tb + 1)
            k0, kn, _ = it["parts"][j]
            for g in range(it["groups"]):
                last = nc.tensor.transpose(k.bank(turn_banks[r % n_tb])[0:kn, g * 128:g * 128 + it["rows"]],
                                           view(i)[:, g, k0:k0 + kn], k.c("ident")[0:it["rows"], 0:it["rows"]])
            last.then_inc(turned, 1)

        def values(r, a, b):
            i, j = rounds[r]
            k0, kn, mms = items[i]["parts"][j]
            if a == 0:
                pe.wait_ge(copied, r + 1)
                before = sum(1 for n in leaving if n < i)
                if j == 0 and before:
                    pe.wait_ge(left, before)
            for out, lhsT, pick, start, stop in mms[a:b]:
                last = nc.tensor.matmul(out, lhsT, pick(probT[0:kn, r % 2, :]), start=start, stop=stop, skip_group_check=True)
            if b == len(mms):
                last.then_inc(summed, 1)

        for tick in ticks:
            for what, *rest in tick:
                if what == "scores":
                    scores(*rest)
                elif what == "turn":
                    turn(*rest)
                elif what == "values":
                    values(*rest)
            yield

    @stage.on("vector")
    def _(dve):
        def mask_and_top(i):
            it = items[i]
            g, n, r = it["groups"], it["n"], it["rows"]
            dve.wait_ge(scored, i + 1)
            if i >= 3:
                dve.wait_ge(turned, rounds_of[i - 3][-1] + 1)
            apart = it.get("apart", n)
            sc = score_bank(i)[0:r, 0:g * apart].rearrange("p (g n) -> p g n", n=apart)[:, :, 0:n]
            if it["mask"] is None:
                step(nc.vector.tensor_copy(view(i), sc))
            else:
                step(nc.vector.tensor_tensor(view(i), sc, bc(it["mask"], 1, g), ALU.add))
            step(nc.vector.tensor_reduce(top(i), view(i), AX, ALU.max))
            nc.vector.tensor_scalar(low(i), top(i), LEAST, -SCALE, ALU.max, ALU.mult).then_inc(masked, 1)

        def normalise(i):
            it = items[i]
            g, n = it["groups"], it["n"]
            dve.wait_ge(expd, i + 1)
            if it["count"] is not None:
                step(nc.vector.tensor_tensor(view(i), view(i), bc(it["count"], 1, g), ALU.mult))
                step(nc.vector.tensor_reduce(den(i), view(i), AX, ALU.add))
            step(nc.vector.tensor_scalar(den(i), den(i), TINY, None, ALU.max))
            step(nc.vector.reciprocal(inv(i), den(i)))
            if it["gate"] is not None:
                step(nc.vector.tensor_tensor(inv(i), inv(i), it["gate"], ALU.mult))
            nc.vector.tensor_tensor(view(i), view(i), bc(inv(i), 2, n), ALU.mult).then_inc(ready, 1)

        for tick in ticks:
            for what, *rest in tick:
                if what == "mask":
                    mask_and_top(*rest)
                elif what == "normalise":
                    normalise(*rest)
                elif what == "leave" and rest[0] in leaving:
                    i = rest[0]
                    dve.wait_ge(summed, rounds_of[i][-1] + 1)
                    for dst, src in items[i]["leave"]:
                        last = nc.vector.tensor_copy(dst, src)
                    last.then_inc(left, 1)
            yield

    @stage.on("scalar")
    def _(act):
        def exps(i):
            act.wait_ge(masked, i + 1)
            for g in range(items[i]["groups"]):
                one = view(i)[:, g, :]
                total = {} if items[i]["count"] is not None else dict(accum_out=den(i)[:, g:g + 1])
                last = nc.scalar.activation(one, one, ACT.Exp, bias=low(i)[:, g:g + 1], scale=SCALE, **total)
            last.then_inc(expd, 1)

        def copy(r):
            i, j = rounds[r]
            it = items[i]
            kn, w = it["parts"][j][1], (it["groups"] - 1) * 128 + it["rows"]
            act.wait_ge(turned, r + 1)
            if r >= 2:
                act.wait_ge(summed, r - 1)
            nc.scalar.copy(probT[0:kn, r % 2, 0:w], k.bank(turn_banks[r % n_tb])[0:kn, 0:w]).then_inc(copied, 1)

        for tick in ticks:
            for what, *rest in tick:
                if what == "exp":
                    exps(*rest)
                elif what == "copy":
                    copy(*rest)
            yield
    return stage


def attention_buffers(k, name, width, turned, ctx, items=3):
    return (k.sbuf(name + "_prob", [128, items, width], ctx=ctx), k.sbuf(name + "_probT", [128, 2, turned], ctx=ctx),
            k.sbuf(name + "_small", [128, 4, 3, 4], ctx=ctx))




class StateInputs:

    def __init__(self, k, ctx):
        self.masks = k.sbuf("level_masks", [128, len(LEVELS) + 1, 128], U32, ctx)
        self.gamma = k.sbuf("hg_gamma", [12, 128], ctx=ctx)
        self.state = k.sbuf("hg_state", [128, HG // 2, DEC_B, HD], ctx=ctx)
        self.landed, self.loads = k.sem("state_inputs_landed"), 2 + HG // 2

    def load(self, k, sp, gamma, state):
        sp.dma_start(self.gamma[:, :], gamma.rearrange("r (c p) -> (r c) p", p=128)).then_inc(self.landed, 16)
        sp.dma_start(self.masks[:, :, :], k.level_masks).then_inc(self.landed, 16)
        for c in range(HG // 2):
            sp.dma_start(self.state[:, c, :, :], state[0, :, 2 * c:2 * c + 2].rearrange("b h k v -> (h k) b v")).then_inc(self.landed, 16)


def recurrence(k, h, hT, cat, inputs, fin, new, norm_g, state_prompt, state_sample):
    nc, step = k.nc, k.dve_steps
    C4 = 4
    pT = hT[:, 0:C4, :]
    fT = hT[:, C4:2 * C4, :]
    s = {n: k.sem("hg_" + n) for n in (
        "gamma_turned", "bounds_diff", "bounds_exp", "sigmoid", "cross_product", "spread", "state_product", "out_product",
        "state_ready", "squares", "root", "gates")}
    products, factors = [[k.sem(f"hg_{n}_tile{t}") for t in range(TILES)] for n in ("products", "factors")]
    with ExitStack() as ctx:
        masks, s0 = inputs.masks, inputs.state
        key = k.sbuf("hg_key", [128, C4, NTOK], ctx=ctx)
        tot = [k.sbuf("hg_tot", [128, C4, NTOK], ctx=ctx) for _ in range(2)]
        sg = k.sbuf("hg_sigmoid", [128, 2 * C4, NTOK], ctx=ctx)
        att = k.sbuf("hg_att", [128, 2, HG, 128], ctx=ctx)
        cross = k.sbuf("hg_cross", [128, HG, 128], ctx=ctx)
        att_s = k.sbuf("hg_att_s", [NS, HG, NS], ctx=ctx)
        small = k.sbuf("hg_small", [128, 48], ctx=ctx)
        q_b = k.sbuf("hg_q_b", [128, C4, DEC_B, NS], ctx=ctx)
        keyT = k.sbuf("hg_keyT", [128, TILES, 512], ctx=ctx)
        v_b = k.sbuf("hg_v_b", [NS, 2, DEC_B, HD], ctx=ctx)

        with nc.Block() as block:
            @block.tensor
            def _(pe):
                pe.wait_ge(inputs.landed, 16 * inputs.loads)
                nc.tensor.transpose(k.bank(0)[:, 0:12], inputs.gamma[:, :], k.c("ident")[0:12, 0:12]).then_inc(s["gamma_turned"], 1)

            @block.scalar
            def _(act):
                nc.scalar.activation(sg[:, :, :], hT[:, :, :], ACT.Sigmoid).then_inc(s["sigmoid"], 1)
                act.wait_ge(s["bounds_diff"], 1)
                nc.scalar.activation(small[:, 16:28], small[:, 16:28], ACT.Exp).then_inc(s["bounds_exp"], 1)

            @block.vector
            def _(dve):
                dve.wait_ge(s["gamma_turned"], 1)
                step(nc.vector.tensor_copy(small[:, 0:12], k.bank(0)[:, 0:12]))
                step(nc.vector.tensor_tensor(small[:, 12:16], small[:, 0:4], small[:, 4:8], ALU.max))
                step(nc.vector.tensor_tensor(small[:, 12:16], small[:, 12:16], small[:, 8:12], ALU.max))
                nc.vector.tensor_tensor(small[:, 16:28].rearrange("p (r c) -> p r c", c=4),
                                        small[:, 0:12].rearrange("p (r c) -> p r c", c=4),
                                        bc(small[:, 12:16], 1, 3), ALU.subtract).then_inc(s["bounds_diff"], 1)
                dve.wait_ge(s["bounds_exp"], 1)
                step(nc.vector.tensor_tensor(small[:, 28:32], small[:, 16:20], small[:, 20:24], ALU.add))
                step(nc.vector.tensor_tensor(small[:, 28:32], small[:, 28:32], small[:, 24:28], ALU.add))
                step(nc.vector.reciprocal(small[:, 28:32], small[:, 28:32]))
                step(nc.vector.tensor_tensor(small[:, 32:36], small[:, 16:20], small[:, 28:32], ALU.mult))
                step(nc.vector.tensor_scalar(small[:, 36:40], small[:, 32:36], -1.0, 1.0, ALU.mult, ALU.add))
                dve.wait_ge(s["sigmoid"], 1)
                nc.vector.tensor_tensor(pT, pT, sg[:, 0:C4, :], ALU.mult)
                for c in range(C4):
                    step(nc.vector.tensor_scalar(fT[:, c, :], sg[:, C4 + c, :], small[:, 36 + c:37 + c],
                                                 small[:, 32 + c:33 + c], ALU.mult, ALU.add))
                nc.vector.tensor_scalar(key[:, :, :], fT, -1.0, 1.0, ALU.mult, ALU.add)
                nc.vector.memset(att[:, :, :, :], 0.0)
                nc.vector.memset(att_s[:, :, :], 0.0)
                step(nc.vector.tensor_copy(tot[0][:, :, :], fT))

        s_levels = 3
        lanes = lambda n: (0, 1, 2) if n < s_levels else (0, 1)
        with nc.Block() as block:
            @block.tensor
            def _(pe):
                for n in range(len(LEVELS) + 1):
                    for t in lanes(n):
                        if n:
                            pe.wait_ge(factors[t], n)
                        for hd in range(HG):
                            p = slice(64 * (hd % 2), 64 * (hd % 2) + 64)
                            dst = k.bank(2 * t + hd % 2)[0:ROWS[t], (hd // 2) * ROWS[t]:(hd // 2 + 1) * ROWS[t]]
                            last = nc.tensor.matmul(dst, key[p, hd // 2, cols(t)], pT[p, hd // 2, cols(t)], start=True, stop=True,
                                                    skip_group_check=True)
                        last.then_inc(products[t], 1)
                for t in range(2):
                    pe.wait_ge(factors[t], len(LEVELS) + 1)
                for hd in range(HG):
                    p = slice(64 * (hd % 2), 64 * (hd % 2) + 64)
                    last = nc.tensor.matmul(k.bank(6 + hd % 2)[:, (hd // 2) * 128:(hd // 2 + 1) * 128], key[p, hd // 2, cols(0)],
                                            pT[p, hd // 2, cols(1)], start=True, stop=True, skip_group_check=True)
                last.then_inc(s["cross_product"], 1)

            @block.vector
            def _(dve):
                def halves(x, a, b, m):
                    v = x[:, :, a:b].rearrange("p c (n z m) -> p c n z m", z=2, m=m)
                    return v[:, :, :, 0, :], v[:, :, :, 1, :]

                for n in range(len(LEVELS) + 1):
                    for t in lanes(n):
                        dve.wait_ge(products[t], n + 1)
                        if t < 2:
                            src = k.ps[:, 2 * t:2 * t + 2, :].rearrange("p a (b t) -> p (a b) t", t=128)
                            nc.vector.copy_predicated(att[:, t, :, :], bc(masks[:, n, :], 1, HG), src)
                        else:
                            for odd in range(2):
                                nc.vector.copy_predicated(att_s[:, C4 * odd:C4 * (odd + 1), :], bc(masks[0:NS, n, 0:NS], 1, C4),
                                                          k.bank(4 + odd)[0:NS, 0:C4 * NS].rearrange("p (h t) -> p h t", t=NS))
                        a, b = cols(t).start, cols(t).stop
                        if n == 0:
                            nc.vector.tensor_tensor(pT[:, :, a:b], pT[:, :, a:b], fT[:, :, a:b], ALU.mult).then_inc(factors[t], 1)
                            continue
                        m = LEVELS[n - 1]
                        old, nxt = tot[(n - 1) % 2], tot[n % 2]
                        cnt = (b - a) // (2 * m)
                        o = old[:, :, a:a + 2 * cnt].rearrange("p c (n z) -> p c n z", z=2)
                        k1, _ = halves(key, a, b, m)
                        _, q2 = halves(pT, a, b, m)
                        nc.vector.tensor_tensor(q2, q2, bc(o[:, :, :, 0], 3, m), ALU.mult)
                        nc.vector.tensor_tensor(k1, k1, bc(o[:, :, :, 1], 3, m), ALU.mult)
                        nc.vector.tensor_tensor(nxt[:, :, a:a + cnt], o[:, :, :, 0], o[:, :, :, 1], ALU.mult).then_inc(factors[t], 1)
                dve.wait_ge(s["cross_product"], 1)
                step(nc.vector.tensor_copy(cross[:, :, :], k.ps[:, 6:8, :].rearrange("p a (b t) -> p (a b) t", t=128)))
                tN = tot[len(LEVELS) % 2]
                step(nc.vector.tensor_tensor(key[:, :, cols(0)], key[:, :, cols(0)],
                                             tN[:, :, COL0[1]:COL0[1] + 1].broadcast_to([128, C4, 128]), ALU.mult))
                for c in range(C4):
                    last = nc.vector.tensor_tensor(q_b[:, c, :, :], bc(pT[:, c, SMP], 1, DEC_B), k.c("batch_cols"), ALU.mult)
                step(last)
        sample_totals = tot[(s_levels - 1) % 2]

        alone(k, transposes(k, "hg_keys", [
            ([key[:, c, cols(t)] for c in range(C4)], keyT[0:ROWS[t], t, :].rearrange("p (c x) -> p c x", x=128))
            for t in range(TILES)]))

        with nc.Block() as block:
            @block.vector
            def _(dve):
                for hd in range(HG):
                    if hd >= 2:
                        dve.wait_ge(s["state_product"], hd - 1)
                    vs = h[0:NS, 2, V0 + HD * hd:V0 + HD * (hd + 1)]
                    nc.vector.tensor_tensor(v_b[:, hd % 2, :, :], bc(vs, 1, DEC_B),
                                            bc(k.c("batch_rows")[0:NS, :], 2, HD), ALU.mult).then_inc(s["spread"], 1)
                dve.wait_ge(s["out_product"], 1)
                step(nc.vector.tensor_copy(fin[:, :, :], k.bank(3)[:, 256:512].rearrange("p (c v) -> p c v", v=HD)))
                dve.wait_ge(s["state_product"], HG)
                for c in range(C4):
                    step(nc.vector.tensor_tensor(new[:, c], s0[:, c], bc(sample_totals[:, c, 0:DEC_B], 2, HD), ALU.mult))
                    step(nc.vector.tensor_tensor(new[:, c], new[:, c], k.bank(4 + c).rearrange("p (b v) -> p b v", v=HD), ALU.add))
                nc.vector.memset(k.pad[:, :], 0.0).then_inc(s["state_ready"], 1)

            @block.tensor
            def _(pe):
                mm = lambda *a, **b: nc.tensor.matmul(*a, skip_group_check=True, **b)
                for hd in range(HG):
                    odd, c = hd % 2, hd // 2
                    p = slice(64 * odd, 64 * odd + 64)
                    hv = slice(V0 + HD * hd, V0 + HD * (hd + 1))
                    hk = slice(HD * hd, HD * (hd + 1))
                    place = C4 * odd + c
                    at = slice(HD * place, HD * (place + 1))
                    o = [k.bank(t)[0:ROWS[t], at] for t in range(TILES)]
                    mm(o[0], att[:, 0, place, :], h[:, 0, hv], start=True, stop=True)
                    mm(o[1], att[:, 1, place, :], h[:, 1, hv], start=True, stop=False)
                    mm(o[1], cross[:, place, :], h[:, 0, hv], start=False, stop=True)
                    mm(o[2], att_s[:, place, :], h[0:NS, 2, hv], start=True, stop=bool(odd))
                    own = k.bank(3)[0:NS, HD * c:HD * (c + 1)] if odd else o[2]
                    for b in range(DEC_B):
                        mm(own, q_b[p, c, b, :], s0[p, c, b, :], start=bool(odd and b == 0), stop=(b == DEC_B - 1))
                    last_state = k.bank(3)[p, 256 + HD * c:256 + HD * (c + 1)]
                    mm(last_state, keyT[:, 0, hk], h[:, 0, hv], start=True, stop=False)
                    last = mm(last_state, keyT[:, 1, hk], h[:, 1, hv], start=False, stop=True)
                last.then_inc(s["out_product"], 1)
                for hd in range(HG):
                    pe.wait_ge(s["spread"], hd + 1)
                    p = slice(64 * (hd % 2), 64 * (hd % 2) + 64)
                    mm(k.bank(4 + hd // 2)[p, :], keyT[0:NS, 2, HD * hd:HD * (hd + 1)],
                       v_b[:, hd % 2].rearrange("p b v -> p (b v)"), start=True, stop=True).then_inc(s["state_product"], 1)

            @block.sync
            def _(sp):
                sp.wait_ge(s["state_ready"], 1)
                k.store(sp, state_prompt[0, 0].rearrange("(c e) k v -> (e k) c v", e=2), fin[:, :, :])
                for c in range(C4):
                    dst = state_sample[0, :, 2 * c:2 * c + 2].rearrange("b h k v -> (h k) b v")
                    k.store(sp, dst, new[:, c])

    with ExitStack() as ctx:
        o = k.sbuf("hg_o", [128, TILES, 512], ctx=ctx)
        sq = k.sbuf("hg_sq", [128, TILES, 512], ctx=ctx)
        sgate = k.sbuf("hg_sgate", [128, TILES, 512], ctx=ctx)
        ms = k.sbuf("hg_ms", [128, TILES, 16], ctx=ctx)
        g = k.sbuf("hg_norm_g", [128, 512], ctx=ctx)
        row = k.sem("hg_row")
        block = ctx.enter_context(nc.Block())

        @block.sync
        def _(sp):
            sp.dma_start(g[:, :], norm_g.partition_broadcast(128)).then_inc(row, 16)

        @block.scalar
        def _(act):
            for t, r in enumerate(ROWS):
                nc.scalar.activation(sgate[0:r, t, :], h[0:r, t, G0:G0 + 512], ACT.Sigmoid).then_inc(s["gates"], 1)
            for t, r in enumerate(ROWS):
                act.wait_ge(s["squares"], t + 1)
                nc.scalar.activation(ms[0:r, t, 8:16], ms[0:r, t, 0:8], ACT.Sqrt).then_inc(s["root"], 1)

        @block.vector
        def _(dve):
            v = nc.vector
            per_head = lambda x: x.rearrange("p (h v) -> p h v", v=HD)

            def each(op):
                for t, r in enumerate(ROWS):
                    last = op(t, r, o[0:r, t, :], sq[0:r, t, :], ms[0:r, t, 0:8], ms[0:r, t, 8:16])
                step(last)

            for odd in range(2):
                back = lambda x, odd=odd: x.rearrange("p (c e v) -> p c e v", e=2, v=HD)[:, :, odd, :]
                each(lambda t, r, o, sq, m, root: v.tensor_copy(
                    back(o), k.bank(t)[0:r, 256 * odd:256 * (odd + 1)].rearrange("p (c v) -> p c v", v=HD)))
            own = back(o[0:NS, 2, :])
            step(v.tensor_tensor(own, own, k.bank(3)[0:NS, 0:256].rearrange("p (c v) -> p c v", v=HD), ALU.add))
            each(lambda t, r, o, sq, m, root: v.tensor_tensor(sq, o, o, ALU.mult))
            each(lambda t, r, o, sq, m, root: v.tensor_reduce(m, per_head(sq), AX, ALU.add))
            for t, r in enumerate(ROWS):
                v.tensor_scalar(ms[0:r, t, 0:8], ms[0:r, t, 0:8], 1.0 / HD, RMS_EPS, ALU.mult, ALU.add).then_inc(s["squares"], 1)
            dve.wait_ge(s["gates"], TILES)
            each(lambda t, r, o, sq, m, root: v.tensor_tensor(sq, h[0:r, t, G0:G0 + 512], sgate[0:r, t, :], ALU.mult))
            dve.wait_ge(s["root"], TILES)
            each(lambda t, r, o, sq, m, root: v.reciprocal(root, root))
            each(lambda t, r, o, sq, m, root: v.tensor_tensor(per_head(o), per_head(o), bc(root, 2, HD), ALU.mult))
            dve.wait_ge(row, 16)
            each(lambda t, r, o, sq, m, root: v.tensor_tensor(o, o, g[0:r, :], ALU.mult))
            each(lambda t, r, o, sq, m, root: v.tensor_tensor(cat[0:r, t, :], o, sq, ALU.mult))




class SparseCaches:

    def __init__(self, k, ctx):
        self.rows = {n: k.sbuf("cache_" + n, [128, DEC_B, NPG, 256], ctx=ctx) for n in ("cmp", "slc", "win")}
        self.pages = k.sbuf("pages", [128, DEC_B * NPG], I32, ctx)
        self.pages_f = k.sbuf("pages_f", [128, DEC_B * NPG], ctx=ctx)
        self.index = k.sbuf("page_rows", [128, DEC_B * NPG], U32, ctx)
        self.pe = k.sbuf("cmp_pe", [32, 128], ctx=ctx)
        self.pages_in, self.index_ready, self.gathered, self.loaded = [
            k.sem(n) for n in ("pages_in", "page_rows_ready", "pages_gathered", "window_cache_in")]

    def stage(self, k, state_inputs, a):
        stage = Stage(k, 1)
        nc, step = k.nc, k.dve_steps

        @stage.on("early loads")
        def _(sp):
            sp.dma_start(self.pages[:, :], a["page_table"].rearrange("b n -> (b n)").partition_broadcast(128)).then_inc(self.pages_in, 16)

        @stage.on("sync")
        def _(sp):
            state_inputs.load(k, sp, a["hg_gamma"], a["state_hgrn"])
            sp.dma_start(self.pe[:, :], a["nsa_cmp_pe"][0].rearrange("r h d -> r (h d)")).then_inc(self.loaded, 16)
            for b in range(DEC_B):
                sp.dma_start(self.rows["win"][:, b], a["cache_win_kv"][0, b].rearrange("(n p) x h d -> p n (x h d)", p=128))\
                  .then_inc(self.loaded, 16)

        @stage.on("vector")
        def _(dve):
            dve.wait_ge(self.pages_in, 16)
            step(nc.vector.tensor_copy(self.pages_f[:, :], self.pages[:, :]))
            step(nc.vector.tensor_scalar(self.pages_f[:, :], self.pages_f[:, :], float(PAGE), k.c("row"), ALU.mult, ALU.add))
            nc.vector.tensor_copy(self.index[:, :], self.pages_f[:, :]).then_inc(self.index_ready, 1)
            yield

        @stage.on("gpsimd")
        def _(pool):
            pool.wait_ge(self.index_ready, 1)
            for n in ("cmp", "slc"):
                rows = a[f"cache_{n}_kv"][0].rearrange("n p x h d -> (n p) (x h d)")
                for j in range(DEC_B * NPG):
                    nc.gpsimd.indirect_dma_start(out=self.rows[n][:, j // NPG, j % NPG, :], out_offset=None, in_=rows,
                                                 in_offset=bass.IndirectOffsetOnAxis(ap=self.index[:, j:j + 1], axis=0))\
                      .then_inc(self.gathered, 16)
        return stage

    def wait(self, eng):
        eng.wait_ge(self.gathered, 16 * 2 * DEC_B * NPG)
        eng.wait_ge(self.loaded, 16 * (1 + DEC_B))


def sparse_attention(k, h, catT, caches, outs):
    nc, step = k.nc, k.dve_steps
    (cmp_p, cmp_s, slc_p, slc_s, win_p, win_s) = outs
    with ExitStack() as outer:
        qn = k.sbuf("qn", [128, TILES, 512], ctx=outer)
        qr = k.sbuf("qr", [128, TILES, 512], ctx=outer)
        gates = k.sbuf("gates", [128, TILES, 24], ctx=outer)
        gates_s = k.sbuf("gates_s", [128, 6], ctx=outer)
        qT = {n: k.sbuf("q_T" + n, [128, GR, NTOK], ctx=outer) for n in ("nope", "rope")}
        kT = {n: k.sbuf("kT_" + n, [128, NTOK], ctx=outer) for n in ("slc", "win")}
        cache, pe_sb = caches.rows, caches.pe
        kTs = {n: k.sbuf("kTs_" + n, [128, DEC_B, PAST], ctx=outer) for n in ("slc", "win")}
        q_b = {n: k.sbuf("q_b" + n, [128, DEC_B, GR, NS], ctx=outer) for n in ("nope", "rope")}
        q_new = k.sbuf("q_new", [128, GR, NS], ctx=outer)
        kc = k.sbuf("kc", [128, 1 + DEC_B, NBLK], ctx=outer)
        vc = k.sbuf("vc", [NBLK, 1 + DEC_B, 128], ctx=outer)
        tmp = k.sbuf("rot_tmp", [128, 4, 256], ctx=outer)
        gate_done, rotated, regrouped = k.sem("gates_ready"), k.sem("rotated"), k.sem("regrouped")

        with nc.Block() as block:
            @block.sync
            def _(sp):
                sp.wait_ge(rotated, 1)
                for at, prompt, sample in ((CMP0, cmp_p, cmp_s), (SLC0, slc_p, slc_s), (WIN0, win_p, win_s)):
                    k.store(sp, prompt[0, 0].rearrange("(t p) x h d -> p t (x h d)", p=128), h[:, 0:2, at:at + 256])
                    k.store(sp, sample[0].rearrange("b t x h d -> (b t) (x h d)"), h[0:NS, 2, at:at + 256])
                caches.wait(sp)

            @block.scalar
            def _(act):
                for t, r in enumerate(ROWS):
                    src = h[0:r, t, Q0:Q0 + 512].rearrange("p (kv g d) -> p g kv d", kv=KV, g=GR)
                    dst = qn[0:r, t, :].rearrange("p (g kv d) -> p g kv d", kv=KV, g=GR)
                    nc.scalar.copy(dst, src).then_inc(regrouped, 1)
                for t, r in enumerate(ROWS):
                    nc.scalar.activation(gates[0:r, t, :], h[0:r, t, GATE0:GATE0 + 24], ACT.Sigmoid).then_inc(gate_done, 1)

            @block.vector
            def _(dve):
                for t, r in enumerate(ROWS):
                    dve.wait_ge(regrouped, t + 1)
                    rotate(k, qn[0:r, t, :], qr[0:r, t, :], (t, r), 8, tmp)
                    for at in (SLC0, WIN0):
                        rotate(k, h[0:r, t, at:at + 128], h[0:r, t, at:at + 128], (t, r), KV, tmp)
                nc.vector.memset(k.pad[:, :], 0.0).then_inc(rotated, 1)
                dve.wait_ge(gate_done, TILES)
                for g in range(GR):
                    src = gates[0:NS, 2, :].rearrange("p (a g) -> p a g", g=GR)[:, :, g]
                    last = nc.vector.tensor_copy(gates_s[NS * g:NS * (g + 1), :], src)
                step(last)

        groups = []
        for t, r in enumerate(ROWS):
            for n, x in (("nope", qn), ("rope", qr)):
                groups.append(([x[0:r, t, 128 * g:128 * (g + 1)] for g in range(GR)], qT[n][:, :, cols(t)]))
            for n, at in (("slc", SLC0), ("win", WIN0)):
                groups.append(([h[0:r, t, at:at + 128]], kT[n][:, cols(t)]))
        for n in ("slc", "win"):
            for b in range(0, DEC_B, 2):
                groups.append(([cache[n][:, b + j // NPG, j % NPG, 0:128] for j in range(2 * NPG)],
                               kTs[n][:, b:b + 2, :].rearrange("p b s -> p (b s)")))
        alone(k, transposes(k, "nsa", groups))

        pooled = k.sem("pooled")
        with nc.Block() as block:
            @block.sync
            def _(sp):
                k.wait_for_stores(sp)

            @block.tensor
            def _(pe):
                pool, mean = k.c("pool"), k.c("mean32")
                mm = lambda *a, **b: nc.tensor.matmul(*a, skip_group_check=True, **b)
                for i in range(1 + DEC_B):
                    raw = (lambda t: h[:, t, CMP0:CMP0 + 256]) if i == 0 else (lambda t, b=i - 1: cache["cmp"][:, b, t, :])
                    kk, vv = k.bank(0)[:, NBLK * i:NBLK * (i + 1)], k.bank(1 + i // 4)[0:NBLK, 128 * (i % 4):128 * (i % 4 + 1)]
                    for t in range(NPG):
                        mm(kk, raw(t)[:, 0:128], pool[:, t, :], start=(t == 0), stop=False)
                        mm(vv, pool[:, t, :], raw(t)[:, 128:256], start=(t == 0), stop=(t == NPG - 1))
                    last = mm(kk, pe_sb[:, :], mean[0:32, :], start=False, stop=True)
                last.then_inc(pooled, 1)

            @block.vector
            def _(dve):
                for n in ("nope", "rope"):
                    for g in range(GR):
                        last = nc.vector.tensor_tensor(q_b[n][:, :, g, :], bc(qT[n][:, g, SMP], 1, DEC_B), k.c("batch_cols"), ALU.mult)
                nc.vector.tensor_copy(q_new[:, :, :], qT["rope"][:, :, SMP])
                dve.wait_ge(pooled, 1)
                nc.vector.tensor_copy(kc[:, :, :], k.bank(0)[:, 0:NBLK * (1 + DEC_B)].rearrange("p (i c) -> p i c", c=NBLK))
                step(nc.vector.tensor_copy(vc[:, :, :].rearrange("p i d -> p (i d)"),
                                           k.ps[0:NBLK, 1:4, :].rearrange("p a b -> p (a b)")[:, 0:128 * (1 + DEC_B)]))

        items = []
        for t in range(2):
            bank = 6 + t
            out = k.bank(bank).rearrange("p (g q) -> p g q", q=128)
            for br, n in ((1, "slc"), (2, "win"), (0, "cmp")):
                for kv in range(KV):
                    p = slice(64 * kv, 64 * kv + 64)
                    nk = NBLK if n == "cmp" else 128 * (t + 1)
                    q = qT["nope" if n == "cmp" else "rope"]
                    keys = kc[p, 0, :] if n == "cmp" else kT[n][p, NS:NS + nk]
                    base = {"cmp": CMP0, "slc": SLC0, "win": WIN0}[n] + 128
                    parts = []
                    for j in range(1 if n == "cmp" else t + 1):
                        val = vc[:, 0, p] if n == "cmp" else h[:, j, base + 64 * kv:base + 64 * kv + 64]
                        kn = NBLK if n == "cmp" else 128
                        parts.append((128 * j, kn, [(k.bank(bank)[p, :], val, lambda pT: pT,
                                                     n == "slc" and j == 0, n == "cmp")]))
                    gate = gates[:, t, :].rearrange("p (a k g) -> p a k g", a=3, k=KV)[:, br, kv, :]
                    leave = [(catT[:, 4:8, cols(t)], out)] if (n, kv) == ("cmp", KV - 1) else []
                    items.append(dict(
                        rows=128, groups=GR, n=nk, mask=k.c("cmp_mask")[:, t, :] if n == "cmp" else k.c("causal")[:, t, 0:nk],
                        scores=[(0, 128, g * nk, nk, q[p, g, cols(t)], keys, True, True) for g in range(GR)],
                        count=None, gate=gate, parts=parts, leave=leave))
        out = k.bank(6)[:, 0:GR * NS]
        for br, n in ((1, "slc"), (2, "win"), (0, "cmp")):
            for kv in range(KV):
                p = slice(64 * kv, 64 * kv + 64)
                nk = NBLK if n == "cmp" else PAST + NS
                qb = q_b["nope" if n == "cmp" else "rope"]
                keys = (lambda b: kc[p, 1 + b, :]) if n == "cmp" else (lambda b: kTs[n][p, b, :])
                width = NBLK if n == "cmp" else PAST
                scores = [(0, 128, 0, width, qb[p, b].rearrange("p g t -> p (g t)"), keys(b), b == 0, b == DEC_B - 1) for b in range(DEC_B)]
                own = lambda b: (lambda pT: pT[:, 0:128].rearrange("p (g t) -> p g t", t=NS)[:, :, DEC_T * b:DEC_T * (b + 1)])
                dst = lambda b: out[p, :].rearrange("p (g t) -> p g t", t=NS)[:, :, DEC_T * b:DEC_T * (b + 1)]
                base = {"cmp": CMP0, "slc": SLC0, "win": WIN0}[n] + 128 + 64 * kv
                if n == "cmp":
                    parts = [(0, NBLK, [(dst(b), vc[:, 1 + b, p], own(b), False, True) for b in range(DEC_B)])]
                else:
                    scores.append((0, 128, PAST, NS, q_new[p].rearrange("p g t -> p (g t)"), kT[n][p, SMP], True, True))
                    parts = [(PAST, NS, [(out[p, :], h[0:NS, 2, base:base + 64], lambda pT: pT[:, 0:128], n == "slc", False)])]
                    parts += [(128 * j, 128, [(dst(b), cache[n][:, b, j, 128 + 64 * kv:192 + 64 * kv], own(b), False, False)
                                              for b in range(DEC_B)]) for j in range(NPG)]
                leave = [(catT[:, 4:8, SMP], out.rearrange("p (g t) -> p g t", t=NS))] if (n, kv) == ("cmp", KV - 1) else []
                items.append(dict(rows=128, groups=1, n=nk, mask=None if n == "cmp" else k.c("new_causal"), scores=scores, count=None,
                                  gate=gates_s[:, KV * br + kv:KV * br + kv + 1], parts=parts, leave=leave))
        alone(k, attention(k, "nsa", items, attention_buffers(k, "nsa", 1024, 512, outer)))




def rotate_and_store(k, name, qk, val, tiles, out_p, out_s, tmp):
    nc = k.nc
    rotated = k.sem(name, "rotated")
    stage = Stage(k, 4 * len(tiles), 2.5)

    @stage.on("vector")
    def _(dve):
        for n, t in enumerate(tiles):
            r = ROWS[t]
            for at in (0, 512, 1024, 1536):
                rotate(k, qk[0:r, n, at:at + 512], qk[0:r, n, at:at + 512], (t, r), HEADS // 2, tmp)
                if at == 1536:
                    nc.vector.memset(k.pad[:, :], 0.0).then_inc(rotated, 1)
                yield

    @stage.on("sync")
    def _(sp):
        for n, t in enumerate(tiles):
            sp.wait_ge(rotated, n + 1)
            dst = out_s[0].rearrange("b t x h d -> (b t) x (h d)") if t == 2 else \
                out_p[0, 0, 128 * t:128 * (t + 1)].rearrange("p x h d -> p x (h d)")
            k.store(sp, dst[:, 0, :], qk[0:ROWS[t], n, D:2 * D])
            k.store(sp, dst[:, 1, :], val[0:ROWS[t], t, :])
        k.wait_for_stores(sp)
    return stage


def dilated_prompt(k, name, t, qT, kT, val, catT, bufs, pairs, turn_banks, out_bank):
    items = []
    nk = 128 * (t + 1)
    for q4 in range(HEADS // 4):
        head = [4 * q4 + g for g in (0, 2, 1, 3)]
        parts = []
        for j in range(t + 1):
            parts.append((128 * j, 128, [
                (k.bank(out_bank)[64 * (head[g] % 2):64 * (head[g] % 2) + 64, 128 * (g % 2):128 * (g % 2 + 1)],
                 val[:, j, HD * head[g]:HD * (head[g] + 1)], (lambda pT, g=g: pT[:, 128 * g:128 * (g + 1)]),
                 j == 0 and g % 2 == 0, j == t) for g in range(4)]))
        items.append(dict(
            rows=128, groups=4, n=nk, apart=SEQ, mask=k.c("dil_mask")[:, t, 0:nk], count=k.c("dil_count")[:, t, 0:nk], gate=None,
            scores=[(0, 128, g * SEQ, nk, qT[64 * (hd % 2):64 * (hd % 2) + 64, hd // 2, cols(t)],
                     kT[64 * (hd % 2):64 * (hd % 2) + 64, hd // 2, NS:NS + nk], True, True) for g, hd in enumerate(head)],
            parts=parts,
            leave=[(catT[:, 2 * q4:2 * q4 + 2, cols(t)], k.bank(out_bank)[:, 0:256].rearrange("p (c q) -> p c q", q=128))]))
    return attention(k, name, items, bufs, pairs, turn_banks)


def dilated_sample(k, name, q4, cache, qT, kT, val, catT, cached, ctx, banks, pairs, turn_banks, out_bank):
    nc = k.nc
    kTs = k.sbuf(name + "_kTs", [128, 2, DEC_B, PAST], ctx=ctx)
    q_b = k.sbuf(name + "_q_b", [128, 2, DEC_B, NS], ctx=ctx)
    bufs = attention_buffers(k, name, PAST + NS, 128, ctx, 1)
    kv = cached
    loads = [[(kv[:, x, b], cache[0, b, :, x, 4 * q4:4 * q4 + 4].rearrange("(n p) h d -> p n (h d)", p=128)) for b in range(DEC_B)]
             for x in range(2)]
    groups = []
    for c in range(2):
        for b in range(0, DEC_B, 2):
            groups.append(([kv[:, 0, b + j // NPG, j % NPG, 128 * c:128 * (c + 1)] for j in range(2 * NPG)],
                           kTs[:, c, b:b + 2, :].rearrange("p b s -> p (b s)")))
    turn_keys = transposes(k, name + "_k", groups, banks, loads[0], True)
    values_in = k.sem(name, "values_in")
    spread = Stage(k, 1)

    @spread.on("early loads")
    def _(sp):
        for dst, src in loads[1]:
            sp.dma_start(dst, src).then_inc(values_in, 16)

    @spread.on("vector")
    def _(dve):
        for c in range(2):
            last = nc.vector.tensor_tensor(q_b[:, c], bc(qT[:, 2 * q4 + c, SMP], 1, DEC_B), k.c("batch_cols"), ALU.mult)
        k.dve_steps(last)
        dve.wait_ge(values_in, 16 * DEC_B)
        yield
    scores, new, old = [], [], [[] for _ in range(NPG)]
    out = lambda g: k.bank(out_bank)[64 * (g % 2):64 * (g % 2) + 64, NS * (g // 2):NS * (g // 2 + 1)]
    for g in range(4):
        p = slice(64 * (g % 2), 64 * (g % 2) + 64)
        hd = 4 * q4 + g
        for b in range(DEC_B):
            scores.append((NS * g, NS, 0, PAST, q_b[p, g // 2, b, :], kTs[p, g // 2, b, :], b == 0, b == DEC_B - 1))
            for j in range(NPG):
                c0 = NS * g + DEC_T * b
                old[j].append((out(g)[:, DEC_T * b:DEC_T * (b + 1)], kv[:, 1, b, j, HD * g:HD * (g + 1)],
                               (lambda pT, c0=c0: pT[:, c0:c0 + DEC_T]), False, j == NPG - 1))
        scores.append((NS * g, NS, PAST, NS, qT[p, hd // 2, SMP], kT[p, hd // 2, SMP], True, True))
        new.append((out(g), val[0:NS, 2, HD * hd:HD * (hd + 1)],
                    (lambda pT, g=g: pT[:, NS * g:NS * (g + 1)]), g < 2, False))
    parts = [(PAST, NS, new)] + [(128 * j, 128, old[j]) for j in range(NPG)]
    item = dict(rows=128, groups=1, n=PAST + NS, mask=k.c("new_mask"), count=k.c("new_count"), gate=None, scores=scores, parts=parts,
                leave=[(catT[:, 2 * q4:2 * q4 + 2, SMP], k.bank(out_bank)[:, 0:2 * NS].rearrange("p (c q) -> p c q", q=NS))])
    return [turn_keys, spread, attention(k, name, [item], bufs, pairs, turn_banks)]




def turn_keys(k, name, sub_keys, keys, keysT, banks):
    return transposes(k, name, [([keys[:, 4 * i + j, :] for j in range(4)], keysT[:, 4 * i:4 * i + 4, :]) for i in range(4)],
                      banks, [(keys[:, :, :], sub_keys.rearrange("h c k d -> k (h c) d"))], True)


def route(k, name, layer, t, qT, keysT, slots, gate, xs, ctx, bank0, routed=None):
    nc, step = k.nc, k.dve_steps
    HC, r, v = 2 * PH, ROWS[t], k.nc.vector
    s = k.sbuf(name + "_s", [128, HC, NK], ctx=ctx)
    val = k.sbuf(name + "_val", [128, HC, PK], ctx=ctx)
    at = k.sbuf(name + "_at", [128, HC, PK], U32, ctx)
    atf = k.sbuf(name + "_atf", [128, HC, PK], ctx=ctx)
    top = k.sbuf(name + "_top", [128, PH, PK], ctx=ctx)
    sel = k.sbuf(name + "_sel", [128, PH, PK], U32, ctx)
    half = k.sbuf(name + "_half", [128, 2, PH, PK], U32, ctx)
    halff = k.sbuf(name + "_halff", [128, 2, PH, PK], ctx=ctx)
    ef = k.sbuf(name + "_ef", [128, 2, PH, PK], ctx=ctx)
    e = k.sbuf(name + "_e", [128, PH, PK], ctx=ctx)
    den = k.sbuf(name + "_den", [128, PH], ctx=ctx)
    scored, less, expd = k.sem(name, "scored"), k.sem(name, "less_top"), k.sem(name, "expd")
    cand = s[:, :, :].rearrange("p (h x) n -> p h (x n)", x=2)
    PIECE = 4
    SCORE_TICKS = 4
    EXP_TICK = SCORE_TICKS + 2 + 3 * (HC // PIECE) + 2 + 3 * (PH // PIECE) + 10
    TICKS = EXP_TICK + 3
    stage = Stage(k, TICKS, 1.0)

    @stage.on("tensor")
    def _(pe):
        for i in range(HC):
            last = nc.tensor.matmul(k.bank(bank0 + i // 4)[0:r, 128 * (i % 4):128 * (i % 4 + 1)], qT[:, i, cols(t)],
                                    keysT[:, i, :], start=True, stop=True, skip_group_check=True)
            if i == HC - 1:
                last.then_inc(scored, 1)
            if i % 4 == 3:
                yield
        for _ in range(TICKS - SCORE_TICKS):
            yield

    @stage.on("scalar")
    def _(act):
        for _ in range(EXP_TICK):
            yield
        act.wait_ge(less, 1)
        nc.scalar.activation(e[0:r], e[0:r], ACT.Exp).then_inc(expd, 1)
        for _ in range(TICKS - EXP_TICK):
            yield

    @stage.on("vector")
    def _(dve):
        count = 0
        for _ in range(SCORE_TICKS):
            count += 1
            yield
        dve.wait_ge(scored, 1)
        for b in range(0, 4, 2):
            step(v.tensor_copy(s[0:r, 4 * b:4 * b + 8].rearrange("p a b -> p (a b)"),
                               k.ps[0:r, bank0 + b:bank0 + b + 2, :].rearrange("p a b -> p (a b)")))
            count += 1
            yield

        def sixteen_best(x, best, where, n):
            for i0 in range(0, n, PIECE):
                some = range(i0, i0 + PIECE)
                for i in some:
                    last = v.max(best[0:r, i, 0:8], x[0:r, i, :])
                step(last)
                for i in some:
                    last = v.max_index(where[0:r, i, 0:8], best[0:r, i, 0:8], x[0:r, i, :])
                step(last)
                yield
                for i in some:
                    last = v.match_replace(x[0:r, i, :], best[0:r, i, 0:8], x[0:r, i, :], -3e38)
                step(last)
                for i in some:
                    last = v.max(best[0:r, i, 8:16], x[0:r, i, :])
                step(last)
                yield
                for i in some:
                    last = v.max_index(where[0:r, i, 8:16], best[0:r, i, 8:16], x[0:r, i, :])
                step(last)
                yield

        for _ in sixteen_best(s, val, at, HC):
            count += 1
            yield
        v.tensor_copy(atf[0:r], at[0:r])
        for hd in range(PH):
            last = v.tensor_tensor(cand[0:r, hd].rearrange("p (i j) -> p i j", j=PK), bc(val[0:r, 2 * hd, :], 2, PK),
                                   bc(val[0:r, 2 * hd + 1, :], 1, PK), ALU.add)
            if hd % 4 == 3:
                step(last)
                count += 1
                yield
        for _ in sixteen_best(cand, top, sel, PH):
            count += 1
            yield
        v.tensor_scalar(half[0:r, 0], sel[0:r], 4, None, ALU.logical_shift_right)
        step(v.tensor_scalar(half[0:r, 1], sel[0:r], 15, None, ALU.bitwise_and))
        step(v.tensor_copy(halff[0:r], half[0:r]))
        for c in range(2):
            for op in (ALU.is_equal, ALU.mult):
                for hd in range(PH):
                    eq = cand[0:r, hd].rearrange("p (k j) -> p k j", j=PK)
                    if op == ALU.is_equal:
                        last = v.tensor_tensor(eq, bc(halff[0:r, c, hd, :], 2, PK), bc(k.c("iota16")[0:r, :], 1, PK), op)
                    else:
                        last = v.tensor_tensor(eq, eq, bc(atf[0:r, 2 * hd + c, :], 1, PK), op)
                    if hd % 4 == 3:
                        step(last)
                        count += 1
                        yield
            step(v.tensor_reduce(ef[0:r, c].rearrange("p h k -> p (h k)"), cand[0:r].rearrange("p h (k j) -> p (h k) j", j=PK),
                                 AX, ALU.add))
            count += 1
            yield
        step(v.scalar_tensor_tensor(ef[0:r, 0], ef[0:r, 0], float(NK), ef[0:r, 1], ALU.mult, ALU.add))
        step(v.tensor_scalar(ef[0:r, 0], ef[0:r, 0], float(layer * EXPERTS), None, ALU.add))
        v.tensor_tensor(e[0:r], top[0:r], top[0:r, :, 0:1].broadcast_to([r, PH, PK]), ALU.subtract).then_inc(less, 1)
        assert count == EXP_TICK, count
        count += 1
        yield
        dve.wait_ge(expd, 1)
        step(v.tensor_reduce(den[0:r], e[0:r], AX, ALU.add))
        step(v.reciprocal(den[0:r], den[0:r]))
        step(v.tensor_tensor(e[0:r], e[0:r], bc(den[0:r], 2, PK), ALU.mult))
        count += 1
        yield
        if t < 2:
            v.tensor_copy(slots, ef[:, 0].rearrange("p h k -> p (h k)"))
            last = v.tensor_copy(gate, e[:].rearrange("p h k -> p (h k)"))
        else:
            for q in range(4):
                some = slice(NS * q, NS * (q + 1))
                v.tensor_copy(slots[some, 0:NS], ef[0:r, 0].rearrange("p h k -> p (h k)")[:, some])
                v.tensor_copy(xs[some, :], k.x[0:NS, 2, :])
                last = v.tensor_copy(gate[some, 0:NS], e[0:r].rearrange("p h k -> p (h k)")[:, some])
        step(last)
        if routed is not None:
            v.memset(k.pad[:, :], 0.0).then_inc(routed, 1)
        while count < TICKS:
            count += 1
            yield
    return stage


ORDER = (2, 0, 1)
VISITS = [(layer, t) for layer in range(DEPTH) for t in ORDER]
STEPS = [SLOTS // 4 if t == 2 else SLOTS for _, t in VISITS]
FIRST = [sum(STEPS[:i]) for i in range(len(STEPS) + 1)]

WINDOWS = (
    ("route 0 0", FIRST[0], ()),
    ("route 0 1", FIRST[1], ()),
    ("mixer 2", FIRST[1] + 30, (3,)),
    ("route 1 2", FIRST[2] + 16, ()),
    ("mixer 0", FIRST[2] + 46, (3,)),
    ("route 1 0", FIRST[3] - 16, ()),
    ("mixer 1", FIRST[3] + 16, (3,)),
    ("route 1 1", FIRST[5] - 34, ()),
    ("nothing", FIRST[5], (3,)),
)


class Experts:

    def __init__(self, k, table, slots, gate, xs, gain, bias, outs, ctx):
        self.k, self.table, self.slots, self.gate, self.xs, self.outs = k, table, slots, gate, xs, outs
        self.gain, self.bias = gain, bias
        self.uv = k.sbuf("uv", [128, RING, 2 * D], ctx=ctx)
        self.dot, self.gelu, self.wgt = [k.sbuf(n, [128, 2, GROUP], ctx=ctx) for n in ("dot", "gelu", "wgt")]
        self.diag = k.sbuf("diag", [128, RING, 128], ctx=ctx)
        self.acc = k.sbuf("acc", [128, D], ctx=ctx)
        self.gb = k.sbuf("ffn_gb", [128, DEPTH, 2, D], ctx=ctx)
        self.z = k.sbuf("ffn_z", [128, D], ctx=ctx)
        self.stats = k.sbuf("ffn_stats", [128, 16], ctx=ctx)
        self.landed = [k.sem(f"row_landed{i}") for i in range(RING)]
        (self.dotted, self.gelued, self.weighed, self.spread, self.used, self.variance, self.rooted, self.rows_in, self.sum_read,
         self.normed, self.routed, self.added, self.folded) = [k.sem(n) for n in (
             "dotted", "gelued", "weighed", "spread", "row_used", "ffn_variance", "ffn_rooted", "ffn_rows_in", "sum_read", "normed",
             "routed", "row_added", "shares_folded")]
        self.n = FIRST[-1]
        self.ticks = self.n + LAG + 3

    def visit(self, s):
        return max(i for i in range(len(VISITS)) if FIRST[i] <= s)

    def at(self, s):
        i = self.visit(s)
        return VISITS[i][1], s - FIRST[i]

    @staticmethod
    def by_dve(s):
        return s % 4 in [rows for _, start, rows in WINDOWS if start <= s][-1]

    def count(self, dve, s):
        return sum(1 for i in range(s + 1) if self.by_dve(i) == dve)

    def shared(self, i):
        return any(self.by_dve(s) for s in range(FIRST[i], FIRST[i + 1]))

    def folds(self, i):
        return sum(1 for n in range(i + 1) if self.shared(n))

    def wait_used(self, eng, s):
        eng.wait_ge(self.added if self.by_dve(s) else self.used, self.count(self.by_dve(s), s))

    def pool(self, pool):
        for s in range(self.n):
            t, j = self.at(s)
            i = self.visit(s)
            if j == 0 and i:
                pool.wait_ge(self.routed, i)
            if s >= RING:
                self.wait_used(pool, s - RING)
            self.k.nc.gpsimd.indirect_dma_start(
                out=self.uv[:, s % RING, :], out_offset=None, in_=self.table,
                in_offset=bass.IndirectOffsetOnAxis(ap=self.slots[:, t, j:j + 1], axis=0)).then_inc(self.landed[s % RING], 16)

    def vector(self, dve):
        k, nc = self.k, self.k.nc
        dve.wait_ge(self.rows_in, 16 * 2 * DEPTH)

        def ending(s):
            return next((i for i in range(len(VISITS)) if FIRST[i + 1] - 1 + LAG == s), None)

        for s in range(self.ticks):
            if s < self.n:
                t, j = self.at(s)
                x = k.x[:, t, :] if t < 2 else self.xs[:, :]
                grp = s // GROUP
                dve.wait_ge(self.landed[s % RING], 16 * (s // RING + 1))
                if s % GROUP == 0 and grp >= 2:
                    dve.wait_ge(self.gelued, grp - 1)
                ins = nc.vector.tensor_tensor_reduce(self.uv[:, s % RING, 0:D], self.uv[:, s % RING, 0:D], x, 1.0, 0.0, ALU.mult, ALU.add,
                                                     self.dot[:, grp % 2, s % GROUP:s % GROUP + 1])
                if s % GROUP == GROUP - 1:
                    ins.then_inc(self.dotted, 1)
            if s % GROUP == 0 and 0 < s <= self.n:
                grp = s // GROUP - 1
                t, j = self.at(s - GROUP)
                dve.wait_ge(self.gelued, grp + 1)
                if grp >= 2:
                    dve.wait_ge(self.spread, grp - 1)
                nc.vector.tensor_tensor(self.wgt[:, grp % 2, :], self.gelu[:, grp % 2, :], self.gate[:, t, j:j + GROUP], ALU.mult)\
                    .then_inc(self.weighed, 1)
            q = s - 2
            if 0 <= q < self.n and self.by_dve(q):
                grp, i, done = q // GROUP, self.visit(q), self.count(True, q) - 1
                w, v = self.wgt[:, grp % 2, q % GROUP:q % GROUP + 1], self.uv[:, q % RING, D:2 * D]
                dve.wait_ge(self.weighed, grp + 1)
                if done:
                    dve.wait_ge(self.added, done)
                if not any(self.by_dve(other) for other in range(FIRST[i], q)):
                    nc.vector.tensor_scalar(self.acc[:, :], v, w, None, ALU.mult).then_inc(self.added, 1)
                else:
                    nc.vector.scalar_tensor_tensor(self.acc[:, :], v, w, self.acc[:, :], ALU.mult, ALU.add).then_inc(self.added, 1)
            for later in range(3):
                i = ending(s - later)
                if i is None:
                    continue
                layer, t = VISITS[i]
                r = ROWS[t]
                z, stats = self.z[0:r, :], self.stats[0:r, :]
                if later == 0:
                    if self.shared(i):
                        dve.wait_ge(self.folded, self.folds(i))
                    else:
                        dve.wait_ge(self.used, self.count(False, s - LAG))
                    out = k.ps[0:r, 0:2, :].rearrange("p a b -> p (a b)")
                    nc.vector.scalar_tensor_tensor(z, k.x[0:r, t, :], ALPHA, out, ALU.mult, ALU.add).then_inc(self.sum_read, 1)
                    dve.wait_ge(self.sum_read, i + 1)
                    norm_first(k, z, stats, self.variance)
                elif later == 1:
                    dve.wait_ge(self.rooted, i + 1)
                    norm_second(k, z, stats)
                else:
                    norm_third(k, z, k.x[0:r, t, :], self.gb[0:r, layer, 0, :], self.gb[0:r, layer, 1, :])
                    nc.vector.memset(k.pad[:, :], 0.0).then_inc(self.normed, 1)
            yield

    def scalar(self, act):
        k, nc = self.k, self.k.nc
        for s in range(self.ticks):
            if s < self.n and s % GROUP == GROUP - 1:
                grp = s // GROUP
                act.wait_ge(self.dotted, grp + 1)
                if grp >= 2:
                    act.wait_ge(self.weighed, grp - 1)
                nc.scalar.activation(self.gelu[:, grp % 2, :], self.dot[:, grp % 2, :], ACT.Gelu).then_inc(self.gelued, 1)
            if s % GROUP == 0 and 0 < s <= self.n:
                grp = s // GROUP - 1
                act.wait_ge(self.weighed, grp + 1)
                for g in range(GROUP):
                    step = s - GROUP + g
                    if self.by_dve(step):
                        continue
                    if step >= RING:
                        act.wait_ge(self.used, self.count(False, step - RING))
                    t, _ = self.at(step)
                    shape, w = ("ident", 128) if t < 2 else ("fold", NS)
                    last = nc.scalar.activation(self.diag[:, step % RING, 0:w], k.c(shape), ACT.Copy,
                                                scale=self.wgt[:, grp % 2, g:g + 1])
                last.then_inc(self.spread, 1)
            i = next((i for i in range(len(VISITS)) if FIRST[i + 1] - 1 + LAG == s), None)
            if i is not None:
                r = ROWS[VISITS[i][1]]
                act.wait_ge(self.variance, i + 1)
                nc.scalar.activation(self.stats[0:r, 15:16], self.stats[0:r, 14:15], ACT.Sqrt).then_inc(self.rooted, 1)
            yield

    def tensor(self, pe):
        k, nc = self.k, self.k.nc
        for tick in range(self.ticks):
            s = tick - LAG
            if 0 <= s < self.n:
                i = self.visit(s)
                t, j = self.at(s)
                m = ROWS[t]
                if s % GROUP == 0:
                    pe.wait_ge(self.spread, s // GROUP + 1)
                if j == 0 and i:
                    pe.wait_ge(self.sum_read, i)
                if not self.by_dve(s):
                    for c in range(2):
                        last = nc.tensor.matmul(k.bank(c)[0:m, :], self.diag[:, s % RING, 0:m],
                                                self.uv[:, s % RING, D + 512 * c:D + 512 * (c + 1)],
                                                start=(j == 0), stop=(j == STEPS[i] - 1 and not self.shared(i)), skip_group_check=True)
                    last.then_inc(self.used, 1)
                if j == STEPS[i] - 1 and self.shared(i):
                    pe.wait_ge(self.added, self.count(True, s))
                    for c in range(2):
                        last = nc.tensor.matmul(k.bank(c)[0:m, :], k.c("ident" if t < 2 else "fold")[:, 0:m],
                                                self.acc[:, 512 * c:512 * (c + 1)], start=False, stop=True, skip_group_check=True)
                    last.then_inc(self.folded, 1)
            yield

    def loads(self, sp):
        for layer in range(DEPTH):
            sp.dma_start(self.gb[:, layer, 0, :], self.gain[layer].partition_broadcast(128)).then_inc(self.rows_in, 16)
            sp.dma_start(self.gb[:, layer, 1, :], self.bias[layer].partition_broadcast(128)).then_inc(self.rows_in, 16)

    def stores(self, sp):
        y_prompt, y_sample = self.outs
        for i in range(len(ORDER)):
            t = ORDER[i]
            sp.wait_ge(self.normed, len(ORDER) + i + 1)
            dst = y_prompt[0, 128 * t:128 * (t + 1), :] if t < 2 else y_sample.rearrange("b t d -> (b t) d")
            self.k.store(sp, dst, self.k.x[0:ROWS[t], t, :])
        self.k.wait_for_stores(sp)


def side_ticks(k, stages, name, eng, ended, base):
    for n, stage in enumerate([Stage(k, 0)] + stages):
        yield from stage.run(name, eng)
        eng.drain().then_inc(ended, 1)
        yield
        eng.wait_ge(ended, 4 * (base + n + 1))
        yield


def experts_and_side_work(k, experts, windows):
    ended = k.sem("side_stage_ended")
    spans = []
    for i in range(len(windows)):
        spans.append((windows[i][0], windows[i + 1][0] if i + 1 < len(windows) else experts.ticks))

    def both(name, eng):
        main = {"tensor": experts.tensor, "vector": experts.vector, "scalar": experts.scalar}[name](eng)
        base = 0
        for (a, b), (_, stages) in zip(spans, windows):
            side = side_ticks(k, stages, name, eng, ended, base) if stages else iter(())
            weights = [0.5] * 2 + [w for st in stages for w in st.weights + [0.5] * 2] if stages else []
            base += len(stages) + 1 if stages else 0
            reached = np.cumsum(weights)
            done = 0
            for n in range(b - a):
                next(main)
                while done < len(weights) and (n == b - a - 1 or reached[done] * (b - a) <= reached[-1] * (n + 1)):
                    next(side)
                    done += 1
            for _ in side:
                raise AssertionError("side work left over")
        for _ in main:
            raise AssertionError("steps left over")

    with k.nc.Block() as block:
        @block.gpsimd
        def _(pool):
            experts.pool(pool)

        @block.tensor
        def _(pe):
            both("tensor", pe)

        @block.vector
        def _(dve):
            both("vector", dve)

        @block.scalar
        def _(act):
            both("scalar", act)

        @block.sync
        def _(sp):
            experts.loads(sp)
            n = 0
            for _, stages in windows:
                if not stages:
                    continue
                chain = [Stage(k, 0)] + stages
                for stage, following in zip(chain, stages + [None]):
                    if "sync" in stage.parts:
                        stage.parts["sync"](sp)
                    if following and "early loads" in following.parts:
                        following.parts["early loads"](sp)
                    n += 1
                    sp.sem_inc(ended, 1)
                    sp.wait_ge(ended, 4 * n)
                    for sem in stage.sems:
                        sp.sem_clear(sem)
            experts.stores(sp)


def dilated_tile(k, name, t, a, o, val, kT):
    r, tiles = ROWS[t], (t,)
    stages = [transpose_x(k, name + "_x", tiles, SIDE_BANKS)]
    with ExitStack() as outer:
        catT = k.xT
        qT = k.sbuf(name + "_qT", [128, HP, COL0[t] + r], ctx=outer)
        cached = k.sbuf(name + "_cache", [128, 2, DEC_B, NPG, 256], ctx=outer) if t == 2 else None
        with ExitStack() as inner:
            qk = k.sbuf(name + "_qk", [128, 1, 2 * D], ctx=inner)
            with ExitStack() as load:
                if t == 2:
                    wbuf = cached[:, :].rearrange("p x b n (c z) -> p (x b n c) z", z=256)\
                        .rearrange("p (s c n) z -> p s c (n z)", s=4, c=4)
                else:
                    wbuf = k.sbuf(name + "_w", [128, 3, 4, 512], ctx=load)
                out = lambda j, _: qk[0:r, 0, 512 * j:512 * (j + 1)] if j < 4 else val[0:r, t, 512 * (j - 4):512 * (j - 3)]
                stages.append(project_rows(k, name + "_in", a["odd_w_in"][0], [512] * 6, out, wbuf, tiles, SIDE_BANKS))
            with ExitStack() as rot:
                tmp = k.sbuf(name + "_tmp", [128, 4, 256], ctx=rot)
                stages.append(rotate_and_store(k, name + "_rot", qk, val, tiles, o["dil_p"], o["dil_s"], tmp))
            groups = [([qk[0:r, 0, at + 128 * (c + j):at + 128 * (c + j + 1)] for j in range(4)], dst[:, c:c + 4, cols(t)])
                      for dst, at in ((qT, 0), (kT, D)) for c in range(0, HP, 4)]
            stages.append(transposes(k, name + "_qk", groups, SIDE_BANKS))
        if t == 2:
            w = cached[:, 0].rearrange("p b n (c z) -> p (b n c) z", z=256).rearrange("p (s c n) z -> p s c (n z)", s=2, c=2)
        else:
            w = k.sbuf(name + "_w_out", [128, 3, 2, D], ctx=outer)
        if t == 2:
            for q4 in range(HEADS // 4):
                with ExitStack() as inner:
                    stages += dilated_sample(k, f"{name}_s{q4}", q4, a["cache_dil_kv"], qT, kT, val, catT, cached, inner, SIDE_BANKS,
                                             (2, 4), (6,), 7)
        else:
            with ExitStack() as inner:
                bufs = attention_buffers(k, f"{name}_p{t}", 512 * (t + 1), 512, inner)
                stages.append(dilated_prompt(k, f"{name}_p{t}", t, qT, kT, val, catT, bufs, (2, 4), (6,), 7))
        gb = k.sbuf(name + "_gb", [128, 2, D], ctx=outer)
        z, stats = k.sbuf(name + "_z", [128, D], ctx=outer), k.sbuf(name + "_stats", [128, 16], ctx=outer)
        w_v = a["odd_w_out"][0].rearrange("(c p) n -> p c n", p=128)
        stages.append(project_out_and_norm(k, name + "_out", catT, lambda i, dst: [(dst, w_v[:, 2 * i:2 * i + 2, :])], a["ln_mix_g"][1],
                                           a["ln_mix_b"][1], w, gb, z, stats, tiles, SIDE_BANKS))
    stages.append(transpose_x(k, name + "_y", tiles, SIDE_BANKS))
    return stages


def late_routing(k, name, t, a, route_tile):
    with ExitStack() as late:
        qT = k.sbuf(name + "_qT", [128, 2 * PH, COL0[t] + ROWS[t]], ctx=late)
        keysT = k.sbuf(name + "_keysT", [128, 2 * PH, NK], ctx=late)
        with ExitStack() as load:
            wbuf = k.sbuf(name + "_w", [128, 3, 8, 256], ctx=load)
            keys = k.sbuf(name + "_keys", [128, 2 * PH, 128], ctx=load) if t == 2 else qT[:, :, 0:128]
            stages = [turn_keys(k, name + "_keys", a["peer_sub_keys"][1], keys, keysT, SIDE_BANKS),
                      project_cols(k, name + "_q", a["peer_w_q"][1], 2 * PH * 128, qT, wbuf, cols(t), SIDE_BANKS)]
        with ExitStack() as inner:
            return stages, [route_tile(1, t, qT, keysT, inner)]


def first_mixer(k, a, o):
    with ExitStack() as ctx:
        h = k.sbuf("h", [128, TILES, EVEN_ROWS], ctx=ctx)
        w_in = a["even_w_in"][0]
        widths = [512, 512, 512, 512, 280]
        caches = SparseCaches(k, ctx)
        fin = k.sbuf("hg_fin", [128, HG // 2, HD], ctx=ctx)
        new = k.sbuf("hg_new", [128, HG // 2, DEC_B, HD], ctx=ctx)
        with ExitStack() as hg:
            cat = k.sbuf("cat", [128, TILES, 512], ctx=hg)
            hT = k.sbuf("hT", [128, 8, NTOK], ctx=hg)
            state_inputs = StateInputs(k, hg)
            with ExitStack() as load:
                wbuf = k.sbuf("even_w", [128, 4, 4, 512], ctx=load)
                wbuf_T = k.sbuf("even_wT", [128, 3, 8, 256], ctx=load)
                out = lambda j, t: h[0:ROWS[t], t, 512 * j:512 * j + widths[j]]
                rows = project_rows(k, "even", w_in[:, 1024:], widths, out, wbuf)
                columns = project_cols(k, "even_T", w_in, 1024, hT, wbuf_T)
                alone(k, transpose_x(k, "x0"), following=(rows,))
                alone(k, caches.stage(k, state_inputs, a), rows, following=(columns,))
                alone(k, columns)
            recurrence(k, h, hT, cat, state_inputs, fin, new, a["hg_norm_g"][0], o["state_prompt"], o["state_sample"])
            alone(k, transposes(k, "cat", [([cat[0:r, t, 128 * c:128 * (c + 1)] for c in range(4)], k.xT[:, 0:4, cols(t)])
                                           for t, r in enumerate(ROWS)]))
        sparse_attention(k, h, k.xT, caches, [o[n] for n in ("cmp_p", "cmp_s", "slc_p", "slc_s", "win_p", "win_s")])


def build(nc, a, o):
    with ExitStack() as whole:
        k = Core(nc, whole)
        k.pad = k.sbuf("progress", [128, 1])
        k.level_masks = a["level_masks"]
        load_inputs(k, a["x_prompt"], a["x_sample"], a["const"])
        first_mixer(k, a, o)
        k.fresh_semaphores()
        with ExitStack() as ctx:
            slots = k.sbuf("slots", [128, TILES, SLOTS], U32, ctx)
            gate = k.sbuf("gate", [128, TILES, SLOTS], ctx=ctx)
            xs = k.sbuf("xs", [128, D], ctx=ctx)
            experts = Experts(k, a["experts"], slots, gate, xs, a["ln_ffn_g"], a["ln_ffn_b"], (o["y_prompt"], o["y_sample"]), ctx)
            r = lambda layer, t, qT, keysT, inner, routed=experts.routed: route(
                k, f"route{layer}{t}", layer, t, qT, keysT, slots[:, t], gate[:, t], xs, inner, 0 if routed is None else 2, routed)
            w_out = a["even_w_out"][0]

            def even_piece(i, dst):
                if i < 2:
                    return [(dst, w_out[256 * i:256 * (i + 1)].rearrange("(c p) n -> p c n", p=128))]
                return [(dst[64 * kv:64 * kv + 64], w_out[512 + 256 * kv + 128 * (i - 2):512 + 256 * kv + 128 * (i - 1)]
                         .rearrange("(g d) n -> d g n", d=HD)) for kv in range(KV)]

            with ExitStack() as first:
                qT = k.sbuf("peer_qT", [128, 2 * PH, NTOK], ctx=first)
                keysT = k.sbuf("peer_keysT", [128, 2 * PH, NK], ctx=first)
                wbuf = experts.uv[:, :, :].rearrange("p s (c n) -> p s c n", n=256)
                with ExitStack() as load:
                    keys = k.sbuf("peer_keys", [128, 2 * PH, 128], ctx=load)
                    turn = turn_keys(k, "peer_keys", a["peer_sub_keys"][0], keys, keysT, (6, 7))
                    qs = k.sbuf("peer_qs", [NS, 2 * PH * 128], ctx=load)
                    sample_queries = project_rows(k, "peer_qs", a["peer_w_q"][0], [512] * 4, lambda j, _: qs[:, 512 * j:512 * (j + 1)],
                                                  experts.uv[:, :, :].rearrange("p s (c n) -> p s c n", n=512), (2,), (0, 1, 2, 3, 4, 5))
                    with ExitStack() as mix:
                        w = k.sbuf("even_w_out", [128, 4, 2, D], ctx=mix)
                        gb, z, stats = experts.gb[:, 0], experts.z, experts.stats
                        alone(k, project_out_and_norm(k, "even_out", k.xT, even_piece, a["ln_mix_g"][0], a["ln_mix_b"][0], w, gb, z, stats),
                              following=(turn, sample_queries))
                    alone(k, transpose_x(k, "x1"))
                    alone(k, turn, sample_queries)
                    alone(k, transposes(k, "peer_qs_T", [([qs[:, 128 * (4 * i + j):128 * (4 * i + j + 1)] for j in range(4)],
                                                          qT[:, 4 * i:4 * i + 4, SMP]) for i in range(4)]))
                with ExitStack() as load:
                    sample, prompt = r(0, 2, qT, keysT, load, None), project_cols(
                        k, "peer_qp", a["peer_w_q"][0], 2 * PH * 128, qT, wbuf, slice(NS, NTOK), (4, 5, 6, 7), ("scalar",))
                    alone(k, sample, prompt, scalar=(prompt, sample))
                k.side = True
                work = {"nothing": []}
                for t in range(2):
                    with ExitStack() as inner:
                        work[f"route 0 {t}"] = [r(0, t, qT, keysT, inner)]
            with ExitStack() as second:
                val = k.sbuf("dil_val", [128, TILES, D], ctx=second)
                kT = k.sbuf("dil_kT", [128, HP, NTOK], ctx=second)
                for t, name in zip(ORDER, ("sample", "first", "last")):
                    work[f"mixer {t}"] = dilated_tile(k, name, t, a, o, val, kT)
                    late, work[f"route 1 {t}"] = late_routing(k, name, t, a, r)
                    work[f"mixer {t}"] += late
            k.side = False
            experts_and_side_work(k, experts, [(start, work[name]) for name, start, _ in WINDOWS])


_OUTS = [("y_prompt", (1, SEQ, D)), ("y_sample", (DEC_B, DEC_T, D)), ("state_prompt", (1, 1, HG, 64, 64)),
         ("state_sample", (1, DEC_B, HG, 64, 64))]
for _n in ("cmp", "slc", "win"):
    _OUTS += [(_n + "_p", (1, 1, SEQ, 2, KV, HD)), (_n + "_s", (1, DEC_B, DEC_T, 2, KV, HD))]
_OUTS += [("dil_p", (1, 1, SEQ, 2, HEADS, HD)), ("dil_s", (1, DEC_B, DEC_T, 2, HEADS, HD))]


def kernel(**inputs):
    import numpy as _np
    import concourse.bacc as _bacc
    from concourse import mybir as _mybir
    from concourse.bass_utils import run_bass_kernel_spmd as _run

    nc = _bacc.Bacc("TRN2", target_bir_lowering=False, num_devices=1)
    given = {n: _np.ascontiguousarray(x) for n, x in inputs.items() if n not in ("peer_u", "peer_v")}
    u, v = _np.asarray(inputs["peer_u"]), _np.asarray(inputs["peer_v"])
    given["experts"] = _np.concatenate([u, v], axis=2).reshape(DEPTH * EXPERTS, 2 * D)
    given["const"], given["level_masks"] = CONST, LEVEL_MASKS
    arrays = {f"in_{n}_dram": x for n, x in given.items()}
    a = {n: nc.dram_tensor(f"in_{n}_dram", x.shape, _mybir.dt.from_np(x.dtype), kind="ExternalInput").ap() for n, x in given.items()}
    o = {n: nc.dram_tensor(f"out_{n}_dram", shape, F32, kind="ExternalOutput").ap() for n, shape in _OUTS}
    build(nc, a, o)
    r = _run(nc, [arrays], core_ids=[0])
    return tuple(r.results[0][f"out_{n}_dram"] for n, _ in _OUTS)
```
